# Optimizing a Trainium2 kernel written in Bass

```python
import jax, jax.numpy as jnp
from jax import lax
import numpy as np

D_MODEL = 1024
BATCH = 1
SEQ = 128
DEPTH = 1
DEC_BATCH = 1
DEC_SEQ = 512
PAST_LEN = 256

GRID_W = 64
ATT_WIDTH = D_MODEL // 2
CONV_WIDTH = D_MODEL - ATT_WIDTH
HEAD_DIM = 64
N_ATT_HEADS = ATT_WIDTH // HEAD_DIM
CONV_K = 3
WIN_ROWS_MAX = 8
WIN_COLS = 16
COL_BLOCK = 16
KEY_SPAN = COL_BLOCK + WIN_COLS
N_COL_BLOCKS = GRID_W // COL_BLOCK
CTX_Q_BLOCK = 128
N_GROUPS = 4
EXPERTS_PER_GROUP = 4
N_EXPERTS = N_GROUPS * EXPERTS_PER_GROUP
TOP_K = 2
D_EXPERT = D_MODEL // 4
ALPHA = (2 * DEPTH) ** 0.25
BETA = (8 * DEPTH) ** -0.25
LN_EPS = 1e-5
NEG_INF = -1e30

kernel_name = "hybrid_natten_shortconv_hmoe_diffusion_step"

def _layer_norm(x, g, b):
    xf = x.astype(jnp.float32)
    mu = jnp.mean(xf, axis=-1, keepdims=True)
    var = jnp.mean(jnp.square(xf - mu), axis=-1, keepdims=True)
    return ((xf - mu) * lax.rsqrt(var + LN_EPS)).astype(x.dtype) * g + b

def _modulation(cond, w_ada, b_ada):
    m = jax.nn.silu(cond) @ w_ada + b_ada
    return jnp.split(m, 6, axis=-1)

def _heads(t):
    B, L, _ = t.shape
    return t.reshape(B, L, N_ATT_HEADS, HEAD_DIM).transpose(0, 2, 1, 3)

def _project(h, w_in):
    z = h @ w_in
    splits = [ATT_WIDTH, 2 * ATT_WIDTH, 3 * ATT_WIDTH,
              3 * ATT_WIDTH + CONV_WIDTH, 3 * ATT_WIDTH + 2 * CONV_WIDTH]
    q, k, v, bg, cg, u = jnp.split(z, splits, axis=-1)
    return _heads(q), _heads(k), _heads(v), bg, cg, u

def _short_conv(bg, cg, u, w):
    y = cg * u
    yp = jnp.pad(y, ((0, 0), (1, 1), (0, 0)))
    conv = w[0] * yp[:, :-2] + w[1] * yp[:, 1:-1] + w[2] * yp[:, 2:]
    return bg * conv

def _merge(att, conv, w_out):
    B, H, L, Dh = att.shape
    a = att.transpose(0, 2, 1, 3).reshape(B, L, H * Dh)
    return jnp.concatenate([a, conv], axis=-1) @ w_out

def _context_attention(q, k, v):
    B, H, L, Dh = q.shape
    nb = L // CTX_Q_BLOCK
    qb = q.reshape(B, H, nb, CTX_Q_BLOCK, Dh).transpose(2, 0, 1, 3, 4)
    scale = HEAD_DIM ** -0.5

    def block(qi):
        s = jnp.einsum("bhqd,bhkd->bhqk", qi, k, preferred_element_type=jnp.float32) * scale
        p = jax.nn.softmax(s, axis=-1).astype(v.dtype)
        return jnp.einsum("bhqk,bhkd->bhqd", p, v)

    o = lax.map(block, qb)
    return o.transpose(1, 2, 0, 3, 4).reshape(B, H, L, Dh)

def _window_geometry():
    qcol = np.arange(GRID_W).reshape(N_COL_BLOCKS, COL_BLOCK)
    col_start = np.clip(qcol - WIN_COLS // 2, 0, GRID_W - WIN_COLS)
    key_start = np.clip(np.arange(N_COL_BLOCKS) * COL_BLOCK - WIN_COLS // 2, 0, GRID_W - KEY_SPAN)
    key_col = key_start[:, None] + np.arange(KEY_SPAN)[None, :]
    kc = key_col[:, None, :]
    valid = (kc >= col_start[:, :, None]) & (kc < col_start[:, :, None] + WIN_COLS)
    dc_idx = np.clip(kc - qcol[:, :, None] + WIN_COLS - 1, 0, 2 * WIN_COLS - 2)
    return key_col, valid, dc_idx

def _latent_attention(q, k, v, ck, cv, rpb):
    B, H, T, Dh = q.shape
    rows = T // GRID_W
    wr = min(WIN_ROWS_MAX, rows)
    key_col, valid, dc_idx = _window_geometry()
    scale = HEAD_DIM ** -0.5
    qg = q.reshape(B, H, rows, N_COL_BLOCKS, COL_BLOCK, Dh)
    kblk = jnp.take(k.reshape(B, H, rows, GRID_W, Dh), key_col, axis=3)
    vblk = jnp.take(v.reshape(B, H, rows, GRID_W, Dh), key_col, axis=3)
    mask = valid[:, :, None, :]
    n_loc = wr * KEY_SPAN

    def row(r):
        rs = jnp.clip(r - WIN_ROWS_MAX // 2, 0, rows - wr)
        q_r = lax.dynamic_index_in_dim(qg, r, axis=2, keepdims=False)
        kb = lax.dynamic_slice_in_dim(kblk, rs, wr, axis=2)
        vb = lax.dynamic_slice_in_dim(vblk, rs, wr, axis=2)
        dr_idx = rs + jnp.arange(wr) - r + WIN_ROWS_MAX - 1
        bias = rpb[:, dr_idx[None, None, :, None], dc_idx[:, :, None, :]]
        s_loc = jnp.einsum("bhncd,bhwnkd->bhncwk", q_r, kb,
                           preferred_element_type=jnp.float32) * scale + bias[None]
        s_loc = jnp.where(mask, s_loc, NEG_INF).reshape(B, H, N_COL_BLOCKS, COL_BLOCK, n_loc)
        s_ctx = jnp.einsum("bhncd,bhld->bhncl", q_r, ck,
                           preferred_element_type=jnp.float32) * scale
        p = jax.nn.softmax(jnp.concatenate([s_loc, s_ctx], axis=-1), axis=-1).astype(v.dtype)
        p_loc = p[..., :n_loc].reshape(B, H, N_COL_BLOCKS, COL_BLOCK, wr, KEY_SPAN)
        return (jnp.einsum("bhncwk,bhwnkd->bhncd", p_loc, vb)
                + jnp.einsum("bhncl,bhld->bhncd", p[..., n_loc:], cv))

    o = lax.map(row, jnp.arange(rows))
    return o.transpose(1, 2, 0, 3, 4, 5).reshape(B, H, T, Dh)

def _hier_moe(h, wg, bg, we, be, w_exp_in, w_exp_out):
    shape = h.shape
    t = h.reshape(-1, shape[-1])
    g_prob = jax.nn.softmax((t @ wg + bg).astype(jnp.float32), axis=-1)
    g_p, g_idx = lax.top_k(g_prob, 1)
    e_logits = (t @ we + be).astype(jnp.float32).reshape(-1, N_GROUPS, EXPERTS_PER_GROUP)
    e_prob = jax.nn.softmax(jnp.take_along_axis(e_logits, g_idx[:, :, None], axis=1)[:, 0], axis=-1)
    e_p, e_idx = lax.top_k(e_prob, TOP_K)
    w = g_p * e_p / jnp.sum(e_p, axis=-1, keepdims=True)
    ids = g_idx * EXPERTS_PER_GROUP + e_idx
    gate = jnp.sum(jax.nn.one_hot(ids, N_EXPERTS, dtype=jnp.float32) * w[..., None], axis=1).astype(h.dtype)
    hid = jnp.einsum("nd,edf->nef", t, w_exp_in)
    a, up = jnp.split(hid, 2, axis=-1)
    act = jax.nn.silu(a) * up * gate[:, :, None]
    return jnp.einsum("nef,efd->nd", act, w_exp_out).reshape(shape)

def setup_inputs(seed: int = 0) -> dict:
    key = jax.random.key(seed)
    ks = jax.random.split(key, 22)
    D = D_MODEL
    mix = ATT_WIDTH + CONV_WIDTH

    def nrm(k, shape, s):
        return s * jax.random.normal(k, shape, jnp.float32)

    return {
        "x_prompt": nrm(ks[0], (BATCH, SEQ, D), 1.0),
        "x_sample": nrm(ks[1], (DEC_BATCH, DEC_SEQ, D), 1.0),
        "cache_k": nrm(ks[2], (DEC_BATCH, DEPTH, N_ATT_HEADS, PAST_LEN, HEAD_DIM), 1.0),
        "cache_v": nrm(ks[3], (DEC_BATCH, DEPTH, N_ATT_HEADS, PAST_LEN, HEAD_DIM), 1.0),
        "c": nrm(ks[4], (DEC_BATCH, D), 1.0),
        "c_ctx": nrm(ks[5], (D,), 1.0),
        "w_ada": nrm(ks[6], (DEPTH, D, 6 * D), 0.5 * D ** -0.5),
        "b_ada": nrm(ks[7], (DEPTH, 6 * D), 0.02),
        "w_in": nrm(ks[8], (DEPTH, D, 3 * ATT_WIDTH + 3 * CONV_WIDTH), D ** -0.5),
        "conv_w": nrm(ks[9], (DEPTH, CONV_K, CONV_WIDTH), CONV_K ** -0.5),
        "rpb": nrm(ks[10], (DEPTH, N_ATT_HEADS, 2 * WIN_ROWS_MAX - 1, 2 * WIN_COLS - 1), 0.1),
        "w_out": nrm(ks[11], (DEPTH, mix, D), BETA * mix ** -0.5),
        "ln1_g": 1.0 + nrm(ks[12], (DEPTH, D), 0.02),
        "ln1_b": nrm(ks[13], (DEPTH, D), 0.02),
        "w_router_group": nrm(ks[14], (DEPTH, D, N_GROUPS), D ** -0.5),
        "b_router_group": nrm(ks[15], (DEPTH, N_GROUPS), 0.01),
        "w_router_expert": nrm(ks[16], (DEPTH, D, N_EXPERTS), D ** -0.5),
        "b_router_expert": nrm(ks[17], (DEPTH, N_EXPERTS), 0.01),
        "w_expert_in": nrm(ks[18], (DEPTH, N_EXPERTS, D, 2 * D_EXPERT), D ** -0.5),
        "w_expert_out": nrm(ks[19], (DEPTH, N_EXPERTS, D_EXPERT, D), BETA * D_EXPERT ** -0.5),
        "ln2_g": 1.0 + nrm(ks[20], (DEPTH, D), 0.02),
        "ln2_b": nrm(ks[21], (DEPTH, D), 0.02),
    }

def reference(x_prompt, x_sample, cache_k, cache_v, c, c_ctx, w_ada, b_ada, w_in, conv_w, rpb,
              w_out, ln1_g, ln1_b, w_router_group, b_router_group, w_router_expert,
              b_router_expert, w_expert_in, w_expert_out, ln2_g, ln2_b):
    xp = x_prompt
    xs = x_sample
    new_k = []
    new_v = []
    for l in range(DEPTH):
        moe_params = (w_router_group[l], b_router_group[l], w_router_expert[l],
                      b_router_expert[l], w_expert_in[l], w_expert_out[l])
        sa, ca, ga, sf, cf, gf = _modulation(c_ctx[None, None, :], w_ada[l], b_ada[l])
        q, k, v, bg, cg, u = _project(xp * (1 + ca) + sa, w_in[l])
        mix = _merge(_context_attention(q, k, v), _short_conv(bg, cg, u, conv_w[l]), w_out[l])
        xp = _layer_norm(ALPHA * xp + ga * mix, ln1_g[l], ln1_b[l])
        xp = _layer_norm(ALPHA * xp + gf * _hier_moe(xp * (1 + cf) + sf, *moe_params),
                         ln2_g[l], ln2_b[l])
        new_k.append(k)
        new_v.append(v)
        sa, ca, ga, sf, cf, gf = _modulation(c[:, None, :], w_ada[l], b_ada[l])
        q, k, v, bg, cg, u = _project(xs * (1 + ca) + sa, w_in[l])
        att = _latent_attention(q, k, v, cache_k[:, l], cache_v[:, l], rpb[l])
        mix = _merge(att, _short_conv(bg, cg, u, conv_w[l]), w_out[l])
        xs = _layer_norm(ALPHA * xs + ga * mix, ln1_g[l], ln1_b[l])
        xs = _layer_norm(ALPHA * xs + gf * _hier_moe(xs * (1 + cf) + sf, *moe_params),
                         ln2_g[l], ln2_b[l])
    new_cache_k = jnp.stack(new_k, axis=1)
    new_cache_v = jnp.stack(new_v, axis=1)
    return (xp, xs, new_cache_k, new_cache_v)


_drawn_inputs = setup_inputs


def setup_inputs(seed=0):
    import zlib

    import numpy as np

    out = dict(_drawn_inputs(seed))
    spreads = {}
    factors = {'cache_k': 8.0,
     'cache_v': 6.845,
     'rpb': 64.0,
     'ln1_g': 2.789,
     'b_router_group': 159.06,
     'b_router_expert': 45.259,
     'ln2_g': 25.804,
     'ln2_b': 23.994,
     'ln1_b': 3.844}
    for name, (base, spread) in spreads.items():
        noise = np.random.default_rng([zlib.crc32(name.encode()), seed]).standard_normal(out[name].shape)
        drawn = base * np.exp(spread * noise) if base else spread * noise
        out[name] = __import__('jax').numpy.asarray(drawn.astype(out[name].dtype))
    for name, factor in factors.items():
        out[name] = (out[name] * factor).astype(out[name].dtype)
    return out
```

```python
import concourse.bass as bass
from concourse import mybir
from contextlib import ExitStack


def build(nc, ins, outs):
    fp32 = mybir.dt.float32
    fp32r = mybir.dt.float32r
    i32 = mybir.dt.int32
    ALU = mybir.AluOpType
    ACT = mybir.ActivationFunctionType
    AX = mybir.AxisListType

    NS = ins["x_sample"].shape[1]
    NP = ins["x_prompt"].shape[1]
    D = ins["x_sample"].shape[2]
    TOK = NS + NP
    P = 128
    KD = D // P
    NT = TOK // P
    TS = NS // P
    HEADS, PAST, DH = ins["cache_k"].shape[2:]
    AW = HEADS * DH
    HP = HEADS // 2
    GRID = 64
    ROWS = NS // GRID
    NB, CB, SPAN = 4, 16, 32
    KEY0 = [0, 8, 24, 32]
    KIND = [2, 1, 1, 0]
    LOC = ROWS * SPAN
    NE = ins["w_expert_in"].shape[1]
    NG = 4
    EG = NE // NG
    DE = ins["w_expert_out"].shape[2]
    CH = 512
    HALF = TOK // 2
    ALPHA = 2.0 ** 0.25
    EPS = 1e-5
    CAP = P
    MORE = (2 * TOK) // CAP
    SLOTS = (NE + MORE) * CAP
    NA = 2 * 6
    RP0 = CB
    RPW = 64
    DR = 2 * ROWS - 1
    TW = DR * SPAN
    UNITS = 2 * HP * NB
    NU = UNITS + 2

    C_ID, C_TRI, C_MASK = 0, P, 2 * P
    C_RANK = C_MASK + 3 * SPAN
    C_E128 = C_RANK + NG
    C_OVER = C_E128 + NE
    C_TOK = C_OVER + NE
    C_IOTA = C_TOK + NT
    C_BACK = C_IOTA + MORE
    C_END = C_BACK + P

    ctx = ExitStack()
    with ctx:
        def sb(name, shape, dt=fp32):
            return ctx.enter_context(nc.sbuf_tensor(name, shape, dt))

        def sem(name):
            return ctx.enter_context(nc.semaphore(name))

        act_hi = sb("act_hi", [P, KD * TOK], fp32r)
        act_lo = sb("act_lo", [P, KD * TOK], fp32r)
        w_hi = sb("w_hi", [P, 2, KD * CH], fp32r)
        w_lo = sb("w_lo", [P, 2, KD * CH], fp32r)
        raw = sb("raw", [P, 2, KD * CH])
        g1 = sb("g1", [P, NT * D])
        uni = sb("uni", [P, 11856])
        const = sb("const", [P, C_END])
        rows = sb("rows", [P, P])
        cols = sb("cols", [P, P])
        modc = sb("modc", [P, 6 * KD, 2])
        wr = sb("wr", [P, KD, NG + NE])
        logits = sb("logits", [P, NT, NG + NE])
        small = sb("small", [P, 96])
        gates = sb("gates", [P, 2, NT])
        rb = sb("rb", [P, NG + NE])
        over_i = sb("over_i", [P, 1 + MORE], i32)
        over_col = sb("over_col", [P, 1], i32)
        slot_i = sb("slot_i", [P, 2, NT], i32)
        PS = ctx.enter_context(nc.psum_tensor("PS", [P, 8, 512], fp32))

        ones = rows
        ident = const[:, C_ID:C_ID + P]
        back = const[:, C_BACK:C_BACK + P]
        tri = const[:, C_TRI:C_TRI + P]
        mask3 = const[:, C_MASK:C_MASK + 3 * SPAN].rearrange("p (a k) -> p a k", a=3)

        def dram(name, shape, dt=fp32):
            return nc.dram_tensor(name, shape, dt, kind="Internal").ap()

        def dap(t, offset, pattern):
            return bass.AP(tensor=t.tensor, offset=offset, ap=pattern)

        v_dram = dram("v_scratch", (NS, AW))
        rp_dram = dram("rpb_padded", (HEADS * DR, RPW))
        bias_dram = dram("bias_windows", (HEADS * CB, 3 * TW))
        mod_dram = dram("mod_rows", (4 * KD * 2, P))
        h2_dram = dram("h2_rows", (TOK, D))
        list_dram = dram("slot_tokens", (SLOTS, 1))
        y_dram = dram("expert_rows", (SLOTS, D))

        x_nat = g1[:, :].rearrange("p (t d) -> p t d", t=NT)
        qT = g1[:, 0:HP * TOK].rearrange("p (m t) -> p m t", m=HP)
        kT = g1[:, HP * TOK:2 * HP * TOK].rearrange("p (m t) -> p m t", m=HP)
        x1 = x_nat
        h_hi = act_hi[:, :].rearrange("p (k t) -> p k t", k=KD)
        h_lo = act_lo[:, :].rearrange("p (k t) -> p k t", k=KD)
        PADW = TOK + 8
        conv_y = uni[:, 0:4 * PADW].rearrange("p (m t) -> p m t", m=4)
        conv_o = uni[:, 4 * PADW:8 * PADW].rearrange("p (m t) -> p m t", m=4)
        o = 8 * PADW
        bias_t = uni[:, o:o + 3 * TW].rearrange("p (a r k) -> p a r k", a=3, r=DR)
        h_tmp = uni[:, 6700:6700 + 2 * TOK].rearrange("p (b t) -> p b t", b=2)
        rp_pad = uni[:, 8000:8000 + RPW]
        ck_nat = uni[:, 8064:8064 + 2 * AW].rearrange("p (a n) -> p a n", a=2)
        silu_t = uni[:, 9100:9100 + P]
        stage = uni[:, 10832:10832 + 2 * AW].rearrange("p (b n) -> p b n", b=2)
        vblk = uni[:, 0:8 * AW].rearrange("p (j n) -> p j n", j=8)
        ctx_v = uni[:, 8 * AW:10 * AW].rearrange("p (j n) -> p j n", j=2)
        ck_T = uni[:, 5200:5200 + HP * PAST].rearrange("p (m t) -> p m t", m=HP)
        bias_s = uni[:, 6224:6224 + 2 * 3 * LOC].rearrange("p (b a n) -> p b a n", b=2, a=3)
        prob = uni[:, 7760:7760 + 1024].rearrange("p (b n) -> p b n", b=2)
        prob_T = uni[:, 8784:8784 + 1024].rearrange("p (b n) -> p b n", b=2)
        att_o = uni[:, 9808:9808 + 1024].rearrange("p (b n c) -> p b n c", b=2, n=NB)
        gate_a = uni[:, 0:2 * D].rearrange("p (j d) -> p j d", j=2)
        lin_a = uni[:, 2 * D:4 * D].rearrange("p (j d) -> p j d", j=2)
        lin_b = uni[:, 4 * D:6 * D].rearrange("p (j d) -> p j d", j=2)
        ln1_g = uni[:, 6 * D:7 * D]
        ln1_b = uni[:, 7 * D:8 * D]
        ln_t = uni[:, 8 * D:10 * D].rearrange("p (b d) -> p b d", b=2)
        h2_T = uni[:, 10 * D:11 * D].rearrange("p (k t) -> p k t", k=KD)
        rt = uni[:, 0:4096]
        raw_o = uni[:, 0:2 * 2 * D].rearrange("p (b n) -> p b n", b=2)
        hg = uni[:, 4096:4096 + 2 * D].rearrange("p (b n) -> p b n", b=2)
        y_sb = uni[:, 6144:6144 + 2 * D].rearrange("p (b n) -> p b n", b=2)
        sil = uni[:, 8192:8192 + 3 * DE].rearrange("p (b n) -> p b n", b=3)
        list_s = uni[:, 9120:9120 + NE + MORE].bitcast(i32)
        list_r = uni[:, 9400:9400 + CAP]
        slot_f = uni[:, 9200:9200 + 2 * NT].rearrange("p (c t) -> p c t", c=2)
        hgT_hi = act_hi[:, 0:2 * D].rearrange("p (b k t) -> p b k t", b=2, k=KD)
        hgT_lo = act_lo[:, 0:2 * D].rearrange("p (b k t) -> p b k t", b=2, k=KD)
        aT_hi = act_hi[:, 2 * D:2 * D + 4 * P].rearrange("p (b k t) -> p b k t", b=2, k=2)
        aT_lo = act_lo[:, 2 * D:2 * D + 4 * P].rearrange("p (b k t) -> p b k t", b=2, k=2)
        wo_hi = act_hi[:, 2560:2560 + 2 * D].rearrange("p (k n) -> p k n", k=2)
        wo_lo = act_lo[:, 2560:2560 + 2 * D].rearrange("p (k n) -> p k n", k=2)
        fin_v = raw[:, 0, :].rearrange("p (a d) -> p a d", a=4)
        fin_y = raw[:, 1, :].rearrange("p (b a d) -> p b a d", b=2, a=2)
        nmax = small[:, 0:8].rearrange("p (b n) -> p b n", b=2)
        rsum = small[:, 8:24].rearrange("p (b n) -> p b n", b=4)
        rinv = small[:, 24:32].rearrange("p (b n) -> p b n", b=2)
        stat = small[:, 32:44]
        mv = small[:, 44:46]
        rstd = small[:, 46:47]
        std = small[:, 47:48]
        eps = small[:, 48:49]

        w_ada, w_in, w_out = ins["w_ada"][0], ins["w_in"][0], ins["w_out"][0]
        we_in, we_out = ins["w_expert_in"][0], ins["w_expert_out"][0]
        IN_ORDER = [4, 5, 3, 0, 1, 2]
        stream = [(w_ada, c) for c in range(4)] + [(w_in, c) for c in IN_ORDER]
        stream += [(w_ada, c) for c in range(4, NA)] + [(w_out, c) for c in range(2)]
        NCH = len(stream)
        ADA_N = [0, 1, 2, 3] + list(range(10, 18))
        SPLIT_N = list(range(4, 10)) + [18, 19]
        E0 = len(SPLIT_N)

        s_const = sem("const_loaded")
        s_small = sem("small_rows_loaded")
        s_silu = sem("silu_steps")
        s_rows = sem("rows_transposed")
        s_cols = sem("cols_ready")
        s_raw = [sem("raw_loaded_0"), sem("raw_loaded_1")]
        s_ada = sem("ada_chunks_multiplied")
        s_mod = sem("modulation_steps")
        s_x = sem("x_loaded")
        s_xt = sem("x_transposed")
        s_h = sem("h_modulated")
        s_hhi = sem("h_hi_ready")
        s_hlo = sem("h_lo_ready")
        s_whi = sem("w_hi_ready")
        s_wlo = sem("w_lo_ready")
        s_acc = sem("proj_sums_ready")
        s_acc_a = sem("proj_sums_read_by_scalar")
        s_acc_d = sem("proj_sums_read_by_vector")
        s_vout = [sem("v_tile_stored_0"), sem("v_tile_stored_1")]
        s_cache = sem("cache_stored")
        s_kp = sem("k_prompt_transposed")
        s_kps = sem("k_prompt_staged")
        s_ck = sem("ctx_k_loaded")
        s_ckt = sem("ctx_k_transposed")
        s_cks = sem("ctx_k_ready")
        s_rpz = sem("rpb_pad_zeroed")
        s_rp = sem("rpb_steps")
        s_bt = sem("bias_window_loaded")
        s_bm = sem("bias_masked")
        s_bd = sem("bias_stored")
        s_bias = [sem("bias_head_loaded_0"), sem("bias_head_loaded_1")]
        s_mrow = sem("mod_rows_transposed")
        s_mrs = sem("mod_rows_staged")
        s_mrd = sem("mod_rows_stored")
        s_chi = sem("conv_hi_ready")
        s_clo = sem("conv_lo_ready")
        s_vb = sem("v_blocks_loaded")
        s_s = sem("scores_ready")
        s_nm = sem("row_max_ready")
        s_dv = sem("vector_chain")
        s_p = sem("probs_ready")
        s_pt = sem("probs_transposed")
        s_pts = sem("probs_T_ready")
        s_o = sem("att_out_ready")
        s_os = sem("att_out_scaled")
        s_ot = sem("att_out_transposed")
        s_mhi = sem("mix_hi_ready")
        s_mlo = sem("mix_lo_ready")
        s_vec = [sem("ln1_vectors_loaded_sample"), sem("ln1_vectors_loaded_prompt")]
        s_xr = [sem("x_reloaded_sample"), sem("x_reloaded_prompt")]
        s_wrl = sem("router_weights_loaded")
        s_mo = sem("mix_out_ready")
        s_mor = sem("mix_out_read")
        s_var = sem("variance_ready")
        s_std = sem("std_ready")
        s_xn = sem("normed_ready")
        s_h2 = sem("h2_ready")
        s_h2s = [sem("h2_stored_0"), sem("h2_stored_1")]
        s_x1 = sem("x1_ready")
        s_plc = sem("pool_chain")
        s_h2t = sem("h2_transposed")
        s_h2c = sem("h2_T_ready")
        s_rb = sem("router_biases_loaded")
        s_sl = sem("expert_silu_steps")
        s_lg = sem("logits_sum_ready")
        s_one = sem("choices_ready")
        s_pos = sem("positions_ready")
        s_slot = sem("slots_ready")
        s_gexp = sem("group_exp_ready")
        s_lz = sem("list_zeroed")
        s_lst = sem("list_scattered")
        s_ll = sem("list_loaded")
        s_lt = sem("list_transposed")
        s_lc = sem("list_ready")
        s_rawo = [sem("raw_out_loaded_0"), sem("raw_out_loaded_1")]
        s_hg = [sem("rows_gathered_0"), sem("rows_gathered_1")]
        s_hgt = sem("rows_transposed_for_expert")
        s_ghi = sem("gathered_hi_ready")
        s_glo = sem("gathered_lo_ready")
        s_ohi = sem("expert_out_w_hi_ready")
        s_olo = sem("expert_out_w_lo_ready")
        s_hid = sem("hidden_ready")
        s_ex = sem("silu_exp_ready")
        s_act = sem("expert_act_ready")
        s_at = sem("expert_act_transposed")
        s_ahi = sem("expert_act_hi_ready")
        s_alo = sem("expert_act_lo_ready")
        s_y = sem("expert_rows_ready")
        s_ya = sem("expert_rows_half_0_copied")
        s_yd = sem("expert_rows_half_1_copied")
        s_yst = [sem("expert_rows_stored_0"), sem("expert_rows_stored_1")]
        s_yz = sem("overflow_slots_filled")
        s_over = sem("overflow_table_ready")
        s_ovw = sem("overflow_weights_loaded")
        s_ovc = sem("overflow_column_ready")
        s_ovg = sem("overflow_rows_gathered")
        s_ovs = sem("overflow_rows_stored")
        s_fv = sem("final_vectors_loaded")
        s_fy = [sem("final_rows_gathered_0"), sem("final_rows_gathered_1")]
        s_fin = sem("final_tile_ready")
        s_done = sem("outputs_stored")

        block = ctx.enter_context(nc.Block())

        def raw_full(eng, n):
            eng.wait_ge(s_raw[n % 2], 16 * (n // 2 + 1))

        def chunk_src(w, c):
            return w[:, c * CH:(c + 1) * CH].rearrange("(k p) n -> p k n", p=P)

        def raw_slot(n):
            return raw[:, n % 2, :].rearrange("p (k n) -> p k n", k=KD)

        def w_slot(t, w):
            return t[:, w % 2, :].rearrange("p (k n) -> p k n", k=KD)

        def acc_read(eng, i):
            if i < 4:
                eng.wait_ge(s_acc_a, i + 1)
            elif i < 12:
                eng.wait_ge(s_acc_d, i - 3)
            else:
                eng.wait_ge(s_acc_a, i - 7)

        def w_used(eng, w):
            if w < 6:
                eng.wait_ge(s_acc, 4 * (w + 1) if w < 5 else 25)
            else:
                eng.wait_ge(s_mo, NT)

        def overflow_chunks(eng):
            eng.wait_ge(s_over, 1)
            return eng.value_load(over_i[0:1, 0:1], min_val=0, max_val=MORE)

        T_ORDER = [NT - 1] + list(range(NT - 1))

        def cond_of(t):
            return 1 if t == NT - 1 else 0

        @block.sync
        def _(sp):
            sp.dma_start(const[:, :], ins["const"]).then_inc(s_const, 16)

            def load_chunk(n):
                if n - 2 in ADA_N:
                    sp.wait_ge(s_ada, ADA_N.index(n - 2) + 1)
                elif n - 2 in SPLIT_N:
                    sp.wait_ge(s_wlo, SPLIT_N.index(n - 2) + 1)
                sp.dma_start(raw_slot(n), chunk_src(*stream[n])).then_inc(s_raw[n % 2], 16)

            load_chunk(0)
            load_chunk(1)
            sp.dma_start(x_nat[:, 0:TS, :], ins["x_sample"][0].rearrange("(t p) d -> p t d", p=P)).then_inc(s_x, 16)
            sp.dma_start(x_nat[:, TS, :], ins["x_prompt"][0]).then_inc(s_x, 16)
            for n in range(2, NCH):
                load_chunk(n)
            def expert_in(e, slot):
                sp.wait_ge(s_wlo, e + E0 - 1)
                sp.dma_start(raw_slot(slot), we_in[e].rearrange("(k p) n -> p k n", p=P)).then_inc(s_raw[slot], 16)

            def expert_out(e, slot, first):
                if first:
                    sp.wait_ge(s_slot, 1)
                else:
                    sp.wait_ge(s_olo, e - 1)
                sp.dma_start(raw_o[:, slot, :].rearrange("p (k n) -> p k n", k=2),
                             we_out[e].rearrange("(k p) n -> p k n", p=P)).then_inc(s_rawo[slot], 16)

            for b in range(2):
                expert_in(b, b)
            for b in range(2):
                expert_out(b, b, True)
            with sp.Fori(1, NE // 2) as i:
                for b in range(2):
                    expert_in(2 * i + b, b)
                    expert_out(2 * i + b, b, False)
            sp.wait_ge(s_wlo, E0 + NE - 1)
            for j in range(2):
                sp.dma_start(fin_v[:, j, :].rearrange("p (s c) -> p s c", s=KD),
                             dap(mod_dram, (3 * KD * 2 + j) * P, [[0, P], [2 * P, KD], [1, P]])).then_inc(s_fv, 16)
            sp.dma_start(fin_v[:, 2, :], dap(ins["ln2_g"], 0, [[0, P], [1, D]])).then_inc(s_fv, 16)
            sp.dma_start(fin_v[:, 3, :], dap(ins["ln2_b"], 0, [[0, P], [1, D]])).then_inc(s_fv, 16)
            for n, t in enumerate(T_ORDER):
                sp.wait_ge(s_fin, n + 1)
                dst = outs["y_prompt"][0] if t == NT - 1 else outs["y_sample"][0][t * P:(t + 1) * P, :]
                sp.dma_start(dst, x1[:, t, :]).then_inc(s_done, 16)
            sp.wait_ge(s_done, 16 * NT)
            sp.wait_ge(s_cache, 32)

        @block.gpsimd
        def _(pool):
            nc.gpsimd.memset(rows[:, :], 0.0).then_inc(s_rpz, 1)
            nc.gpsimd.memset(rp_pad, 0.0).then_inc(s_rpz, 1)
            nc.gpsimd.memset(eps, EPS).then_inc(s_rpz, 1)
            pool.wait_ge(s_rpz, 3)
            pool.dma_start(rows[0:48, :], ins["b_ada"][0].rearrange("(s c) -> s c", c=P)).then_inc(s_small, 16)
            pool.dma_start(rows[64:76, :], ins["conv_w"][0].rearrange("k (m c) -> (k m) c", c=P)).then_inc(s_small, 16)
            pool.dma_start(rows[96:104, :], ins["c"][0].rearrange("(k c) -> k c", c=P)).then_inc(s_small, 16)
            pool.dma_start(rows[104:112, :], ins["c_ctx"].rearrange("(k c) -> k c", c=P)).then_inc(s_small, 16)
            pool.dma_start(rp_pad[0:HEADS * DR, RP0:RP0 + 2 * CB - 1],
                           ins["rpb"][0].rearrange("h r c -> (h r) c")).then_inc(s_rp, 16)
            pool.dma_start(ck_nat.rearrange("p a (h d) -> p a h d", h=HEADS)[:, 0],
                           ins["cache_k"][0, 0][:, 0:P, :].rearrange("h t d -> t h d")).then_inc(s_ck, 16)
            pool.dma_start(ck_nat.rearrange("p a (h d) -> p a h d", h=HEADS)[:, 1],
                           ins["cache_k"][0, 0][:, P:2 * P, :].rearrange("h t d -> t h d")).then_inc(s_ck, 16)
            pool.dma_start(wr[:, :, 0:NG], ins["w_router_group"][0].rearrange("(k p) n -> p k n", p=P)).then_inc(s_wrl, 16)
            pool.dma_start(wr[:, :, NG:NG + NE], ins["w_router_expert"][0].rearrange("(k p) n -> p k n", p=P)).then_inc(s_wrl, 16)
            pool.dma_start(rb[:, 0:NG], dap(ins["b_router_group"], 0, [[0, P], [1, NG]])).then_inc(s_rb, 16)
            pool.dma_start(rb[:, NG:NG + NE], dap(ins["b_router_expert"], 0, [[0, P], [1, NE]])).then_inc(s_rb, 16)
            pool.wait_ge(s_rp, 16)
            pool.dma_start(rp_dram, rp_pad[0:HEADS * DR, :]).then_inc(s_rp, 16)
            pool.wait_ge(s_rp, 32)
            for h in range(HEADS):
                for a in range(3):
                    src = dap(rp_dram, h * DR * RPW + RP0 - CB + 8 * a, [[1, CB], [RPW, DR], [1, SPAN]])
                    pool.dma_start(bias_t[CB * h:CB * h + CB, a, :, :], src).then_inc(s_bt, 16)
            pool.wait_ge(s_silu, 2)
            nc.gpsimd.memset(silu_t, 0.0).then_inc(s_rpz, 1)
            pool.wait_ge(s_rows, 1)
            nc.gpsimd.memset(ones[:, :], 1.0).then_inc(s_rpz, 1)
            pool.wait_ge(s_rpz, 5)
            pool.dma_start(list_dram.rearrange("(p n) a -> p (n a)", p=P), silu_t[:, 0:SLOTS // P]).then_inc(s_lz, 16)
            pool.wait_ge(s_bm, 1)
            pool.dma_start(bias_dram, bias_t.rearrange("p a r k -> p (a r k)")).then_inc(s_bd, 16)
            pool.wait_ge(s_bd, 16)

            def load_bias(h):
                if h >= 2:
                    pool.wait_ge(s_nm, NB * (h - 1))
                for a in range(3):
                    src = dap(bias_dram, h * CB * 3 * TW + a * TW,
                              [[SPAN, ROWS], [3 * TW, CB], [1, LOC]])
                    pool.dma_start(bias_s[:, h % 2, a, :], src).then_inc(s_bias[h % 2], 16)

            pool.wait_ge(s_clo, 1)
            pool.wait_ge(s_lz, 16)
            for b in range(2):
                pool.wait_ge(s_vout[b], 16 * (TS // 2))
            for n in range(NB):
                for j in range(2):
                    src = dap(v_dram, (j * 4 * GRID + KEY0[n]) * AW, [[GRID * AW, 4], [AW, SPAN], [1, AW]])
                    pool.dma_start(vblk[:, 2 * n + j, :], src).then_inc(s_vb, 16)
            for j in range(2):
                pool.dma_start(ctx_v[:, j, :].rearrange("p (h d) -> p h d", h=HEADS),
                               ins["cache_v"][0, 0][:, j * P:(j + 1) * P, :].rearrange("h t d -> t h d")).then_inc(s_vb, 16)
            for h in range(HEADS):
                load_bias(h)
                if h == 1:
                    for j in range(2):
                        r0 = (NE + j * MORE // 2) * CAP
                        pool.dma_start(y_dram[r0:r0 + MORE // 2 * CAP, :].rearrange("(p a) d -> p (a d)", p=P),
                                       g1[:, :]).then_inc(s_yz, 16)
            pool.wait_ge(s_mrd, 16)
            pool.wait_ge(s_yz, 32)
            pool.wait_ge(s_mlo, HP + 1)
            pool.dma_start(x1[:, NT - 1, :], ins["x_prompt"][0]).then_inc(s_xr[1], 16)
            for j in (1, 0):
                for v, dst in ((0, gate_a), (2, lin_a), (1, lin_b)):
                    pool.dma_start(dst[:, j, :].rearrange("p (s c) -> p s c", s=KD),
                                   dap(mod_dram, (v * KD * 2 + j) * P, [[0, P], [2 * P, KD], [1, P]])).then_inc(s_vec[j], 16)
                if j == 1:
                    pool.dma_start(ln1_g, dap(ins["ln1_g"], 0, [[0, P], [1, D]])).then_inc(s_vec[j], 16)
                    pool.dma_start(ln1_b, dap(ins["ln1_b"], 0, [[0, P], [1, D]])).then_inc(s_vec[j], 16)
            pool.dma_start(x1[:, 0:TS, :], ins["x_sample"][0].rearrange("(t p) d -> p t d", p=P)).then_inc(s_xr[0], 16)
            for n, t in enumerate(T_ORDER):
                pool.wait_ge(s_xn, n + 1)
                nc.gpsimd.tensor_tensor(x1[:, t, :], ln_t[:, n % 2, :], ln1_g, ALU.mult).then_inc(s_plc, 1)
                pool.wait_ge(s_plc, n + 1)
                nc.gpsimd.tensor_tensor(x1[:, t, :], x1[:, t, :], ln1_b, ALU.add).then_inc(s_x1, 1)
                pool.wait_ge(s_h2, n + 1)
                pool.dma_start(h2_dram[t * P:(t + 1) * P, :], ln_t[:, n % 2, :]).then_inc(s_h2s[n % 2], 16)
            pool.wait_ge(s_slot, 1)
            for c in range(2):
                for t in range(NT):
                    pool.indirect_dma_start(list_dram, bass.IndirectOffsetOnAxis(ap=slot_i[:, c, t:t + 1], axis=0),
                                            const[:, C_TOK + t:C_TOK + t + 1], None).then_inc(s_lst, 16)
            pool.wait_ge(s_lst, 16 * 2 * NT)
            pool.dma_start(list_r[0:NE + MORE, :], list_dram.rearrange("(e p) a -> e (p a)", p=CAP)).then_inc(s_ll, 16)
            pool.wait_ge(s_lc, 1)
            for b in range(2):
                pool.wait_ge(s_h2s[b], 16 * (NT // 2 + 1 - b))

            def gather(c, b, col):
                pool.indirect_dma_start(hg[:, b, :], None, h2_dram,
                                        bass.IndirectOffsetOnAxis(ap=col, axis=0)).then_inc(s_hg[b], 16)

            def store_rows(c):
                pool.wait_ge(s_ya, c + 1)
                pool.wait_ge(s_yd, c + 1)
                pool.dma_start(y_dram[c * CAP:(c + 1) * CAP, :], y_sb[:, c % 2, :]).then_inc(s_yst[c % 2], 16)

            for c in range(NE):
                if c >= 2:
                    pool.wait_ge(s_hgt, c - 1)
                gather(c, c % 2, list_s[:, c:c + 1])
                if c >= 3:
                    store_rows(c - 3)
            for c in range(NE - 3, NE):
                store_rows(c)
            more = overflow_chunks(pool)
            with pool.If(more > 0):
                with pool.Fori(0, more) as i:
                    pool.wait_ge(s_hgt, i + NE)
                    nc.gpsimd.tensor_copy(over_col[:, :], list_s[:, bass.ds(i + NE, 1)]).then_inc(s_ovc, 1)
                    with pool.If(more > 0):
                        pool.wait_ge(s_ovc, i + 1)
                    pool.indirect_dma_start(hg[:, 1, :], None, h2_dram,
                                            bass.IndirectOffsetOnAxis(ap=over_col[:, 0:1], axis=0)).then_inc(s_ovg, 16)
                    pool.wait_ge(s_ya, i + (NE + 1))
                    pool.wait_ge(s_yd, i + (NE + 1))
                    pool.dma_start(y_dram[bass.ds((i + NE) * CAP, CAP), :], y_sb[:, 1, :]).then_inc(s_ovs, 16)
                    pool.wait_ge(s_ovs, 16 * i + 16)
            for b in range(2):
                pool.wait_ge(s_yst[b], 16 * (NE // 2))
            pool.wait_ge(s_wlo, E0 + NE)
            def token_rows(n):
                t = T_ORDER[n]
                if n >= 2:
                    pool.wait_ge(s_fin, n - 1)
                for c in range(2):
                    pool.indirect_dma_start(fin_y[:, n % 2, c, :], None, y_dram,
                                            bass.IndirectOffsetOnAxis(ap=slot_i[:, c, t:t + 1], axis=0)).then_inc(s_fy[n % 2], 16)

            token_rows(0)
            token_rows(1)
            for n in range(2, NT):
                token_rows(n)

        @block.scalar
        def _(act):
            act.wait_ge(s_small, 64)
            nc.scalar.activation(silu_t[96:112, :], rows[96:112, :], ACT.Exp, scale=-1.0).then_inc(s_silu, 1)

            def split_hi(w, n):
                raw_full(act, n)
                if w >= 2:
                    w_used(act, w - 2)
                nc.scalar.activation(w_hi[:, w % 2, :], raw[:, n % 2, :], ACT.Copy).then_inc(s_whi, 1)

            split_hi(0, SPLIT_N[0])
            for k in range(KD):
                act.wait_ge(s_h, k + 1)
                nc.scalar.activation(h_hi[:, k, :], h_tmp[:, k % 2, :], ACT.Copy).then_inc(s_hhi, 1)
            split_hi(1, SPLIT_N[1])

            def q_back(m, r0, r1):
                return bass.AP(tensor=g1, offset=m * TOK + P - 1 - CB * r0,
                               ap=[[NT * D, P], [-CB, r1 - r0], [P, NB], [-1, CB]])

            def evac(i):
                act.wait_ge(s_acc, i + 1)
                w, m = divmod(i, 4)
                b = 2 * (i % 2)
                if w == 0:
                    nc.scalar.activation(conv_y[:, m, 1:1 + HALF], PS[:, b, 0:HALF], ACT.Copy)
                    nc.scalar.activation(conv_y[:, m, 1 + HALF:1 + NS], PS[:, b + 1, 0:NS - HALF], ACT.Copy)
                    nc.scalar.activation(conv_y[:, m, 2 + NS:2 + TOK], PS[:, b + 1, NS - HALF:HALF], ACT.Copy).then_inc(s_acc_a, 1)
                elif w == 3:
                    r0 = HALF // GRID
                    nc.scalar.activation(q_back(m, 0, r0), PS[:, b, 0:HALF].rearrange("p (r n c) -> p r n c", n=NB, c=CB),
                                         ACT.Copy, scale=DH ** -0.5)
                    nc.scalar.activation(q_back(m, r0, ROWS), PS[:, b + 1, 0:NS - HALF].rearrange("p (r n c) -> p r n c", n=NB, c=CB),
                                         ACT.Copy, scale=DH ** -0.5)
                    nc.scalar.activation(qT[:, m, NS:TOK], PS[:, b + 1, NS - HALF:HALF], ACT.Copy,
                                         scale=DH ** -0.5).then_inc(s_acc_a, 1)
                elif w == 4:
                    nc.scalar.activation(kT[:, m, 0:HALF], PS[:, b, 0:HALF], ACT.Copy)
                    nc.scalar.activation(kT[:, m, HALF:TOK], PS[:, b + 1, 0:HALF], ACT.Copy).then_inc(s_acc_a, 1)
                else:
                    t = i - 20
                    if t >= 2:
                        act.wait_ge(s_vout[t % 2], 16 * (t // 2))
                    nc.scalar.activation(stage[:, t % 2, :], PS[:, b, :], ACT.Copy).then_inc(s_acc_a, 1)
                    act.wait_ge(s_acc_a, i - 7)
                    if t < TS:
                        act.dma_start(v_dram[t * P:(t + 1) * P, :], stage[:, t % 2, :]).then_inc(s_vout[t % 2], 16)
                    else:
                        act.dma_start(outs["new_v"][0, 0].rearrange("h s d -> s h d"),
                                      stage[:, t % 2, :].rearrange("p (h d) -> p h d", h=HEADS)).then_inc(s_cache, 16)

            for m in range(4):
                evac(m)
            for w in range(2, 6):
                split_hi(w, SPLIT_N[w])
                if w - 1 in (3, 4):
                    for m in range(4):
                        evac(4 * (w - 1) + m)
            for t in range(NT):
                evac(20 + t)
            act.wait_ge(s_kp, 1)
            act.wait_ge(s_vout[1], 32)
            nc.scalar.activation(stage[:, 1, :], PS[:, 6, :], ACT.Copy).then_inc(s_kps, 1)
            act.wait_ge(s_kps, 1)
            act.dma_start(outs["new_k"][0, 0].rearrange("h s d -> s h d"),
                          stage[:, 1, :].rearrange("p (h d) -> p h d", h=HEADS)).then_inc(s_cache, 16)
            act.wait_ge(s_acc_d, 8)
            act.wait_ge(s_acc, 25)
            nc.scalar.activation(h_hi[:, 4:8, 0:NS], conv_o[:, :, 1:1 + NS], ACT.Copy)
            nc.scalar.activation(h_hi[:, 4:8, NS:TOK], conv_o[:, :, 2 + NS:2 + TOK], ACT.Copy).then_inc(s_chi, 1)
            act.wait_ge(s_mrow, 1)
            nc.scalar.activation(cols[0:64, :], PS[0:64, 0, 0:P], ACT.Copy).then_inc(s_mrs, 1)
            act.wait_ge(s_mrs, 1)
            act.dma_start(mod_dram, cols[0:64, :]).then_inc(s_mrd, 16)
            split_hi(6, SPLIT_N[6])
            split_hi(7, SPLIT_N[7])

            def exps(u):
                act.wait_ge(s_nm, u + 1)
                if u >= 2:
                    act.wait_ge(s_pt, u - 1)
                if u < UNITS:
                    nc.scalar.activation(prob[:, u % 2, :], PS[:, u % 2, :], ACT.Exp, bias=nmax[:, u % 2, 0:1],
                                         accum_out=rsum[:, u % 4, 0:1]).then_inc(s_p, 1)
                else:
                    for j in range(4):
                        a = nc.scalar.activation(prob[:, u % 2, j * P:(j + 1) * P], PS[:, u % 2, j * P:(j + 1) * P], ACT.Exp,
                                                 bias=nmax[:, u % 2, j:j + 1], accum_out=rsum[:, u % 4, j:j + 1])
                    a.then_inc(s_p, 1)

            def copy_pt(u):
                act.wait_ge(s_pt, u + 1)
                if u >= 2:
                    act.wait_ge(s_o, u - 1)
                nc.scalar.activation(prob_T[:, u % 2, :], PS[:, 2 + u % 2, :], ACT.Copy).then_inc(s_pts, 1)

            def mix_hi(g):
                act.wait_ge(s_ot, g + 1)
                src = PS[:, 6 + g % 2, :]
                if g < HP:
                    s4 = src.rearrange("p (n r c) -> p n r c", n=NB, r=ROWS)
                    d4 = h_hi[:, g, 0:NS].rearrange("p (r n c) -> p n r c", n=NB, r=ROWS)
                    for n in range(NB):
                        a = nc.scalar.activation(d4[:, n], s4[:, n], ACT.Copy)
                    a.then_inc(s_mhi, 1)
                else:
                    nc.scalar.activation(h_hi[:, 0:HP, NS:TOK], src.rearrange("p (m t) -> p m t", m=HP), ACT.Copy).then_inc(s_mhi, 1)

            for u in range(NU + 1):
                if u < NU:
                    exps(u)
                if u >= 1:
                    copy_pt(u - 1)
                if u >= 3 and (u - 3) % 8 == 7 and u - 3 < UNITS:
                    mix_hi((u - 3) // 8)
            mix_hi(HP)

            def h2_copy(n):
                act.wait_ge(s_h2t, n + 1)
                if n >= 1:
                    act.wait_ge(s_lg, n)
                else:
                    act.wait_ge(s_mlo, HP + 1)
                nc.scalar.activation(h2_T[:, 0:4, :], PS[:, 4, :].rearrange("p (k t) -> p k t", k=4), ACT.Copy)
                nc.scalar.activation(h2_T[:, 4:8, :], PS[:, 5, :].rearrange("p (k t) -> p k t", k=4), ACT.Copy).then_inc(s_h2c, 1)

            def root(n):
                act.wait_ge(s_var, n + 1)
                nc.scalar.activation(std, mv[:, 1:2], ACT.Sqrt, bias=eps).then_inc(s_std, 1)

            root(0)
            for n in range(1, NT):
                h2_copy(n - 1)
                root(n)
            h2_copy(NT - 1)

            def expert_whi(e, b, first=False):
                act.wait_ge(s_raw[b], 16 * (NCH // 2 + 1) + 8 * (e - b))
                if first:
                    act.wait_ge(s_mo, NT)
                else:
                    act.wait_ge(s_hid, e - 1)
                nc.scalar.activation(w_hi[:, b, :], raw[:, b, :], ACT.Copy).then_inc(s_whi, 1)

            def expert_ohi(e, b, first=False):
                act.wait_ge(s_rawo[b], 16 + 8 * (e - b))
                if not isinstance(e, int) or e >= 1:
                    act.wait_ge(s_y, e)
                nc.scalar.activation(wo_hi, raw_o[:, b, :].rearrange("p (k n) -> p k n", k=2), ACT.Copy).then_inc(s_ohi, 1)

            def gathered_hi(c, b):
                act.wait_ge(s_hgt, c + 1)
                if not isinstance(c, int) or c >= 2:
                    act.wait_ge(s_hid, c - 1)
                nc.scalar.activation(hgT_hi[:, b, 0:4, :], PS[:, 2, :].rearrange("p (k t) -> p k t", k=4), ACT.Copy)
                nc.scalar.activation(hgT_hi[:, b, 4:8, :], PS[:, 3, :].rearrange("p (k t) -> p k t", k=4), ACT.Copy).then_inc(s_ghi, 1)

            def exp_neg(c, b):
                act.wait_ge(s_hid, c + 1)
                nc.scalar.activation(sil[:, 0, :], PS[:, b, 0:DE], ACT.Exp, scale=-1.0).then_inc(s_ex, 1)

            def act_hi_copy(c, b):
                act.wait_ge(s_at, c + 1)
                nc.scalar.activation(aT_hi[:, b, :, :], PS[:, 4, 0:2 * P].rearrange("p (k t) -> p k t", k=2), ACT.Copy).then_inc(s_ahi, 1)

            def y_copy(c, b):
                act.wait_ge(s_y, c + 1)
                if not isinstance(c, int) or c >= 2:
                    act.wait_ge(s_yst[b], 8 * (c - b))
                nc.scalar.activation(y_sb[:, b, 0:CH], PS[:, 6, :], ACT.Copy).then_inc(s_ya, 1)

            act.wait_ge(s_one, 1)
            nc.scalar.activation(rt[:, 0:NG * NT], rt[:, 0:NG * NT], ACT.Exp)
            nc.scalar.activation(rt[:, 900:900 + NT], rt[:, 900:900 + NT], ACT.Exp).then_inc(s_gexp, 1)

            expert_whi(0, 0, True)
            expert_whi(1, 1, True)
            gathered_hi(0, 0)

            def act_pair(i, last=False):
                for b in range(2):
                    c = 2 * i + b
                    exp_neg(c, b)
                    if not (isinstance(c, int) and c == 0):
                        y_copy(c - 1, 1 - b)
                    if not (last and b == 1):
                        gathered_hi(c + 1, 1 - b)
                    expert_ohi(c, b)
                    act_hi_copy(c, b)
                    if not last:
                        expert_whi(c + 2, b)

            act_pair(0)
            with act.Fori(1, NE // 2 - 1) as i:
                act_pair(i)
            act_pair(NE // 2 - 1, True)
            y_copy(NE - 1, 1)
            more = overflow_chunks(act)
            with act.If(more > 0):
                act.wait_ge(s_yst[1], 16 * (NE // 2))
                with act.Fori(0, more) as i:
                    e = act.value_load(over_i[0:1, bass.ds(i + 1, 1)], min_val=0, max_val=NE - 1)
                    act.wait_ge(s_wlo, i + (E0 + NE))
                    act.wait_ge(s_olo, i + NE)
                    act.dma_start(raw_slot(1), we_in[e].rearrange("(k p) n -> p k n", p=P)).then_inc(s_ovw, 16)
                    act.dma_start(raw_o[:, 1, :].rearrange("p (k n) -> p k n", k=2),
                                  we_out[e].rearrange("(k p) n -> p k n", p=P)).then_inc(s_ovw, 16)
                    act.wait_ge(s_ovw, 32 * i + 32)
                    act.wait_ge(s_hid, i + NE)
                    nc.scalar.activation(w_hi[:, 1, :], raw[:, 1, :], ACT.Copy).then_inc(s_whi, 1)
                    act.wait_ge(s_y, i + NE)
                    nc.scalar.activation(wo_hi, raw_o[:, 1, :].rearrange("p (k n) -> p k n", k=2), ACT.Copy).then_inc(s_ohi, 1)
                    gathered_hi(i + NE, 1)
                    exp_neg(i + NE, 1)
                    act_hi_copy(i + NE, 1)
                    act.wait_ge(s_y, i + (NE + 1))
                    nc.scalar.activation(y_sb[:, 1, 0:CH], PS[:, 6, :], ACT.Copy).then_inc(s_ya, 1)
            for n in range(NT):
                root(NT + n)

        @block.vector
        def _(dve):
            chain = [0]

            def link(ins_):
                chain[0] += 1
                ins_.then_inc(s_dv, 1)
                dve.wait_ge(s_dv, chain[0])

            V = nc.vector
            dve.wait_ge(s_silu, 1)
            link(V.tensor_scalar(silu_t[96:112, :], silu_t[96:112, :], 1.0, None, ALU.add))
            link(V.reciprocal(silu_t[96:112, :], silu_t[96:112, :]))
            V.tensor_tensor(rows[96:112, :], rows[96:112, :], silu_t[96:112, :], ALU.mult).then_inc(s_silu, 1)
            dve.wait_ge(s_rows, 1)
            V.tensor_copy(cols[:, :], PS[:, 0, 0:P]).then_inc(s_cols, 1)
            dve.wait_ge(s_const, 16)
            dve.wait_ge(s_bt, 16 * 3 * HEADS)
            for a in range(3):
                m = V.tensor_tensor(bias_t[:, a, :, :], bias_t[:, a, :, :],
                                    mask3[:, a, :].unsqueeze(1).to_broadcast([P, DR, SPAN]), ALU.add)
            m.then_inc(s_bm, 1)

            def split_lo(w, n):
                dve.wait_ge(s_whi, w + 1)
                V.tensor_tensor(w_lo[:, w % 2, :], raw[:, n % 2, :], w_hi[:, w % 2, :].bitcast(fp32), ALU.subtract).then_inc(s_wlo, 1)

            dve.wait_ge(s_cols, 1)
            dve.wait_ge(s_ada, 4)
            link(V.tensor_tensor(modc[:, 0:16, :], PS[:, 1, 0:32].rearrange("p (s j) -> p s j", j=2),
                                 cols[:, 0:16].unsqueeze(2).to_broadcast([P, 16, 2]), ALU.add))
            link(V.tensor_scalar(modc[:, 8:16, :], modc[:, 8:16, :], 1.0, None, ALU.add))
            for k in range(KD + 1):
                if k < KD:
                    dve.wait_ge(s_xt, k + 1)
                    if k >= 2:
                        dve.wait_ge(s_hhi, k - 1)
                        dve.wait_ge(s_hlo, k - 1)
                    b = 4 + 2 * (k % 2)
                    V.tensor_scalar(h_tmp[:, k % 2, 0:NS], PS[:, b, :], modc[:, 8 + k, 0:1], modc[:, k, 0:1], ALU.mult, ALU.add)
                    V.tensor_scalar(h_tmp[:, k % 2, NS:TOK], PS[:, b + 1, 0:NP], modc[:, 8 + k, 1:2], modc[:, k, 1:2], ALU.mult, ALU.add).then_inc(s_h, 1)
                if k >= 1:
                    dve.wait_ge(s_hhi, k)
                    V.tensor_tensor(h_lo[:, k - 1, :], h_tmp[:, (k - 1) % 2, :], h_hi[:, k - 1, :].bitcast(fp32), ALU.subtract).then_inc(s_hlo, 1)
                if k == 3:
                    split_lo(0, SPLIT_N[0])
            split_lo(1, SPLIT_N[1])
            for at in (0, NS + 1, TOK + 2):
                link(V.memset(conv_y[:, :, at:at + 1], 0.0))
            for m in range(4):
                dve.wait_ge(s_acc_a, m + 1)
                dve.wait_ge(s_acc, 5 + m)
                b = 2 * (m % 2)
                V.tensor_tensor(conv_y[:, m, 1:1 + HALF], PS[:, b, 0:HALF], conv_y[:, m, 1:1 + HALF], ALU.mult)
                V.tensor_tensor(conv_y[:, m, 1 + HALF:1 + NS], PS[:, b + 1, 0:NS - HALF], conv_y[:, m, 1 + HALF:1 + NS], ALU.mult)
                V.tensor_tensor(conv_y[:, m, 2 + NS:2 + TOK], PS[:, b + 1, NS - HALF:HALF],
                                conv_y[:, m, 2 + NS:2 + TOK], ALU.mult).then_inc(s_acc_d, 1)
                if m == 1:
                    split_lo(2, SPLIT_N[2])
            dve.wait_ge(s_acc_d, 4)
            for m in range(4):
                link(V.tensor_scalar(conv_o[:, m, 1:2 + TOK], conv_y[:, m, 0:1 + TOK], cols[:, 64 + m:65 + m], None, ALU.mult))
                for tap in (1, 2):
                    link(V.scalar_tensor_tensor(out=conv_o[:, m, 1:2 + TOK], in0=conv_y[:, m, tap:tap + 1 + TOK],
                                                scalar=cols[:, 64 + 4 * tap + m:65 + 4 * tap + m], in1=conv_o[:, m, 1:2 + TOK],
                                                op0=ALU.mult, op1=ALU.add))
                if m == 1:
                    split_lo(3, SPLIT_N[3])
            for m in range(4):
                dve.wait_ge(s_acc, 9 + m)
                b = 2 * (m % 2)
                V.tensor_tensor(conv_o[:, m, 1:1 + HALF], PS[:, b, 0:HALF], conv_o[:, m, 1:1 + HALF], ALU.mult)
                V.tensor_tensor(conv_o[:, m, 1 + HALF:1 + NS], PS[:, b + 1, 0:NS - HALF], conv_o[:, m, 1 + HALF:1 + NS], ALU.mult)
                V.tensor_tensor(conv_o[:, m, 2 + NS:2 + TOK], PS[:, b + 1, NS - HALF:HALF],
                                conv_o[:, m, 2 + NS:2 + TOK], ALU.mult).then_inc(s_acc_d, 1)
            split_lo(4, SPLIT_N[4])
            split_lo(5, SPLIT_N[5])
            dve.wait_ge(s_ckt, 1)
            dve.wait_ge(s_bd, 16)
            for j in range(2):
                a = V.tensor_copy(ck_T[:, 2 * j:2 * j + 2, :], PS[:, 4 + j, :].rearrange("p (m t) -> p m t", m=2))
            a.then_inc(s_cks, 1)
            dve.wait_ge(s_chi, 1)
            V.tensor_tensor(h_lo[:, 4:8, 0:NS], conv_o[:, :, 1:1 + NS], h_hi[:, 4:8, 0:NS].bitcast(fp32), ALU.subtract)
            V.tensor_tensor(h_lo[:, 4:8, NS:TOK], conv_o[:, :, 2 + NS:2 + TOK],
                            h_hi[:, 4:8, NS:TOK].bitcast(fp32), ALU.subtract).then_inc(s_clo, 1)
            dve.wait_ge(s_ada, NA)
            V.tensor_tensor(modc[:, 16:48, :], PS[:, 7, 0:64].rearrange("p (s j) -> p s j", j=2),
                            cols[:, 16:48].unsqueeze(2).to_broadcast([P, 32, 2]), ALU.add).then_inc(s_mod, 1)
            split_lo(6, SPLIT_N[6])
            split_lo(7, SPLIT_N[7])

            def softmax_max(u):
                dve.wait_ge(s_s, u + 1)
                if u >= 2:
                    dve.wait_ge(s_p, u - 1)
                if u < UNITS:
                    h, n = u // NB, u % NB
                    if n == 0:
                        dve.wait_ge(s_bias[h % 2], 48 * (h // 2 + 1))
                    link(V.tensor_tensor(PS[:, u % 2, 0:LOC], PS[:, u % 2, 0:LOC], bias_s[:, h % 2, KIND[n], :], ALU.add))
                    V.tensor_reduce(nmax[:, u % 2, 0:1], PS[:, u % 2, :], AX.X, ALU.max, negate=True).then_inc(s_nm, 1)
                else:
                    V.tensor_reduce(nmax[:, u % 2, :], PS[:, u % 2, :].rearrange("p (j t) -> p j t", j=4), AX.X, ALU.max,
                                    negate=True).then_inc(s_nm, 1)

            def scale_out(u):
                dve.wait_ge(s_p, u + 1)
                dve.wait_ge(s_o, u + 1)
                if u < UNITS:
                    h, n = u // NB, u % NB
                    g = h // 2
                    if g >= 2 and u % 8 == 0:
                        dve.wait_ge(s_ot, g - 1)
                    link(V.reciprocal(rinv[:, u % 2, 0:1], rsum[:, u % 4, 0:1]))
                    V.tensor_scalar(att_o[:, g % 2, n, (h % 2) * DH:(h % 2 + 1) * DH], PS[:, 4 + u % 2, 0:DH],
                                    rinv[:, u % 2, 0:1], None, ALU.mult).then_inc(s_os, 1)
                else:
                    j = u - UNITS
                    if j == 0:
                        dve.wait_ge(s_ot, HP - 1)
                    link(V.reciprocal(rinv[:, u % 2, :], rsum[:, u % 4, :]))
                    V.tensor_tensor(att_o[:, 0, :, j * DH:(j + 1) * DH],
                                    PS[:, 4 + u % 2, 0:4 * DH].rearrange("p (j d) -> p j d", j=4),
                                    rinv[:, u % 2, :].unsqueeze(2).to_broadcast([P, 4, DH]), ALU.mult).then_inc(s_os, 1)

            def mix_lo(g):
                dve.wait_ge(s_mhi, g + 1)
                src = PS[:, 6 + g % 2, :]
                if g < HP:
                    s4 = src.rearrange("p (n r c) -> p n r c", n=NB, r=ROWS)
                    for n in range(NB):
                        hh = h_hi[:, g, 0:NS].rearrange("p (r n c) -> p n r c", n=NB, r=ROWS)[:, n]
                        ll = h_lo[:, g, 0:NS].rearrange("p (r n c) -> p n r c", n=NB, r=ROWS)[:, n]
                        a = V.tensor_tensor(ll, s4[:, n], hh.bitcast(fp32), ALU.subtract)
                    a.then_inc(s_mlo, 1)
                else:
                    V.tensor_tensor(h_lo[:, 0:HP, NS:TOK], src.rearrange("p (m t) -> p m t", m=HP),
                                    h_hi[:, 0:HP, NS:TOK].bitcast(fp32), ALU.subtract).then_inc(s_mlo, 1)

            for u in range(NU + 2):
                if u < NU:
                    softmax_max(u)
                if u >= 2:
                    scale_out(u - 2)
                if u >= 4 and (u - 4) % 8 == 7 and u - 4 < UNITS:
                    mix_lo((u - 4) // 8)
            mix_lo(HP)

            def norm(t_, n):
                for j in range(2):
                    a = V.bn_stats(stat[:, 6 * j:6 * j + 6], t_[:, j * CH:(j + 1) * CH])
                link(a)
                V.bn_aggr(mv, stat).then_inc(s_var, 1)
                dve.wait_ge(s_std, n + 1)
                link(V.reciprocal(rstd, std))
                return V.tensor_scalar(t_, t_, mv[:, 0:1], rstd, ALU.subtract, ALU.mult)

            for n, t in enumerate(T_ORDER):
                j = cond_of(t)
                if n <= 1:
                    dve.wait_ge(s_vec[j], 80 if j == 1 else 48)
                    dve.wait_ge(s_xr[j], 16)
                    link(V.tensor_scalar(lin_a[:, j, :], lin_a[:, j, :], 1.0, None, ALU.add))
                    link(V.tensor_tensor(ln_t[:, 0, :] if n == 0 else ln_t[:, 1, :], ln1_b, lin_a[:, j, :], ALU.mult))
                    link(V.tensor_tensor(lin_b[:, j, :], lin_b[:, j, :], ln_t[:, 0, :] if n == 0 else ln_t[:, 1, :], ALU.add))
                    link(V.tensor_tensor(lin_a[:, j, :], lin_a[:, j, :], ln1_g, ALU.mult))
                if n >= 2:
                    dve.wait_ge(s_h2s[n % 2], 16 * (n // 2))
                    dve.wait_ge(s_h2t, n - 1)
                    dve.wait_ge(s_x1, n - 1)
                dve.wait_ge(s_mo, n + 1)
                b = 2 * (n % 2)
                row = ln_t[:, n % 2, :]
                V.tensor_tensor(row, PS[:, b:b + 2, :].rearrange("p a n -> p (a n)"), gate_a[:, j, :], ALU.mult).then_inc(s_mor, 1)
                dve.wait_ge(s_mor, n + 1)
                link(V.scalar_tensor_tensor(out=row, in0=x1[:, t, :], scalar=ALPHA, in1=row, op0=ALU.mult, op1=ALU.add))
                norm(row, n).then_inc(s_xn, 1)
                dve.wait_ge(s_plc, n + 1)
                link(V.tensor_tensor(row, row, lin_a[:, j, :], ALU.mult))
                V.tensor_tensor(row, row, lin_b[:, j, :], ALU.add).then_inc(s_h2, 1)

            L = logits[:, :, :]
            dve.wait_ge(s_lg, NT)
            for b in range(2):
                dve.wait_ge(s_h2s[b], 16 * (NT // 2 + 1 - b))
            dve.wait_ge(s_x1, NT)
            dve.wait_ge(s_rb, 32)
            link(V.tensor_tensor(L, PS[:, 6, 0:NT * (NG + NE)].rearrange("p (t n) -> p t n", t=NT),
                                 rb[:, :].unsqueeze(1).to_broadcast([P, NT, NG + NE]), ALU.add))

            def tile(at, *dims):
                n = 1
                for d in dims:
                    n *= d
                v = rt[:, at:at + NT * n]
                if len(dims) == 1:
                    return v.rearrange("p (t a) -> p t a", t=NT)
                return v.rearrange("p (t a b) -> p t a b", t=NT, a=dims[0])

            gexp, gmax, oh_g = tile(0, NG), tile(100, 1), tile(120, NG)
            tmp16, e4, oh1, oh2 = tile(200, NG, EG), tile(300, EG), tile(340, EG), tile(380, EG)
            m1, m2, e4b, tmp4 = tile(420, 1), tile(440, 1), tile(460, EG), tile(500, NG)
            d12 = rt[:, 900:900 + NT].rearrange("p (t a) -> p t a", t=NT)
            OH1, OH2, OHS = tile(540, NG, EG), tile(640, NG, EG), tile(740, NG, EG)
            rank = const[:, C_RANK:C_RANK + NG].unsqueeze(1).to_broadcast([P, NT, NG])

            def first_of(src, top, dst):
                link(V.tensor_tensor(dst, src, top.to_broadcast([P, NT, NG]), ALU.is_equal))
                link(V.tensor_tensor(dst, dst, rank, ALU.mult))
                link(V.tensor_reduce(tmp4[:, :, 0:1], dst, AX.X, ALU.max))
                link(V.tensor_tensor(dst, rank, tmp4[:, :, 0:1].to_broadcast([P, NT, NG]), ALU.is_equal))

            link(V.tensor_reduce(gmax, L[:, :, 0:NG], AX.X, ALU.max))
            first_of(L[:, :, 0:NG], gmax, oh_g)
            link(V.tensor_tensor(gexp, L[:, :, 0:NG], gmax.to_broadcast([P, NT, NG]), ALU.subtract))
            link(V.tensor_tensor(tmp16, L[:, :, NG:NG + NE].rearrange("p t (a b) -> p t a b", a=NG),
                                 oh_g.unsqueeze(3).to_broadcast([P, NT, NG, EG]), ALU.mult))
            link(V.tensor_reduce(e4, tmp16.rearrange("p t a b -> p t b a"), AX.X, ALU.add))
            link(V.tensor_reduce(m1, e4, AX.X, ALU.max))
            first_of(e4, m1, oh1)
            link(V.scalar_tensor_tensor(out=e4b, in0=oh1, scalar=-3.0e38, in1=e4, op0=ALU.mult, op1=ALU.add))
            link(V.tensor_reduce(m2, e4b, AX.X, ALU.max))
            first_of(e4b, m2, oh2)
            V.tensor_tensor(d12, m2, m1, ALU.subtract).then_inc(s_one, 1)
            for src, dst in ((oh1, OH1), (oh2, OH2)):
                for t in range(NT):
                    a = V.tensor_tensor(dst[:, t], oh_g[:, t, :].unsqueeze(2).to_broadcast([P, NG, EG]),
                                        src[:, t, :].unsqueeze(1).to_broadcast([P, NG, EG]), ALU.mult)
            link(a)
            V.tensor_tensor(OHS, OH1, OH2, ALU.add).then_inc(s_one, 1)
            dve.wait_ge(s_gexp, 1)
            gw = rt[:, 920:920 + 3 * NT].rearrange("p (a t) -> p a t", a=3)
            d12f = rt[:, 900:900 + NT]
            link(V.tensor_reduce(gw[:, 0, :], gexp, AX.X, ALU.add))
            link(V.scalar_tensor_tensor(out=gw[:, 1, :], in0=d12f, scalar=1.0, in1=gw[:, 0, :], op0=ALU.add, op1=ALU.mult))
            link(V.reciprocal(gates[:, 0, :], gw[:, 1, :]))
            link(V.tensor_tensor(gates[:, 1, :], gates[:, 0, :], d12f, ALU.mult))
            pos = rt[:, 1000:1000 + NT * NE].rearrange("p (t e) -> p t e", t=NT)
            cnt = rt[:, 1100:1100 + NE]
            ov = rt[:, 1120:1120 + NE]
            base = rt[:, 1140:1140 + NE]
            t16 = rt[:, 1160:1160 + NE]
            big = rt[:, 1200:1200 + NT * NE].rearrange("p (t e) -> p t e", t=NT)
            dve.wait_ge(s_pos, 1)
            link(V.tensor_copy(pos, PS[:, 7, 0:NT * NE].rearrange("p (t e) -> p t e", t=NT)))
            link(V.tensor_copy(cnt, PS[:, 7, NT * NE:(NT + 1) * NE]))
            link(V.tensor_scalar(ov, cnt, float(CAP), None, ALU.is_gt))
            for j in range(2, NT):
                link(V.tensor_scalar(t16, cnt, float(CAP * j), None, ALU.is_gt))
                link(V.tensor_tensor(ov, ov, t16, ALU.add))
            ends = rt[:, 1180:1180 + NE]
            link(V.memset(base[:, 0:1], 0.0))
            for e in range(1, NE):
                link(V.tensor_tensor(base[:, e:e + 1], base[:, e - 1:e], ov[:, e - 1:e], ALU.add))
            link(V.tensor_tensor(ends, base, ov, ALU.add))
            over_f = rt[:, 1300:1301 + MORE]
            le = rt[:, 1320:1320 + MORE * NE].rearrange("p (i e) -> p i e", i=MORE)
            link(V.tensor_tensor(le, ends.unsqueeze(1).to_broadcast([P, MORE, NE]),
                                 const[:, C_IOTA:C_IOTA + MORE].unsqueeze(2).to_broadcast([P, MORE, NE]), ALU.is_le))
            link(V.tensor_reduce(over_f[:, 1:1 + MORE], le, AX.X, ALU.add))
            link(V.tensor_scalar(over_f[:, 1:1 + MORE], over_f[:, 1:1 + MORE], float(NE - 1), None, ALU.min))
            link(V.tensor_copy(over_f[:, 0:1], ends[:, NE - 1:NE]))
            V.tensor_copy(over_i[:, :], over_f).then_inc(s_over, 1)
            link(V.tensor_scalar(base, base, float(CAP), None, ALU.mult))
            link(V.tensor_tensor(base, base, const[:, C_OVER:C_OVER + NE], ALU.add))
            link(V.tensor_scalar(big, pos, float(CAP), None, ALU.is_ge))
            link(V.tensor_tensor(big, big, base.unsqueeze(1).to_broadcast([P, NT, NE]), ALU.mult))
            link(V.tensor_tensor(pos, pos, big, ALU.add))
            link(V.tensor_tensor(pos, pos, const[:, C_E128:C_E128 + NE].unsqueeze(1).to_broadcast([P, NT, NE]), ALU.add))
            for c, oh in ((0, OH1), (1, OH2)):
                link(V.tensor_tensor(big, pos, oh.rearrange("p t a b -> p t (a b)"), ALU.mult))
                link(V.tensor_reduce(slot_f[:, c, :], big, AX.X, ALU.add))
            V.tensor_copy(slot_i[:, :, :], slot_f).then_inc(s_slot, 1)
            dve.wait_ge(s_lt, 1)
            V.tensor_copy(list_s, PS[:, 5, 0:NE + MORE]).then_inc(s_lc, 1)

            def expert_wlo(e, b):
                dve.wait_ge(s_whi, e + E0 + 1)
                V.tensor_tensor(w_lo[:, b, :], raw[:, b, :], w_hi[:, b, :].bitcast(fp32), ALU.subtract).then_inc(s_wlo, 1)

            def expert_olo(e, b):
                dve.wait_ge(s_ohi, e + 1)
                V.tensor_tensor(wo_lo, raw_o[:, b, :].rearrange("p (k n) -> p k n", k=2), wo_hi.bitcast(fp32),
                                ALU.subtract).then_inc(s_olo, 1)

            def gathered_lo(c, b):
                dve.wait_ge(s_ghi, c + 1)
                for j in range(2):
                    a = V.tensor_tensor(hgT_lo[:, b, 4 * j:4 * j + 4, :], PS[:, 2 + j, :].rearrange("p (k t) -> p k t", k=4),
                                        hgT_hi[:, b, 4 * j:4 * j + 4, :].bitcast(fp32), ALU.subtract)
                a.then_inc(s_glo, 1)

            def silu_up(c, b):
                dve.wait_ge(s_ex, c + 1)
                V.tensor_scalar(sil[:, 1, :], sil[:, 0, :], 1.0, None, ALU.add).then_inc(s_sl, 1)
                dve.wait_ge(s_sl, 4 * c + 1)
                V.reciprocal(sil[:, 1, :], sil[:, 1, :]).then_inc(s_sl, 1)
                dve.wait_ge(s_sl, 4 * c + 2)
                V.tensor_tensor(sil[:, 1, :], sil[:, 1, :], PS[:, b, 0:DE], ALU.mult).then_inc(s_sl, 1)
                dve.wait_ge(s_sl, 4 * c + 3)
                if not isinstance(c, int) or c >= 1:
                    dve.wait_ge(s_at, c)
                V.tensor_tensor(sil[:, 2, :], sil[:, 1, :], PS[:, b, DE:2 * DE], ALU.mult).then_inc(s_sl, 1)
                dve.wait_ge(s_sl, 4 * c + 4)

            def act_lo_sub(c, b):
                dve.wait_ge(s_ahi, c + 1)
                V.tensor_tensor(aT_lo[:, b, :, :], PS[:, 4, 0:2 * P].rearrange("p (k t) -> p k t", k=2),
                                aT_hi[:, b, :, :].bitcast(fp32), ALU.subtract).then_inc(s_alo, 1)

            def y_copy(c, b):
                dve.wait_ge(s_y, c + 1)
                if not isinstance(c, int) or c >= 2:
                    dve.wait_ge(s_yst[b], 8 * (c - b))
                V.tensor_copy(y_sb[:, b, CH:2 * CH], PS[:, 7, :]).then_inc(s_yd, 1)

            expert_wlo(0, 0)
            expert_wlo(1, 1)
            gathered_lo(0, 0)

            def dve_pair(i, last=False):
                for b in range(2):
                    c = 2 * i + b
                    silu_up(c, b)
                    if not (isinstance(c, int) and c == 0):
                        y_copy(c - 1, 1 - b)
                    if not (last and b == 1):
                        gathered_lo(c + 1, 1 - b)
                    expert_olo(c, b)
                    act_lo_sub(c, b)
                    if not last:
                        expert_wlo(c + 2, b)

            dve_pair(0)
            with dve.Fori(1, NE // 2 - 1) as i:
                dve_pair(i)
            dve_pair(NE // 2 - 1, True)
            y_copy(NE - 1, 1)
            more = overflow_chunks(dve)
            with dve.If(more > 0):
                dve.wait_ge(s_yst[1], 16 * (NE // 2))
                with dve.Fori(0, more) as i:
                    expert_wlo(i + NE, 1)
                    expert_olo(i + NE, 1)
                    gathered_lo(i + NE, 1)
                    silu_up(i + NE, 1)
                    act_lo_sub(i + NE, 1)
                    dve.wait_ge(s_y, i + (NE + 1))
                    V.tensor_copy(y_sb[:, 1, CH:2 * CH], PS[:, 7, :]).then_inc(s_yd, 1)

            dve.wait_ge(s_fv, 64)
            dve.wait_ge(s_x1, NT)
            for n, t in enumerate(T_ORDER):
                b = n % 2
                dve.wait_ge(s_fy[b], 32 * (n // 2 + 1))
                y1, y2, xt = fin_y[:, b, 0, :], fin_y[:, b, 1, :], x1[:, t, :]
                link(V.tensor_scalar(y1, y1, gates[:, 0, t:t + 1], None, ALU.mult))
                link(V.scalar_tensor_tensor(out=y1, in0=y2, scalar=gates[:, 1, t:t + 1], in1=y1, op0=ALU.mult, op1=ALU.add))
                link(V.tensor_tensor(y1, y1, fin_v[:, cond_of(t), :], ALU.mult))
                link(V.scalar_tensor_tensor(out=xt, in0=xt, scalar=ALPHA, in1=y1, op0=ALU.mult, op1=ALU.add))
                link(norm(xt, NT + n))
                link(V.tensor_tensor(xt, xt, fin_v[:, 2, :], ALU.mult))
                V.tensor_tensor(xt, xt, fin_v[:, 3, :], ALU.add).then_inc(s_fin, 1)

        @block.tensor
        def _(pe):
            T = nc.tensor

            def three(out, lh, ll, rh, rl, first, last):
                T.matmul(out, lh, rh, start=first, stop=False)
                T.matmul(out, lh, rl, start=False, stop=False)
                return T.matmul(out, ll, rh, start=False, stop=last)

            pe.wait_ge(s_const, 16)
            pe.wait_ge(s_silu, 2)
            T.transpose(PS[:, 0, 0:P], rows[:, :], ident).then_inc(s_rows, 1)

            def ada(a):
                n = ADA_N[a]
                raw_full(pe, n)
                for s in range(4 * a, 4 * a + 4):
                    out = PS[:, 1, 2 * s:2 * s + 2] if a < 4 else PS[:, 7, 2 * s - 32:2 * s - 30]
                    for k in range(KD):
                        m = T.matmul(out, raw_slot(n)[:, k, (s - 4 * a) * P:(s - 4 * a + 1) * P],
                                     cols[:, 96 + k:96 + k + KD + 1:KD], start=(k == 0), stop=(k == KD - 1))
                m.then_inc(s_ada, 1)

            pe.wait_ge(s_cols, 1)
            for a in range(4):
                ada(a)
            pe.wait_ge(s_x, 32)
            for k in range(KD):
                if k >= 2:
                    pe.wait_ge(s_h, k - 1)
                b = 4 + 2 * (k % 2)
                for t in range(TS):
                    T.transpose(PS[:, b, t * P:(t + 1) * P], x_nat[:, t, k * P:(k + 1) * P], ident)
                T.transpose(PS[:, b + 1, 0:P], x_nat[:, TS, k * P:(k + 1) * P], ident).then_inc(s_xt, 1)
            pe.wait_ge(s_hlo, KD)
            for w in range(5):
                pe.wait_ge(s_wlo, w + 1)
                wh, wl = w_slot(w_hi, w), w_slot(w_lo, w)
                for m in range(4):
                    i = 4 * w + m
                    if i >= 2:
                        acc_read(pe, i - 2)
                    for k in range(KD):
                        f, l = k == 0, k == KD - 1
                        a, b = wh[:, k, m * P:(m + 1) * P], wl[:, k, m * P:(m + 1) * P]
                        for h in range(2):
                            out = PS[:, 2 * (i % 2) + h, 0:HALF]
                            sl = slice(h * HALF, (h + 1) * HALF)
                            T.matmul(out, a, h_hi[:, k, sl], start=f, stop=False)
                            T.matmul(out, a, h_lo[:, k, sl], start=False, stop=False)
                        for h in range(2):
                            out = PS[:, 2 * (i % 2) + h, 0:HALF]
                            sl = slice(h * HALF, (h + 1) * HALF)
                            mm = T.matmul(out, b, h_hi[:, k, sl], start=False, stop=l)
                    mm.then_inc(s_acc, 1)
            pe.wait_ge(s_wlo, 6)
            wh, wl = w_slot(w_hi, 5), w_slot(w_lo, 5)
            for t in range(NT):
                acc_read(pe, 18 + t)
                for k in range(KD):
                    ts = slice(t * P, (t + 1) * P)
                    mm = three(PS[:, 2 * (t % 2), :], h_hi[:, k, ts], h_lo[:, k, ts], wh[:, k, :], wl[:, k, :], k == 0, k == KD - 1)
                mm.then_inc(s_acc, 1)
            for m in range(HP):
                mm = T.transpose(PS[:, 6, m * P:(m + 1) * P], kT[:, m, NS:TOK], ident)
            mm.then_inc(s_kp, 1)
            pe.wait_ge(s_ck, 32)
            for m in range(HP):
                for j in range(2):
                    mm = T.transpose(PS[:, 4 + m // 2, (2 * (m % 2) + j) * P:(2 * (m % 2) + j + 1) * P],
                                     ck_nat[:, j, m * P:(m + 1) * P], ident)
            mm.then_inc(s_ckt, 1)
            for a in range(4, NA):
                ada(a)
            pe.wait_ge(s_mod, 1)
            acc_read(pe, 24)
            T.transpose(PS[0:64, 0, 0:P], modc[:, 16:48, :].rearrange("p s j -> p (s j)"), ident).then_inc(s_mrow, 1)

            def scores(u):
                if u >= 2:
                    pe.wait_ge(s_p, u - 1)
                if u < UNITS:
                    h, n = u // NB, u % NB
                    g, r = h // 2, (h % 2) * DH
                    q = qT[r:r + DH, g, n * P:(n + 1) * P]
                    keys = kT[r:r + DH, g, 0:NS].rearrange("p (w c) -> p w c", c=GRID)[:, :, KEY0[n]:KEY0[n] + SPAN]
                    T.matmul(PS[:, u % 2, 0:LOC], q, keys, start=True, stop=True)
                    T.matmul(PS[:, u % 2, LOC:LOC + PAST], q, ck_T[r:r + DH, g, :], start=True, stop=True).then_inc(s_s, 1)
                else:
                    for j in range(4):
                        h = 2 * j + u - UNITS
                        g, r = h // 2, (h % 2) * DH
                        mm = T.matmul(PS[:, u % 2, j * P:(j + 1) * P], qT[r:r + DH, g, NS:TOK], kT[r:r + DH, g, NS:TOK],
                                      start=True, stop=True)
                    mm.then_inc(s_s, 1)

            def turn(u):
                pe.wait_ge(s_p, u + 1)
                if u >= 2:
                    pe.wait_ge(s_pts, u - 1)
                for j in range(4):
                    mm = T.transpose(PS[:, 2 + u % 2, j * P:(j + 1) * P], prob[:, u % 2, j * P:(j + 1) * P], ident)
                mm.then_inc(s_pt, 1)

            def values(u):
                pe.wait_ge(s_pts, u + 1)
                if u >= 2:
                    pe.wait_ge(s_os, u - 1)
                if u < UNITS:
                    h, n = u // NB, u % NB
                    for j in range(4):
                        v = vblk[:, 2 * n + j, h * DH:(h + 1) * DH] if j < 2 else ctx_v[:, j - 2, h * DH:(h + 1) * DH]
                        mm = T.matmul(PS[:, 4 + u % 2, 0:DH], prob_T[:, u % 2, j * P:(j + 1) * P], v, start=(j == 0), stop=(j == 3))
                    mm.then_inc(s_o, 1)
                else:
                    for j in range(4):
                        h = 2 * j + u - UNITS
                        mm = T.matmul(PS[:, 4 + u % 2, j * DH:(j + 1) * DH], prob_T[:, u % 2, j * P:(j + 1) * P],
                                      stage[:, 0, h * DH:(h + 1) * DH], start=True, stop=True)
                    mm.then_inc(s_o, 1)

            def turn_out(g):
                if g < HP:
                    pe.wait_ge(s_os, 8 * (g + 1))
                else:
                    pe.wait_ge(s_os, NU)
                if g >= 2:
                    pe.wait_ge(s_mlo, g - 1)
                for n in range(NB):
                    mm = T.transpose(PS[:, 6 + g % 2, n * P:(n + 1) * P], att_o[:, g % 2, n, :], back if g < HP else ident)
                mm.then_inc(s_ot, 1)

            pe.wait_ge(s_cks, 1)
            pe.wait_ge(s_kps, 1)
            pe.wait_ge(s_mrs, 1)
            pe.wait_ge(s_vb, 160)
            for u in range(NU + 3):
                if u < NU:
                    scores(u)
                if 2 <= u < NU + 2:
                    values(u - 2)
                if 1 <= u < NU + 1:
                    turn(u - 1)
                if u >= 3 and (u - 3) % 8 == 7 and u - 3 < UNITS:
                    turn_out((u - 3) // 8)
            turn_out(HP)

            def mix_out(n):
                t = T_ORDER[n]
                if n >= 2:
                    pe.wait_ge(s_mor, n - 1)
                ts = slice(t * P, (t + 1) * P)
                for c in range(2):
                    wh, wl = w_slot(w_hi, 6 + c), w_slot(w_lo, 6 + c)
                    for k in range(KD):
                        mm = three(PS[:, 2 * (n % 2) + c, :], h_hi[:, k, ts], h_lo[:, k, ts], wh[:, k, :], wl[:, k, :],
                                   k == 0, k == KD - 1)
                mm.then_inc(s_mo, 1)

            def router(n):
                t = T_ORDER[n]
                pe.wait_ge(s_h2, n + 1)
                if n >= 1:
                    pe.wait_ge(s_h2c, n)
                for k in range(KD):
                    mm = T.transpose(PS[:, 4 + k // 4, (k % 4) * P:(k % 4 + 1) * P], ln_t[:, n % 2, k * P:(k + 1) * P], ident)
                mm.then_inc(s_h2t, 1)
                pe.wait_ge(s_h2c, n + 1)
                for k in range(KD):
                    mm = T.matmul(PS[:, 6, t * (NG + NE):(t + 1) * (NG + NE)], h2_T[:, k, :], wr[:, k, :],
                                  start=(k == 0), stop=(k == KD - 1))
                mm.then_inc(s_lg, 1)

            pe.wait_ge(s_mlo, HP + 1)
            pe.wait_ge(s_clo, 1)
            pe.wait_ge(s_wlo, 8)
            pe.wait_ge(s_wrl, 32)
            for n in range(NT + 1):
                if n < NT:
                    mix_out(n)
                if n >= 1:
                    router(n - 1)

            oh = rt[:, 740:740 + NT * NE].rearrange("p (t e) -> p t e", t=NT)
            pe.wait_ge(s_one, 2)
            for t in range(NT + 1):
                for s in range(min(t, NT - 1) + 1):
                    whole = s < t
                    mm = T.matmul(PS[:, 7, t * NE:(t + 1) * NE], ones[:, :] if whole else tri, oh[:, s, :],
                                  start=(s == 0), stop=(s == min(t, NT - 1)))
            mm.then_inc(s_pos, 1)

            def turn_rows(c, b, over=False):
                if over:
                    pe.wait_ge(s_ovg, 16 * (c - NE) + 16)
                else:
                    pe.wait_ge(s_hg[b], 16 + 8 * (c - b))
                if not isinstance(c, int) or c >= 1:
                    pe.wait_ge(s_glo, c)
                for k in range(KD):
                    mm = T.transpose(PS[:, 2 + k // 4, (k % 4) * P:(k % 4 + 1) * P], hg[:, b, k * P:(k + 1) * P], ident)
                mm.then_inc(s_hgt, 1)

            def up(c, b):
                pe.wait_ge(s_wlo, c + E0 + 1)
                pe.wait_ge(s_glo, c + 1)
                if not isinstance(c, int) or c >= 2:
                    pe.wait_ge(s_sl, 4 * c - 4)
                wh, wl = w_slot(w_hi, b), w_slot(w_lo, b)
                for k in range(KD):
                    mm = three(PS[:, b, :], hgT_hi[:, b, k, :], hgT_lo[:, b, k, :], wh[:, k, :], wl[:, k, :], k == 0, k == KD - 1)
                mm.then_inc(s_hid, 1)

            def down(c, b):
                pe.wait_ge(s_alo, c + 1)
                pe.wait_ge(s_olo, c + 1)
                if not isinstance(c, int) or c >= 1:
                    pe.wait_ge(s_ya, c)
                    pe.wait_ge(s_yd, c)
                for h in range(2):
                    for k in range(2):
                        mm = three(PS[:, 6 + h, :], aT_hi[:, b, k, :], aT_lo[:, b, k, :], wo_hi[:, k, h * CH:(h + 1) * CH],
                                   wo_lo[:, k, h * CH:(h + 1) * CH], k == 0, k == 1)
                mm.then_inc(s_y, 1)

            def turn_act(c, b):
                pe.wait_ge(s_sl, 4 * c + 4)
                if not isinstance(c, int) or c >= 1:
                    pe.wait_ge(s_alo, c)
                for k in range(2):
                    mm = T.transpose(PS[:, 4, k * P:(k + 1) * P], sil[:, 2, k * P:(k + 1) * P], ident)
                mm.then_inc(s_at, 1)

            pe.wait_ge(s_ll, 16)
            T.transpose(PS[:, 5, 0:NE + MORE], list_r[0:NE + MORE, :], const[0:NE + MORE, C_ID:C_ID + NE + MORE]).then_inc(s_lt, 1)
            turn_rows(0, 0)

            def pe_pair(i, last=False):
                for b in range(2):
                    c = 2 * i + b
                    up(c, b)
                    if not (isinstance(c, int) and c == 0):
                        down(c - 1, 1 - b)
                    if not (last and b == 1):
                        turn_rows(c + 1, 1 - b)
                    turn_act(c, b)

            pe_pair(0)
            with pe.Fori(1, NE // 2 - 1) as i:
                pe_pair(i)
            pe_pair(NE // 2 - 1, True)
            down(NE - 1, 1)
            more = overflow_chunks(pe)
            with pe.If(more > 0):
                with pe.Fori(0, more) as i:
                    turn_rows(i + NE, 1, True)
                    up(i + NE, 1)
                    turn_act(i + NE, 1)
                    down(i + NE, 1)


def constants():
    import numpy as np
    P, NE, CAP, NT, MORE, SPAN, CB, NS = 128, 16, 128, 5, 10, 32, 16, 8
    ident = np.eye(P, dtype=np.float32)
    tri = np.triu(np.ones((P, P), np.float32), 1)
    k = np.arange(SPAN)[None, :]
    c = CB - 1 - (np.arange(P) % CB)[:, None]
    masks = []
    for kind in range(3):
        key = k + (32, 8, 0)[kind]
        q = c + (48, 16, 0)[kind]
        lo = np.clip(q - 8, 0, 48)
        masks.append(np.where((key >= lo) & (key < lo + 16), 0.0, -1e30).astype(np.float32))
    row = np.concatenate([
        np.arange(4, 0, -1), np.arange(NE) * CAP, NE * CAP - CAP - np.arange(NE) * CAP]).astype(np.float32)
    tok = np.arange(NT)[None, :] * P + np.arange(P)[:, None]
    iota = np.arange(MORE)
    return np.concatenate([ident, tri, *masks, np.tile(row, (P, 1)), tok.astype(np.float32),
                           np.tile(iota, (P, 1)).astype(np.float32), ident[::-1]], axis=1).astype(np.float32)


_INS = ["x_prompt", "x_sample", "cache_k", "cache_v", "c", "c_ctx", "w_ada", "b_ada", "w_in", "conv_w", "rpb", "w_out",
        "ln1_g", "ln1_b", "w_router_group", "b_router_group", "w_router_expert", "b_router_expert", "w_expert_in",
        "w_expert_out", "ln2_g", "ln2_b"]
_OUTS = [("y_prompt", (1, 128, 1024)), ("y_sample", (1, 512, 1024)), ("new_k", (1, 1, 8, 128, 64)),
         ("new_v", (1, 1, 8, 128, 64))]


def kernel(**inputs):
    import numpy as _np
    import concourse.bacc as _bacc
    from concourse import mybir as _mybir
    from concourse.bass_utils import run_bass_kernel_spmd as _run

    nc = _bacc.Bacc("TRN2", target_bir_lowering=False, num_devices=1)
    arrays, ins, outs = {}, {}, {}
    for name in _INS:
        arrays[f"in_{name}"] = _np.ascontiguousarray(inputs[name])
    arrays["in_const"] = constants()
    for name in _INS + ["const"]:
        a = arrays[f"in_{name}"]
        ins[name] = nc.dram_tensor(f"in_{name}", a.shape, _mybir.dt.from_np(a.dtype), kind="ExternalInput").ap()
    for name, shape in _OUTS:
        outs[name] = nc.dram_tensor(f"out_{name}", shape, _mybir.dt.float32, kind="ExternalOutput").ap()
    build(nc, ins, outs)
    r = _run(nc, [arrays], core_ids=[0])
    return tuple(r.results[0][f"out_{name}"] for name, _ in _OUTS)
```

```python
import concourse.bass as bass
from concourse import mybir
from contextlib import ExitStack


def build(nc, ins, outs):
    fp32 = mybir.dt.float32
    fp32r = mybir.dt.float32r
    i32 = mybir.dt.int32
    ALU = mybir.AluOpType
    ACT = mybir.ActivationFunctionType
    AX = mybir.AxisListType

    NS = ins["x_sample"].shape[1]
    NP = ins["x_prompt"].shape[1]
    D = ins["x_sample"].shape[2]
    TOK = NS + NP
    P = 128
    KD = D // P
    NT = TOK // P
    TS = NS // P
    HEADS, PAST, DH = ins["cache_k"].shape[2:]
    AW = HEADS * DH
    HP = HEADS // 2
    GRID = 64
    ROWS = NS // GRID
    NB, CB, SPAN = 4, 16, 32
    KEY0 = [0, 8, 24, 32]
    KIND = [2, 1, 1, 0]
    LOC = ROWS * SPAN
    NE = ins["w_expert_in"].shape[1]
    NG = 4
    EG = NE // NG
    DE = ins["w_expert_out"].shape[2]
    CH = 512
    HALF = TOK // 2
    ALPHA = 2.0 ** 0.25
    EPS = 1e-5
    CAP = P
    MORE = (2 * TOK) // CAP
    SLOTS = (NE + MORE) * CAP
    NA = 2 * 6
    RP0 = CB
    RPW = 64
    DR = 2 * ROWS - 1
    TW = DR * SPAN
    UNITS = 2 * HP * NB
    NU = UNITS + 2

    C_ID, C_TRI, C_MASK = 0, P, 2 * P
    C_RANK = C_MASK + 3 * SPAN
    C_E128 = C_RANK + NG
    C_OVER = C_E128 + NE
    C_TOK = C_OVER + NE
    C_IOTA = C_TOK + NT
    C_BACK = C_IOTA + MORE
    C_END = C_BACK + P

    ctx = ExitStack()
    with ctx:
        def sb(name, shape, dt=fp32):
            return ctx.enter_context(nc.sbuf_tensor(name, shape, dt))

        def sem(name):
            return ctx.enter_context(nc.semaphore(name))

        act_hi = sb("act_hi", [P, KD * TOK], fp32r)
        act_lo = sb("act_lo", [P, KD * TOK], fp32r)
        w_hi = sb("w_hi", [P, 2, KD * CH], fp32r)
        w_lo = sb("w_lo", [P, 2, KD * CH], fp32r)
        raw = sb("raw", [P, 2, KD * CH])
        g1 = sb("g1", [P, NT * D])
        uni = sb("uni", [P, 11264])
        cond_r = sb("cond_r", [P, KD, 4], fp32r)
        const = sb("const", [P, C_END])
        rows = sb("rows", [P, P])
        cols = sb("cols", [P, P])
        modc = sb("modc", [P, 6 * KD, 2])
        wr = sb("wr", [P, KD, NG + NE])
        logits = sb("logits", [P, NT, NG + NE])
        small = sb("small", [P, 96])
        gates = sb("gates", [P, 2, NT])
        rb = sb("rb", [P, NG + NE])
        over_i = sb("over_i", [P, 1 + MORE], i32)
        over_col = sb("over_col", [P, 1], i32)
        slot_i = sb("slot_i", [P, 2, NT], i32)
        PS = ctx.enter_context(nc.psum_tensor("PS", [P, 8, 512], fp32))

        ones = rows
        ident = const[:, C_ID:C_ID + P]
        back = const[:, C_BACK:C_BACK + P]
        tri = const[:, C_TRI:C_TRI + P]
        mask3 = const[:, C_MASK:C_MASK + 3 * SPAN].rearrange("p (a k) -> p a k", a=3)

        def dram(name, shape, dt=fp32):
            return nc.dram_tensor(name, shape, dt, kind="Internal").ap()

        def dap(t, offset, pattern):
            return bass.AP(tensor=t.tensor, offset=offset, ap=pattern)

        v_dram = dram("v_scratch", (NS, AW))
        rp_dram = dram("rpb_padded", (HEADS * DR, RPW))
        bias_dram = dram("bias_windows", (HEADS * CB, 3 * TW))
        mod_dram = dram("mod_rows", (4 * KD * 2, P))
        h2_dram = dram("h2_rows", (TOK, D))
        list_dram = dram("slot_tokens", (SLOTS, 1))
        y_dram = dram("expert_rows", (SLOTS, D))

        x_nat = g1[:, :].rearrange("p (t d) -> p t d", t=NT)
        qT = g1[:, 0:HP * TOK].rearrange("p (m t) -> p m t", m=HP)
        kT = g1[:, HP * TOK:2 * HP * TOK].rearrange("p (m t) -> p m t", m=HP)
        x1 = x_nat
        h_hi = act_hi[:, :].rearrange("p (k t) -> p k t", k=KD)
        h_lo = act_lo[:, :].rearrange("p (k t) -> p k t", k=KD)
        PADW = TOK + 8
        conv_y = uni[:, 0:4 * PADW].rearrange("p (m t) -> p m t", m=4)
        conv_o = uni[:, 4 * PADW:8 * PADW].rearrange("p (m t) -> p m t", m=4)
        o = 8 * PADW
        bias_t = uni[:, o:o + 3 * TW].rearrange("p (a r k) -> p a r k", a=3, r=DR)
        h_tmp = uni[:, 6700:6700 + 2 * TOK].rearrange("p (b t) -> p b t", b=2)
        rp_pad = uni[:, 8000:8000 + RPW]
        ck_nat = uni[:, 8064:8064 + 2 * AW].rearrange("p (a n) -> p a n", a=2)
        silu_t = uni[:, 9100:9100 + P]
        mod_row = uni[0:4, 9300:9300 + 2 * CH].rearrange("p (b n) -> p b n", b=2)
        stage = uni[:, 5200:5200 + 2 * AW].rearrange("p (b n) -> p b n", b=2)
        vblk = raw[:, 0, :].rearrange("p (j n) -> p j n", j=8)
        ctx_v = uni[:, 0:2 * AW].rearrange("p (j n) -> p j n", j=2)
        ck_T = uni[:, 2 * AW:2 * AW + HP * PAST].rearrange("p (m t) -> p m t", m=HP)
        bias_s = uni[:, 6224:6224 + 2 * 3 * LOC].rearrange("p (b a n) -> p b a n", b=2, a=3)
        prob = uni[:, 7760:7760 + 1024].rearrange("p (b n) -> p b n", b=2)
        prob_T = uni[:, 8784:8784 + 1024].rearrange("p (b n) -> p b n", b=2)
        att_o = uni[:, 9808:9808 + 1024].rearrange("p (b n c) -> p b n c", b=2, n=NB)
        gate_a = uni[:, 0:2 * D].rearrange("p (j d) -> p j d", j=2)
        lin_a = uni[:, 2 * D:4 * D].rearrange("p (j d) -> p j d", j=2)
        lin_b = uni[:, 4 * D:6 * D].rearrange("p (j d) -> p j d", j=2)
        ln1_g = uni[:, 6 * D:7 * D]
        ln1_b = uni[:, 7 * D:8 * D]
        ln_t = uni[:, 8 * D:10 * D].rearrange("p (b d) -> p b d", b=2)
        h2_T = uni[:, 10 * D:11 * D].rearrange("p (k t) -> p k t", k=KD)
        rt = uni[:, 0:4096]
        raw_o = uni[:, 0:2 * 2 * D].rearrange("p (b n) -> p b n", b=2)
        hg = uni[:, 4096:4096 + 2 * D].rearrange("p (b n) -> p b n", b=2)
        y_sb = uni[:, 6144:6144 + 2 * D].rearrange("p (b n) -> p b n", b=2)
        sil = uni[:, 8192:8192 + 3 * DE].rearrange("p (b n) -> p b n", b=3)
        list_s = uni[:, 9120:9120 + NE + MORE].bitcast(i32)
        list_r = uni[:, 9400:9400 + CAP]
        slot_f = uni[:, 9200:9200 + 2 * NT].rearrange("p (c t) -> p c t", c=2)
        hgT_hi = act_hi[:, 0:2 * D].rearrange("p (b k t) -> p b k t", b=2, k=KD)
        hgT_lo = act_lo[:, 0:2 * D].rearrange("p (b k t) -> p b k t", b=2, k=KD)
        aT_hi = act_hi[:, 2 * D:2 * D + 4 * P].rearrange("p (b k t) -> p b k t", b=2, k=2)
        aT_lo = act_lo[:, 2 * D:2 * D + 4 * P].rearrange("p (b k t) -> p b k t", b=2, k=2)
        wo_hi = act_hi[:, 2560:2560 + 2 * D].rearrange("p (k n) -> p k n", k=2)
        wo_lo = act_lo[:, 2560:2560 + 2 * D].rearrange("p (k n) -> p k n", k=2)
        fin_v = raw[:, 0, :].rearrange("p (a d) -> p a d", a=4)
        fin_y = raw[:, 1, :].rearrange("p (b a d) -> p b a d", b=2, a=2)
        nmax = small[:, 0:8].rearrange("p (b n) -> p b n", b=2)
        rsum = small[:, 8:24].rearrange("p (b n) -> p b n", b=4)
        rinv = small[:, 24:32].rearrange("p (b n) -> p b n", b=2)
        stat = small[:, 32:44]
        mv = small[:, 44:46]
        rstd = small[:, 46:47]
        std = small[:, 47:48]
        eps = small[:, 48:49]

        w_ada, w_in, w_out = ins["w_ada"][0], ins["w_in"][0], ins["w_out"][0]
        we_in, we_out = ins["w_expert_in"][0], ins["w_expert_out"][0]
        IN_ORDER = [4, 5, 3, 2, 0, 1]
        IN_N = [4, 7, 10, 13, 16, 17]
        ADA_N = [0, 1, 2, 3, 5, 6, 8, 9, 11, 12, 14, 15]
        OUT_N = [18, 19]
        NCH = NA + len(IN_N) + len(OUT_N)
        stream = [None] * NCH
        for i, n in enumerate(ADA_N):
            stream[n] = (w_ada, i)
        for i, n in enumerate(IN_N):
            stream[n] = (w_in, IN_ORDER[i])
        for i, n in enumerate(OUT_N):
            stream[n] = (w_out, i)
        SUM0 = [0, 4, 8, 12, 12 + NT, 16 + NT, 20 + NT]
        E0 = 2 * NCH

        s_const = sem("const_loaded")
        s_small = sem("small_rows_loaded")
        s_silu = sem("silu_steps")
        s_rows = sem("rows_transposed")
        s_cols = sem("cols_ready")
        s_raw = [sem("raw_loaded_0"), sem("raw_loaded_1")]
        s_ada = sem("ada_chunks_multiplied")
        s_ch = sem("condition_hi_ready")
        s_cl = sem("condition_lo_ready")
        s_ar = sem("mod_sums_copied")
        s_at0 = sem("mod_sums_transposed")
        s_mod = sem("modulation_steps")
        s_x = sem("x_loaded")
        s_xt = sem("x_transposed")
        s_h = sem("h_modulated")
        s_hhi = sem("h_hi_ready")
        s_hlo = sem("h_lo_ready")
        s_whi = sem("w_hi_ready")
        s_wlo = sem("w_lo_ready")
        s_acc = sem("proj_sums_ready")
        s_acc_a = sem("proj_sums_read_by_scalar")
        s_acc_d = sem("proj_sums_read_by_vector")
        s_vout = [sem("v_tile_stored_0"), sem("v_tile_stored_1")]
        s_cache = sem("cache_stored")
        s_kp = sem("k_prompt_transposed")
        s_kps = sem("k_prompt_staged")
        s_ck = sem("ctx_k_loaded")
        s_ckt = sem("ctx_k_transposed")
        s_cks = sem("ctx_k_ready")
        s_rpz = sem("rpb_pad_zeroed")
        s_rp = sem("rpb_steps")
        s_bt = sem("bias_window_loaded")
        s_bm = sem("bias_masked")
        s_bd = sem("bias_stored")
        s_bias = [sem("bias_head_loaded_0"), sem("bias_head_loaded_1")]
        s_mrow = sem("mod_rows_transposed")
        s_mrs = sem("mod_rows_staged")
        s_mrd = sem("mod_rows_stored")
        s_chi = sem("conv_hi_ready")
        s_clo = sem("conv_lo_ready")
        s_vb = sem("v_blocks_loaded")
        s_cv = sem("ctx_v_loaded")
        s_s = sem("scores_ready")
        s_nm = sem("row_max_ready")
        s_dv = sem("vector_chain")
        s_p = sem("probs_ready")
        s_pt = sem("probs_transposed")
        s_pts = sem("probs_T_ready")
        s_o = sem("att_out_ready")
        s_os = sem("att_out_scaled")
        s_ot = sem("att_out_transposed")
        s_mhi = sem("mix_hi_ready")
        s_mlo = sem("mix_lo_ready")
        s_vec = [sem("ln1_vectors_loaded_sample"), sem("ln1_vectors_loaded_prompt")]
        s_xr = [sem("x_reloaded_sample"), sem("x_reloaded_prompt")]
        s_wrl = sem("router_weights_loaded")
        s_mo = sem("mix_out_ready")
        s_mor = sem("mix_out_read")
        s_var = sem("variance_ready")
        s_std = sem("std_ready")
        s_xn = sem("normed_ready")
        s_h2 = sem("h2_ready")
        s_h2s = [sem("h2_stored_0"), sem("h2_stored_1")]
        s_x1 = sem("x1_ready")
        s_plc = sem("pool_chain")
        s_h2t = sem("h2_transposed")
        s_h2c = sem("h2_T_ready")
        s_rb = sem("router_biases_loaded")
        s_sl = sem("expert_silu_steps")
        s_lg = sem("logits_sum_ready")
        s_one = sem("choices_ready")
        s_pos = sem("positions_ready")
        s_slot = sem("slots_ready")
        s_gexp = sem("group_exp_ready")
        s_lz = sem("list_zeroed")
        s_lst = sem("list_scattered")
        s_ll = sem("list_loaded")
        s_lt = sem("list_transposed")
        s_lc = sem("list_ready")
        s_rawo = [sem("raw_out_loaded_0"), sem("raw_out_loaded_1")]
        s_hg = [sem("rows_gathered_0"), sem("rows_gathered_1")]
        s_hgt = sem("rows_transposed_for_expert")
        s_ghi = sem("gathered_hi_ready")
        s_glo = sem("gathered_lo_ready")
        s_ohi = sem("expert_out_w_hi_ready")
        s_olo = sem("expert_out_w_lo_ready")
        s_hid = sem("hidden_ready")
        s_ex = sem("silu_exp_ready")
        s_act = sem("expert_act_ready")
        s_at = sem("expert_act_transposed")
        s_ahi = sem("expert_act_hi_ready")
        s_alo = sem("expert_act_lo_ready")
        s_y = sem("expert_rows_ready")
        s_ya = sem("expert_rows_half_0_copied")
        s_yd = sem("expert_rows_half_1_copied")
        s_yst = [sem("expert_rows_stored_0"), sem("expert_rows_stored_1")]
        s_yz = sem("overflow_slots_filled")
        s_over = sem("overflow_table_ready")
        s_ovw = sem("overflow_weights_loaded")
        s_ovc = sem("overflow_column_ready")
        s_ovg = sem("overflow_rows_gathered")
        s_ovs = sem("overflow_rows_stored")
        s_fv = sem("final_vectors_loaded")
        s_fy = [sem("final_rows_gathered_0"), sem("final_rows_gathered_1")]
        s_fin = sem("final_tile_ready")
        s_done = sem("outputs_stored")

        block = ctx.enter_context(nc.Block())

        def raw_full(eng, n):
            eng.wait_ge(s_raw[n % 2], 16 * (n // 2 + 1))

        def chunk_src(w, c):
            return w[:, c * CH:(c + 1) * CH].rearrange("(k p) n -> p k n", p=P)

        def raw_slot(n):
            return raw[:, n % 2, :].rearrange("p (k n) -> p k n", k=KD)

        def w_slot(t, n):
            return t[:, n % 2, :].rearrange("p (k n) -> p k n", k=KD)

        def acc_read(eng, i):
            if i < 4:
                eng.wait_ge(s_acc_a, i + 1)
            elif i < 12:
                eng.wait_ge(s_acc_d, i - 3)
            else:
                eng.wait_ge(s_acc_a, i - 7)

        def w_used(eng, n):
            if n in ADA_N:
                eng.wait_ge(s_ada, ADA_N.index(n) + 1)
            elif n in IN_N:
                eng.wait_ge(s_acc, SUM0[IN_N.index(n) + 1])

        def overflow_chunks(eng):
            eng.wait_ge(s_over, 1)
            return eng.value_load(over_i[0:1, 0:1], min_val=0, max_val=MORE)

        T_ORDER = [NT - 1] + list(range(NT - 1))

        def cond_of(t):
            return 1 if t == NT - 1 else 0

        @block.sync
        def _(sp):
            sp.dma_start(const[:, :], ins["const"]).then_inc(s_const, 16)

            def load_chunk(n):
                if n >= 2:
                    sp.wait_ge(s_wlo, 2 * (n - 1))
                sp.dma_start(raw_slot(n), chunk_src(*stream[n])).then_inc(s_raw[n % 2], 16)

            for n in range(4):
                load_chunk(n)
            sp.dma_start(x_nat[:, 0:TS, :], ins["x_sample"][0].rearrange("(t p) d -> p t d", p=P)).then_inc(s_x, 16)
            sp.dma_start(x_nat[:, TS, :], ins["x_prompt"][0]).then_inc(s_x, 16)
            for n in range(4, NCH):
                load_chunk(n)
            sp.wait_ge(s_wlo, 2 * (OUT_N[0] + 1))
            for b in range(2):
                sp.wait_ge(s_vout[b], 16 * (TS // 2))
            for n in range(NB):
                for j in range(2):
                    src = dap(v_dram, (j * 4 * GRID + KEY0[n]) * AW, [[GRID * AW, 4], [AW, SPAN], [1, AW]])
                    sp.dma_start(vblk[:, 2 * n + j, :], src).then_inc(s_vb, 16)
            sp.wait_ge(s_o, NU)
            def expert_in(e, slot):
                sp.wait_ge(s_wlo, e + E0 - 1)
                sp.dma_start(raw_slot(slot), we_in[e].rearrange("(k p) n -> p k n", p=P)).then_inc(s_raw[slot], 16)

            def expert_out(e, slot, first):
                if first:
                    sp.wait_ge(s_slot, 1)
                else:
                    sp.wait_ge(s_olo, e - 1)
                sp.dma_start(raw_o[:, slot, :].rearrange("p (k n) -> p k n", k=2),
                             we_out[e].rearrange("(k p) n -> p k n", p=P)).then_inc(s_rawo[slot], 16)

            for b in range(2):
                expert_in(b, b)
            for b in range(2):
                expert_out(b, b, True)
            with sp.Fori(1, NE // 2) as i:
                for b in range(2):
                    expert_in(2 * i + b, b)
                    expert_out(2 * i + b, b, False)
            sp.wait_ge(s_wlo, E0 + NE - 1)
            for j in range(2):
                sp.dma_start(fin_v[:, j, :].rearrange("p (s c) -> p s c", s=KD),
                             dap(mod_dram, (3 * KD * 2 + j) * P, [[0, P], [2 * P, KD], [1, P]])).then_inc(s_fv, 16)
            sp.dma_start(fin_v[:, 2, :], dap(ins["ln2_g"], 0, [[0, P], [1, D]])).then_inc(s_fv, 16)
            sp.dma_start(fin_v[:, 3, :], dap(ins["ln2_b"], 0, [[0, P], [1, D]])).then_inc(s_fv, 16)
            for n, t in enumerate(T_ORDER):
                sp.wait_ge(s_fin, n + 1)
                dst = outs["y_prompt"][0] if t == NT - 1 else outs["y_sample"][0][t * P:(t + 1) * P, :]
                sp.dma_start(dst, x1[:, t, :]).then_inc(s_done, 16)
            sp.wait_ge(s_done, 16 * NT)
            sp.wait_ge(s_cache, 32)

        @block.gpsimd
        def _(pool):
            nc.gpsimd.memset(rows[:, :], 0.0).then_inc(s_rpz, 1)
            nc.gpsimd.memset(rp_pad, 0.0).then_inc(s_rpz, 1)
            nc.gpsimd.memset(eps, EPS).then_inc(s_rpz, 1)
            pool.wait_ge(s_rpz, 3)
            pool.dma_start(rp_pad[0:HEADS * DR, RP0:RP0 + 2 * CB - 1],
                           ins["rpb"][0].rearrange("h r c -> (h r) c")).then_inc(s_rp, 16)
            pool.dma_start(ck_nat.rearrange("p a (h d) -> p a h d", h=HEADS)[:, 0],
                           ins["cache_k"][0, 0][:, 0:P, :].rearrange("h t d -> t h d")).then_inc(s_ck, 16)
            pool.dma_start(ck_nat.rearrange("p a (h d) -> p a h d", h=HEADS)[:, 1],
                           ins["cache_k"][0, 0][:, P:2 * P, :].rearrange("h t d -> t h d")).then_inc(s_ck, 16)
            pool.dma_start(wr[:, :, 0:NG], ins["w_router_group"][0].rearrange("(k p) n -> p k n", p=P)).then_inc(s_wrl, 16)
            pool.dma_start(wr[:, :, NG:NG + NE], ins["w_router_expert"][0].rearrange("(k p) n -> p k n", p=P)).then_inc(s_wrl, 16)
            pool.dma_start(rb[:, 0:NG], dap(ins["b_router_group"], 0, [[0, P], [1, NG]])).then_inc(s_rb, 16)
            pool.dma_start(rb[:, NG:NG + NE], dap(ins["b_router_expert"], 0, [[0, P], [1, NE]])).then_inc(s_rb, 16)
            pool.wait_ge(s_rp, 16)
            pool.dma_start(rp_dram, rp_pad[0:HEADS * DR, :]).then_inc(s_rp, 16)
            pool.wait_ge(s_rp, 32)
            for h in range(HEADS):
                for a in range(3):
                    src = dap(rp_dram, h * DR * RPW + RP0 - CB + 8 * a, [[1, CB], [RPW, DR], [1, SPAN]])
                    pool.dma_start(bias_t[CB * h:CB * h + CB, a, :, :], src).then_inc(s_bt, 16)
            pool.wait_ge(s_silu, 2)
            nc.gpsimd.memset(silu_t, 0.0).then_inc(s_rpz, 1)
            pool.wait_ge(s_rows, 1)
            nc.gpsimd.memset(ones[:, :], 1.0).then_inc(s_rpz, 1)
            pool.wait_ge(s_rpz, 5)
            pool.dma_start(list_dram.rearrange("(p n) a -> p (n a)", p=P), silu_t[:, 0:SLOTS // P]).then_inc(s_lz, 16)
            pool.wait_ge(s_bm, 1)
            pool.dma_start(bias_dram, bias_t.rearrange("p a r k -> p (a r k)")).then_inc(s_bd, 16)
            pool.wait_ge(s_bd, 16)

            def load_bias(h):
                if h >= 2:
                    pool.wait_ge(s_nm, NB * (h - 1))
                for a in range(3):
                    src = dap(bias_dram, h * CB * 3 * TW + a * TW,
                              [[SPAN, ROWS], [3 * TW, CB], [1, LOC]])
                    pool.dma_start(bias_s[:, h % 2, a, :], src).then_inc(s_bias[h % 2], 16)

            pool.wait_ge(s_acc_d, 8)
            pool.wait_ge(s_lz, 16)
            for j in range(2):
                pool.dma_start(ctx_v[:, j, :].rearrange("p (h d) -> p h d", h=HEADS),
                               ins["cache_v"][0, 0][:, j * P:(j + 1) * P, :].rearrange("h t d -> t h d")).then_inc(s_cv, 16)
            for h in range(HEADS):
                load_bias(h)
                if h == 2:
                    for j in range(2):
                        r0 = (NE + j * MORE // 2) * CAP
                        pool.dma_start(y_dram[r0:r0 + MORE // 2 * CAP, :].rearrange("(p a) d -> p (a d)", p=P),
                                       g1[:, :]).then_inc(s_yz, 16)
            pool.wait_ge(s_mrd, 16)
            pool.wait_ge(s_yz, 32)
            pool.wait_ge(s_clo, 1)
            pool.wait_ge(s_cache, 32)
            pool.wait_ge(s_mlo, HP + 1)
            pool.dma_start(x1[:, NT - 1, :], ins["x_prompt"][0]).then_inc(s_xr[1], 16)
            for j in (1, 0):
                for v, dst in ((0, gate_a), (2, lin_a), (1, lin_b)):
                    pool.dma_start(dst[:, j, :].rearrange("p (s c) -> p s c", s=KD),
                                   dap(mod_dram, (v * KD * 2 + j) * P, [[0, P], [2 * P, KD], [1, P]])).then_inc(s_vec[j], 16)
                if j == 1:
                    pool.dma_start(ln1_g, dap(ins["ln1_g"], 0, [[0, P], [1, D]])).then_inc(s_vec[j], 16)
                    pool.dma_start(ln1_b, dap(ins["ln1_b"], 0, [[0, P], [1, D]])).then_inc(s_vec[j], 16)
            pool.dma_start(x1[:, 0:TS, :], ins["x_sample"][0].rearrange("(t p) d -> p t d", p=P)).then_inc(s_xr[0], 16)
            for n, t in enumerate(T_ORDER):
                pool.wait_ge(s_xn, n + 1)
                nc.gpsimd.tensor_tensor(x1[:, t, :], ln_t[:, n % 2, :], ln1_g, ALU.mult).then_inc(s_plc, 1)
                pool.wait_ge(s_plc, n + 1)
                nc.gpsimd.tensor_tensor(x1[:, t, :], x1[:, t, :], ln1_b, ALU.add).then_inc(s_x1, 1)
                pool.wait_ge(s_h2, n + 1)
                pool.dma_start(h2_dram[t * P:(t + 1) * P, :], ln_t[:, n % 2, :]).then_inc(s_h2s[n % 2], 16)
            pool.wait_ge(s_slot, 1)
            for c in range(2):
                for t in range(NT):
                    pool.indirect_dma_start(list_dram, bass.IndirectOffsetOnAxis(ap=slot_i[:, c, t:t + 1], axis=0),
                                            const[:, C_TOK + t:C_TOK + t + 1], None).then_inc(s_lst, 16)
            pool.wait_ge(s_lst, 16 * 2 * NT)
            pool.dma_start(list_r[0:NE + MORE, :], list_dram.rearrange("(e p) a -> e (p a)", p=CAP)).then_inc(s_ll, 16)
            pool.wait_ge(s_lc, 1)
            for b in range(2):
                pool.wait_ge(s_h2s[b], 16 * (NT // 2 + 1 - b))

            def gather(c, b, col):
                pool.indirect_dma_start(hg[:, b, :], None, h2_dram,
                                        bass.IndirectOffsetOnAxis(ap=col, axis=0)).then_inc(s_hg[b], 16)

            def store_rows(c):
                pool.wait_ge(s_ya, c + 1)
                pool.wait_ge(s_yd, c + 1)
                pool.dma_start(y_dram[c * CAP:(c + 1) * CAP, :], y_sb[:, c % 2, :]).then_inc(s_yst[c % 2], 16)

            for c in range(NE):
                if c >= 2:
                    pool.wait_ge(s_hgt, c - 1)
                gather(c, c % 2, list_s[:, c:c + 1])
                if c >= 3:
                    store_rows(c - 3)
            for c in range(NE - 3, NE):
                store_rows(c)
            more = overflow_chunks(pool)
            with pool.If(more > 0):
                with pool.Fori(0, more) as i:
                    pool.wait_ge(s_hgt, i + NE)
                    nc.gpsimd.tensor_copy(over_col[:, :], list_s[:, bass.ds(i + NE, 1)]).then_inc(s_ovc, 1)
                    with pool.If(more > 0):
                        pool.wait_ge(s_ovc, i + 1)
                    pool.indirect_dma_start(hg[:, 1, :], None, h2_dram,
                                            bass.IndirectOffsetOnAxis(ap=over_col[:, 0:1], axis=0)).then_inc(s_ovg, 16)
                    pool.wait_ge(s_ya, i + (NE + 1))
                    pool.wait_ge(s_yd, i + (NE + 1))
                    pool.dma_start(y_dram[bass.ds((i + NE) * CAP, CAP), :], y_sb[:, 1, :]).then_inc(s_ovs, 16)
                    pool.wait_ge(s_ovs, 16 * i + 16)
            for b in range(2):
                pool.wait_ge(s_yst[b], 16 * (NE // 2))
            pool.wait_ge(s_wlo, E0 + NE)
            def token_rows(n):
                t = T_ORDER[n]
                if n >= 2:
                    pool.wait_ge(s_fin, n - 1)
                for c in range(2):
                    pool.indirect_dma_start(fin_y[:, n % 2, c, :], None, y_dram,
                                            bass.IndirectOffsetOnAxis(ap=slot_i[:, c, t:t + 1], axis=0)).then_inc(s_fy[n % 2], 16)

            token_rows(0)
            token_rows(1)
            for n in range(2, NT):
                token_rows(n)

        @block.scalar
        def _(act):
            act.wait_ge(s_rpz, 1)
            act.dma_start(rows[96:104, :], ins["c"][0].rearrange("(k c) -> k c", c=P)).then_inc(s_small, 16)
            act.dma_start(rows[104:112, :], ins["c_ctx"].rearrange("(k c) -> k c", c=P)).then_inc(s_small, 16)
            act.dma_start(rows[0:48, :], ins["b_ada"][0].rearrange("(s c) -> s c", c=P)).then_inc(s_small, 16)
            act.dma_start(rows[64:76, :], ins["conv_w"][0].rearrange("k (m c) -> (k m) c", c=P)).then_inc(s_small, 16)
            act.wait_ge(s_small, 64)
            nc.scalar.activation(silu_t[96:112, :], rows[96:112, :], ACT.Exp, scale=-1.0).then_inc(s_silu, 1)
            act.wait_ge(s_cols, 1)
            nc.scalar.activation(cond_r[:, :, 0:2], cols[:, 96:96 + 2 * KD].rearrange("p (j k) -> p k j", j=2),
                                 ACT.Copy).then_inc(s_ch, 1)

            def split_hi(n):
                raw_full(act, n)
                if n >= 2:
                    w_used(act, n - 2)
                for h in range(2):
                    half = slice(h * 4 * CH, (h + 1) * 4 * CH)
                    nc.scalar.activation(w_hi[:, n % 2, half], raw[:, n % 2, half], ACT.Copy).then_inc(s_whi, 1)

            def mod_copy(a):
                act.wait_ge(s_ada, a + 1)
                if a >= 2:
                    act.wait_ge(s_at0, a - 1)
                nc.scalar.activation(mod_row[:, a % 2, :], PS[0:4, (2 if a < 4 else 4) + a % 2, :], ACT.Copy).then_inc(s_ar, 1)

            split_hi(0)
            split_hi(1)
            mod_copy(0)
            split_hi(2)
            mod_copy(1)
            split_hi(3)
            mod_copy(2)
            mod_copy(3)
            split_hi(4)
            for k in range(KD):
                act.wait_ge(s_h, k + 1)
                nc.scalar.activation(h_hi[:, k, :], h_tmp[:, k % 2, :], ACT.Copy).then_inc(s_hhi, 1)
            split_hi(5)

            def q_back(m, r0, r1):
                return bass.AP(tensor=g1, offset=m * TOK + P - 1 - CB * r0,
                               ap=[[NT * D, P], [-CB, r1 - r0], [P, NB], [-1, CB]])

            def evac(i):
                act.wait_ge(s_acc, i + 1)
                w = max(j for j in range(6) if SUM0[j] <= i)
                m = i - SUM0[w]
                b = 2 * (i % 2)
                if w == 0:
                    nc.scalar.activation(conv_y[:, m, 1:1 + HALF], PS[:, b, 0:HALF], ACT.Copy)
                    nc.scalar.activation(conv_y[:, m, 1 + HALF:1 + NS], PS[:, b + 1, 0:NS - HALF], ACT.Copy)
                    nc.scalar.activation(conv_y[:, m, 2 + NS:2 + TOK], PS[:, b + 1, NS - HALF:HALF], ACT.Copy).then_inc(s_acc_a, 1)
                elif w == 4:
                    r0 = HALF // GRID
                    nc.scalar.activation(q_back(m, 0, r0), PS[:, b, 0:HALF].rearrange("p (r n c) -> p r n c", n=NB, c=CB),
                                         ACT.Copy, scale=DH ** -0.5)
                    nc.scalar.activation(q_back(m, r0, ROWS), PS[:, b + 1, 0:NS - HALF].rearrange("p (r n c) -> p r n c", n=NB, c=CB),
                                         ACT.Copy, scale=DH ** -0.5)
                    nc.scalar.activation(qT[:, m, NS:TOK], PS[:, b + 1, NS - HALF:HALF], ACT.Copy,
                                         scale=DH ** -0.5).then_inc(s_acc_a, 1)
                elif w == 5:
                    nc.scalar.activation(kT[:, m, 0:HALF], PS[:, b, 0:HALF], ACT.Copy)
                    nc.scalar.activation(kT[:, m, HALF:TOK], PS[:, b + 1, 0:HALF], ACT.Copy).then_inc(s_acc_a, 1)
                else:
                    t = m
                    if t >= 2:
                        act.wait_ge(s_vout[t % 2], 16 * (t // 2))
                    else:
                        act.wait_ge(s_bd, 16)
                    nc.scalar.activation(stage[:, t % 2, :], PS[:, b, :], ACT.Copy).then_inc(s_acc_a, 1)
                    act.wait_ge(s_acc_a, i - 7)
                    if t < TS:
                        act.dma_start(v_dram[t * P:(t + 1) * P, :], stage[:, t % 2, :]).then_inc(s_vout[t % 2], 16)
                    else:
                        act.dma_start(outs["new_v"][0, 0].rearrange("h s d -> s h d"),
                                      stage[:, t % 2, :].rearrange("p (h d) -> p h d", h=HEADS)).then_inc(s_cache, 16)

            for w in range(6):
                n = IN_N[w]
                first, end = SUM0[w], SUM0[w + 1]
                scalar_reads = w not in (1, 2)
                if scalar_reads:
                    for i in range(first, end - 1):
                        evac(i)
                split_hi(n + 2)
                if scalar_reads:
                    evac(end - 1)
                if w < 4:
                    for a in range(4 + 2 * w, 6 + 2 * w):
                        mod_copy(a)
                        split_hi(ADA_N[a] + 2)
                elif w == 4:
                    act.wait_ge(s_mrow, 1)
                    nc.scalar.activation(cols[0:64, :], PS[0:64, 7, 0:P], ACT.Copy).then_inc(s_mrs, 1)
                    act.wait_ge(s_mrs, 1)
                    act.dma_start(mod_dram, cols[0:64, :]).then_inc(s_mrd, 16)
            act.wait_ge(s_kp, 1)
            act.wait_ge(s_vout[1], 32)
            nc.scalar.activation(stage[:, 1, :], PS[:, 6, :], ACT.Copy).then_inc(s_kps, 1)
            act.wait_ge(s_kps, 1)
            act.dma_start(outs["new_k"][0, 0].rearrange("h s d -> s h d"),
                          stage[:, 1, :].rearrange("p (h d) -> p h d", h=HEADS)).then_inc(s_cache, 16)
            act.wait_ge(s_acc_d, 8)
            act.wait_ge(s_acc, SUM0[6])
            nc.scalar.activation(h_hi[:, 4:8, 0:NS], conv_o[:, :, 1:1 + NS], ACT.Copy)
            nc.scalar.activation(h_hi[:, 4:8, NS:TOK], conv_o[:, :, 2 + NS:2 + TOK], ACT.Copy).then_inc(s_chi, 1)

            def exps(u):
                act.wait_ge(s_nm, u + 1)
                if u >= 2:
                    act.wait_ge(s_pt, u - 1)
                if u < UNITS:
                    nc.scalar.activation(prob[:, u % 2, :], PS[:, u % 2, :], ACT.Exp, bias=nmax[:, u % 2, 0:1],
                                         accum_out=rsum[:, u % 4, 0:1]).then_inc(s_p, 1)
                else:
                    for j in range(4):
                        a = nc.scalar.activation(prob[:, u % 2, j * P:(j + 1) * P], PS[:, u % 2, j * P:(j + 1) * P], ACT.Exp,
                                                 bias=nmax[:, u % 2, j:j + 1], accum_out=rsum[:, u % 4, j:j + 1])
                    a.then_inc(s_p, 1)

            def copy_pt(u):
                act.wait_ge(s_pt, u + 1)
                if u >= 2:
                    act.wait_ge(s_o, u - 1)
                nc.scalar.activation(prob_T[:, u % 2, :], PS[:, 2 + u % 2, :], ACT.Copy).then_inc(s_pts, 1)

            def mix_hi(g):
                act.wait_ge(s_ot, g + 1)
                src = PS[:, 6 + g % 2, :]
                if g < HP:
                    s4 = src.rearrange("p (n r c) -> p n r c", n=NB, r=ROWS)
                    d4 = h_hi[:, g, 0:NS].rearrange("p (r n c) -> p n r c", n=NB, r=ROWS)
                    for n in range(NB):
                        a = nc.scalar.activation(d4[:, n], s4[:, n], ACT.Copy)
                    a.then_inc(s_mhi, 1)
                else:
                    nc.scalar.activation(h_hi[:, 0:HP, NS:TOK], src.rearrange("p (m t) -> p m t", m=HP), ACT.Copy).then_inc(s_mhi, 1)

            for u in range(NU + 1):
                if u < NU:
                    exps(u)
                if u >= 1:
                    copy_pt(u - 1)
                if u >= 3 and (u - 3) % 8 == 7 and u - 3 < UNITS:
                    mix_hi((u - 3) // 8)
            mix_hi(HP)

            def h2_copy(n):
                act.wait_ge(s_h2t, n + 1)
                if n >= 1:
                    act.wait_ge(s_lg, n)
                else:
                    act.wait_ge(s_mlo, HP + 1)
                nc.scalar.activation(h2_T[:, 0:4, :], PS[:, 4, :].rearrange("p (k t) -> p k t", k=4), ACT.Copy)
                nc.scalar.activation(h2_T[:, 4:8, :], PS[:, 5, :].rearrange("p (k t) -> p k t", k=4), ACT.Copy).then_inc(s_h2c, 1)

            def root(n):
                act.wait_ge(s_var, n + 1)
                nc.scalar.activation(std, mv[:, 1:2], ACT.Sqrt, bias=eps).then_inc(s_std, 1)

            root(0)
            for n in range(1, NT):
                h2_copy(n - 1)
                root(n)
            h2_copy(NT - 1)

            def expert_whi(e, b, first=False):
                act.wait_ge(s_raw[b], 16 * (NCH // 2 + 1) + 8 * (e - b))
                if first:
                    act.wait_ge(s_mo, NT)
                else:
                    act.wait_ge(s_hid, e - 1)
                nc.scalar.activation(w_hi[:, b, :], raw[:, b, :], ACT.Copy).then_inc(s_whi, 1)

            def expert_ohi(e, b, first=False):
                act.wait_ge(s_rawo[b], 16 + 8 * (e - b))
                if not isinstance(e, int) or e >= 1:
                    act.wait_ge(s_y, e)
                nc.scalar.activation(wo_hi, raw_o[:, b, :].rearrange("p (k n) -> p k n", k=2), ACT.Copy).then_inc(s_ohi, 1)

            def gathered_hi(c, b):
                act.wait_ge(s_hgt, c + 1)
                if not isinstance(c, int) or c >= 2:
                    act.wait_ge(s_hid, c - 1)
                nc.scalar.activation(hgT_hi[:, b, 0:4, :], PS[:, 2, :].rearrange("p (k t) -> p k t", k=4), ACT.Copy)
                nc.scalar.activation(hgT_hi[:, b, 4:8, :], PS[:, 3, :].rearrange("p (k t) -> p k t", k=4), ACT.Copy).then_inc(s_ghi, 1)

            def exp_neg(c, b):
                act.wait_ge(s_hid, c + 1)
                nc.scalar.activation(sil[:, 0, :], PS[:, b, 0:DE], ACT.Exp, scale=-1.0).then_inc(s_ex, 1)

            def act_hi_copy(c, b):
                act.wait_ge(s_at, c + 1)
                nc.scalar.activation(aT_hi[:, b, :, :], PS[:, 4, 0:2 * P].rearrange("p (k t) -> p k t", k=2), ACT.Copy).then_inc(s_ahi, 1)

            def y_copy(c, b):
                act.wait_ge(s_y, c + 1)
                if not isinstance(c, int) or c >= 2:
                    act.wait_ge(s_yst[b], 8 * (c - b))
                nc.scalar.activation(y_sb[:, b, 0:CH], PS[:, 6, :], ACT.Copy).then_inc(s_ya, 1)

            act.wait_ge(s_one, 1)
            nc.scalar.activation(rt[:, 0:NG * NT], rt[:, 0:NG * NT], ACT.Exp)
            nc.scalar.activation(rt[:, 900:900 + NT], rt[:, 900:900 + NT], ACT.Exp).then_inc(s_gexp, 1)

            expert_whi(0, 0, True)
            expert_whi(1, 1, True)
            gathered_hi(0, 0)

            def act_pair(i, last=False):
                for b in range(2):
                    c = 2 * i + b
                    exp_neg(c, b)
                    if not (isinstance(c, int) and c == 0):
                        y_copy(c - 1, 1 - b)
                    if not (last and b == 1):
                        gathered_hi(c + 1, 1 - b)
                    expert_ohi(c, b)
                    act_hi_copy(c, b)
                    if not last:
                        expert_whi(c + 2, b)

            act_pair(0)
            with act.Fori(1, NE // 2 - 1) as i:
                act_pair(i)
            act_pair(NE // 2 - 1, True)
            y_copy(NE - 1, 1)
            more = overflow_chunks(act)
            with act.If(more > 0):
                act.wait_ge(s_yst[1], 16 * (NE // 2))
                with act.Fori(0, more) as i:
                    e = act.value_load(over_i[0:1, bass.ds(i + 1, 1)], min_val=0, max_val=NE - 1)
                    act.wait_ge(s_wlo, i + (E0 + NE))
                    act.wait_ge(s_olo, i + NE)
                    act.dma_start(raw_slot(1), we_in[e].rearrange("(k p) n -> p k n", p=P)).then_inc(s_ovw, 16)
                    act.dma_start(raw_o[:, 1, :].rearrange("p (k n) -> p k n", k=2),
                                  we_out[e].rearrange("(k p) n -> p k n", p=P)).then_inc(s_ovw, 16)
                    act.wait_ge(s_ovw, 32 * i + 32)
                    act.wait_ge(s_hid, i + NE)
                    nc.scalar.activation(w_hi[:, 1, :], raw[:, 1, :], ACT.Copy).then_inc(s_whi, 1)
                    act.wait_ge(s_y, i + NE)
                    nc.scalar.activation(wo_hi, raw_o[:, 1, :].rearrange("p (k n) -> p k n", k=2), ACT.Copy).then_inc(s_ohi, 1)
                    gathered_hi(i + NE, 1)
                    exp_neg(i + NE, 1)
                    act_hi_copy(i + NE, 1)
                    act.wait_ge(s_y, i + (NE + 1))
                    nc.scalar.activation(y_sb[:, 1, 0:CH], PS[:, 6, :], ACT.Copy).then_inc(s_ya, 1)
            for n in range(NT):
                root(NT + n)

        @block.vector
        def _(dve):
            chain = [0]

            def link(ins_):
                chain[0] += 1
                ins_.then_inc(s_dv, 1)
                dve.wait_ge(s_dv, chain[0])

            V = nc.vector
            dve.wait_ge(s_silu, 1)
            link(V.tensor_scalar(silu_t[96:112, :], silu_t[96:112, :], 1.0, None, ALU.add))
            link(V.reciprocal(silu_t[96:112, :], silu_t[96:112, :]))
            V.tensor_tensor(rows[96:112, :], rows[96:112, :], silu_t[96:112, :], ALU.mult).then_inc(s_silu, 1)
            dve.wait_ge(s_rows, 1)
            V.tensor_copy(cols[:, :], PS[:, 0, 0:P]).then_inc(s_cols, 1)
            dve.wait_ge(s_ch, 1)
            V.tensor_tensor(cond_r[:, :, 2:4], cols[:, 96:96 + 2 * KD].rearrange("p (j k) -> p k j", j=2),
                            cond_r[:, :, 0:2].bitcast(fp32), ALU.subtract).then_inc(s_cl, 1)

            def split_lo(n):
                for h in range(2):
                    half = slice(h * 4 * CH, (h + 1) * 4 * CH)
                    dve.wait_ge(s_whi, 2 * n + h + 1)
                    V.tensor_tensor(w_lo[:, n % 2, half], raw[:, n % 2, half], w_hi[:, n % 2, half].bitcast(fp32),
                                    ALU.subtract).then_inc(s_wlo, 1)

            def mod_columns(bank, first, end):
                src = PS[:, bank, 0:4 * (end - first)].rearrange("p (s j) -> p s j", j=4)
                link(V.tensor_tensor(modc[:, first:end, :], src[:, :, 0:2],
                                     cols[:, first:end].unsqueeze(2).to_broadcast([P, end - first, 2]), ALU.add))
                return V.tensor_tensor(modc[:, first:end, :], src[:, :, 2:4], modc[:, first:end, :], ALU.add)

            for n in range(4):
                split_lo(n)
            dve.wait_ge(s_at0, 4)
            link(mod_columns(1, 0, 16))
            link(V.tensor_scalar(modc[:, 8:16, :], modc[:, 8:16, :], 1.0, None, ALU.add))
            for k in range(KD + 1):
                if k < KD:
                    dve.wait_ge(s_xt, k + 1)
                    if k >= 2:
                        dve.wait_ge(s_hhi, k - 1)
                        dve.wait_ge(s_hlo, k - 1)
                    b = 4 + 2 * (k % 2)
                    V.tensor_scalar(h_tmp[:, k % 2, 0:NS], PS[:, b, :], modc[:, 8 + k, 0:1], modc[:, k, 0:1], ALU.mult, ALU.add)
                    V.tensor_scalar(h_tmp[:, k % 2, NS:TOK], PS[:, b + 1, 0:NP], modc[:, 8 + k, 1:2], modc[:, k, 1:2], ALU.mult, ALU.add).then_inc(s_h, 1)
                if k >= 1:
                    dve.wait_ge(s_hhi, k)
                    V.tensor_tensor(h_lo[:, k - 1, :], h_tmp[:, (k - 1) % 2, :], h_hi[:, k - 1, :].bitcast(fp32), ALU.subtract).then_inc(s_hlo, 1)
                if k == 5:
                    split_lo(4)
            dve.wait_ge(s_const, 16)
            dve.wait_ge(s_bt, 16 * 3 * HEADS)
            for a in range(3):
                m = V.tensor_tensor(bias_t[:, a, :, :], bias_t[:, a, :, :],
                                    mask3[:, a, :].unsqueeze(1).to_broadcast([P, DR, SPAN]), ALU.add)
            m.then_inc(s_bm, 1)
            split_lo(5)
            for at in (0, NS + 1, TOK + 2):
                link(V.memset(conv_y[:, :, at:at + 1], 0.0))
            for n in (6, 7, 8):
                split_lo(n)
            for m in range(4):
                dve.wait_ge(s_acc_a, m + 1)
                dve.wait_ge(s_acc, 5 + m)
                b = 2 * (m % 2)
                V.tensor_tensor(conv_y[:, m, 1:1 + HALF], PS[:, b, 0:HALF], conv_y[:, m, 1:1 + HALF], ALU.mult)
                V.tensor_tensor(conv_y[:, m, 1 + HALF:1 + NS], PS[:, b + 1, 0:NS - HALF], conv_y[:, m, 1 + HALF:1 + NS], ALU.mult)
                V.tensor_tensor(conv_y[:, m, 2 + NS:2 + TOK], PS[:, b + 1, NS - HALF:HALF],
                                conv_y[:, m, 2 + NS:2 + TOK], ALU.mult).then_inc(s_acc_d, 1)
            for n in (9, 10):
                split_lo(n)
            dve.wait_ge(s_acc_d, 4)
            for m in range(4):
                link(V.tensor_scalar(conv_o[:, m, 1:2 + TOK], conv_y[:, m, 0:1 + TOK], cols[:, 64 + m:65 + m], None, ALU.mult))
                for tap in (1, 2):
                    link(V.scalar_tensor_tensor(out=conv_o[:, m, 1:2 + TOK], in0=conv_y[:, m, tap:tap + 1 + TOK],
                                                scalar=cols[:, 64 + 4 * tap + m:65 + 4 * tap + m], in1=conv_o[:, m, 1:2 + TOK],
                                                op0=ALU.mult, op1=ALU.add))
                dve.wait_ge(s_acc, 9 + m)
                b = 2 * (m % 2)
                V.tensor_tensor(conv_o[:, m, 1:1 + HALF], PS[:, b, 0:HALF], conv_o[:, m, 1:1 + HALF], ALU.mult)
                V.tensor_tensor(conv_o[:, m, 1 + HALF:1 + NS], PS[:, b + 1, 0:NS - HALF], conv_o[:, m, 1 + HALF:1 + NS], ALU.mult)
                V.tensor_tensor(conv_o[:, m, 2 + NS:2 + TOK], PS[:, b + 1, NS - HALF:HALF],
                                conv_o[:, m, 2 + NS:2 + TOK], ALU.mult).then_inc(s_acc_d, 1)
                if m == 1:
                    split_lo(11)
            for n in range(12, 18):
                split_lo(n)
            dve.wait_ge(s_at0, NA)
            mod_columns(7, 16, 48).then_inc(s_mod, 1)
            dve.wait_ge(s_ckt, 1)
            dve.wait_ge(s_acc_d, 8)
            for j in range(2):
                a = V.tensor_copy(ck_T[:, 2 * j:2 * j + 2, :], PS[:, 4 + j, :].rearrange("p (m t) -> p m t", m=2))
            a.then_inc(s_cks, 1)
            split_lo(18)
            split_lo(19)
            dve.wait_ge(s_chi, 1)
            V.tensor_tensor(h_lo[:, 4:8, 0:NS], conv_o[:, :, 1:1 + NS], h_hi[:, 4:8, 0:NS].bitcast(fp32), ALU.subtract)
            V.tensor_tensor(h_lo[:, 4:8, NS:TOK], conv_o[:, :, 2 + NS:2 + TOK],
                            h_hi[:, 4:8, NS:TOK].bitcast(fp32), ALU.subtract).then_inc(s_clo, 1)

            def softmax_max(u):
                dve.wait_ge(s_s, u + 1)
                if u >= 2:
                    dve.wait_ge(s_p, u - 1)
                if u < UNITS:
                    h, n = u // NB, u % NB
                    if n == 0:
                        dve.wait_ge(s_bias[h % 2], 48 * (h // 2 + 1))
                    link(V.tensor_tensor(PS[:, u % 2, 0:LOC], PS[:, u % 2, 0:LOC], bias_s[:, h % 2, KIND[n], :], ALU.add))
                    V.tensor_reduce(nmax[:, u % 2, 0:1], PS[:, u % 2, :], AX.X, ALU.max, negate=True).then_inc(s_nm, 1)
                else:
                    V.tensor_reduce(nmax[:, u % 2, :], PS[:, u % 2, :].rearrange("p (j t) -> p j t", j=4), AX.X, ALU.max,
                                    negate=True).then_inc(s_nm, 1)

            def scale_out(u):
                dve.wait_ge(s_p, u + 1)
                dve.wait_ge(s_o, u + 1)
                if u < UNITS:
                    h, n = u // NB, u % NB
                    g = h // 2
                    if g >= 2 and u % 8 == 0:
                        dve.wait_ge(s_ot, g - 1)
                    link(V.reciprocal(rinv[:, u % 2, 0:1], rsum[:, u % 4, 0:1]))
                    V.tensor_scalar(att_o[:, g % 2, n, (h % 2) * DH:(h % 2 + 1) * DH], PS[:, 4 + u % 2, 0:DH],
                                    rinv[:, u % 2, 0:1], None, ALU.mult).then_inc(s_os, 1)
                else:
                    j = u - UNITS
                    if j == 0:
                        dve.wait_ge(s_ot, HP - 1)
                    link(V.reciprocal(rinv[:, u % 2, :], rsum[:, u % 4, :]))
                    V.tensor_tensor(att_o[:, 0, :, j * DH:(j + 1) * DH],
                                    PS[:, 4 + u % 2, 0:4 * DH].rearrange("p (j d) -> p j d", j=4),
                                    rinv[:, u % 2, :].unsqueeze(2).to_broadcast([P, 4, DH]), ALU.mult).then_inc(s_os, 1)

            def mix_lo(g):
                dve.wait_ge(s_mhi, g + 1)
                src = PS[:, 6 + g % 2, :]
                if g < HP:
                    s4 = src.rearrange("p (n r c) -> p n r c", n=NB, r=ROWS)
                    for n in range(NB):
                        hh = h_hi[:, g, 0:NS].rearrange("p (r n c) -> p n r c", n=NB, r=ROWS)[:, n]
                        ll = h_lo[:, g, 0:NS].rearrange("p (r n c) -> p n r c", n=NB, r=ROWS)[:, n]
                        a = V.tensor_tensor(ll, s4[:, n], hh.bitcast(fp32), ALU.subtract)
                    a.then_inc(s_mlo, 1)
                else:
                    V.tensor_tensor(h_lo[:, 0:HP, NS:TOK], src.rearrange("p (m t) -> p m t", m=HP),
                                    h_hi[:, 0:HP, NS:TOK].bitcast(fp32), ALU.subtract).then_inc(s_mlo, 1)

            for u in range(NU + 2):
                if u < NU:
                    softmax_max(u)
                if u >= 2:
                    scale_out(u - 2)
                if u >= 4 and (u - 4) % 8 == 7 and u - 4 < UNITS:
                    mix_lo((u - 4) // 8)
            mix_lo(HP)

            def norm(t_, n):
                for j in range(2):
                    a = V.bn_stats(stat[:, 6 * j:6 * j + 6], t_[:, j * CH:(j + 1) * CH])
                link(a)
                V.bn_aggr(mv, stat).then_inc(s_var, 1)
                dve.wait_ge(s_std, n + 1)
                link(V.reciprocal(rstd, std))
                return V.tensor_scalar(t_, t_, mv[:, 0:1], rstd, ALU.subtract, ALU.mult)

            for n, t in enumerate(T_ORDER):
                j = cond_of(t)
                if n <= 1:
                    dve.wait_ge(s_vec[j], 80 if j == 1 else 48)
                    dve.wait_ge(s_xr[j], 16)
                    link(V.tensor_scalar(lin_a[:, j, :], lin_a[:, j, :], 1.0, None, ALU.add))
                    link(V.tensor_tensor(ln_t[:, 0, :] if n == 0 else ln_t[:, 1, :], ln1_b, lin_a[:, j, :], ALU.mult))
                    link(V.tensor_tensor(lin_b[:, j, :], lin_b[:, j, :], ln_t[:, 0, :] if n == 0 else ln_t[:, 1, :], ALU.add))
                    link(V.tensor_tensor(lin_a[:, j, :], lin_a[:, j, :], ln1_g, ALU.mult))
                if n >= 2:
                    dve.wait_ge(s_h2s[n % 2], 16 * (n // 2))
                    dve.wait_ge(s_h2t, n - 1)
                    dve.wait_ge(s_x1, n - 1)
                dve.wait_ge(s_mo, n + 1)
                b = 2 * (n % 2)
                row = ln_t[:, n % 2, :]
                V.tensor_tensor(row, PS[:, b:b + 2, :].rearrange("p a n -> p (a n)"), gate_a[:, j, :], ALU.mult).then_inc(s_mor, 1)
                dve.wait_ge(s_mor, n + 1)
                link(V.scalar_tensor_tensor(out=row, in0=x1[:, t, :], scalar=ALPHA, in1=row, op0=ALU.mult, op1=ALU.add))
                norm(row, n).then_inc(s_xn, 1)
                dve.wait_ge(s_plc, n + 1)
                link(V.tensor_tensor(row, row, lin_a[:, j, :], ALU.mult))
                V.tensor_tensor(row, row, lin_b[:, j, :], ALU.add).then_inc(s_h2, 1)

            L = logits[:, :, :]
            dve.wait_ge(s_lg, NT)
            for b in range(2):
                dve.wait_ge(s_h2s[b], 16 * (NT // 2 + 1 - b))
            dve.wait_ge(s_x1, NT)
            dve.wait_ge(s_rb, 32)
            link(V.tensor_tensor(L, PS[:, 6, 0:NT * (NG + NE)].rearrange("p (t n) -> p t n", t=NT),
                                 rb[:, :].unsqueeze(1).to_broadcast([P, NT, NG + NE]), ALU.add))

            def tile(at, *dims):
                n = 1
                for d in dims:
                    n *= d
                v = rt[:, at:at + NT * n]
                if len(dims) == 1:
                    return v.rearrange("p (t a) -> p t a", t=NT)
                return v.rearrange("p (t a b) -> p t a b", t=NT, a=dims[0])

            gexp, gmax, oh_g = tile(0, NG), tile(100, 1), tile(120, NG)
            tmp16, e4, oh1, oh2 = tile(200, NG, EG), tile(300, EG), tile(340, EG), tile(380, EG)
            m1, m2, e4b, tmp4 = tile(420, 1), tile(440, 1), tile(460, EG), tile(500, NG)
            d12 = rt[:, 900:900 + NT].rearrange("p (t a) -> p t a", t=NT)
            OH1, OH2, OHS = tile(540, NG, EG), tile(640, NG, EG), tile(740, NG, EG)
            rank = const[:, C_RANK:C_RANK + NG].unsqueeze(1).to_broadcast([P, NT, NG])

            def first_of(src, top, dst):
                link(V.tensor_tensor(dst, src, top.to_broadcast([P, NT, NG]), ALU.is_equal))
                link(V.tensor_tensor(dst, dst, rank, ALU.mult))
                link(V.tensor_reduce(tmp4[:, :, 0:1], dst, AX.X, ALU.max))
                link(V.tensor_tensor(dst, rank, tmp4[:, :, 0:1].to_broadcast([P, NT, NG]), ALU.is_equal))

            link(V.tensor_reduce(gmax, L[:, :, 0:NG], AX.X, ALU.max))
            first_of(L[:, :, 0:NG], gmax, oh_g)
            link(V.tensor_tensor(gexp, L[:, :, 0:NG], gmax.to_broadcast([P, NT, NG]), ALU.subtract))
            link(V.tensor_tensor(tmp16, L[:, :, NG:NG + NE].rearrange("p t (a b) -> p t a b", a=NG),
                                 oh_g.unsqueeze(3).to_broadcast([P, NT, NG, EG]), ALU.mult))
            link(V.tensor_reduce(e4, tmp16.rearrange("p t a b -> p t b a"), AX.X, ALU.add))
            link(V.tensor_reduce(m1, e4, AX.X, ALU.max))
            first_of(e4, m1, oh1)
            link(V.scalar_tensor_tensor(out=e4b, in0=oh1, scalar=-3.0e38, in1=e4, op0=ALU.mult, op1=ALU.add))
            link(V.tensor_reduce(m2, e4b, AX.X, ALU.max))
            first_of(e4b, m2, oh2)
            V.tensor_tensor(d12, m2, m1, ALU.subtract).then_inc(s_one, 1)
            for src, dst in ((oh1, OH1), (oh2, OH2)):
                for t in range(NT):
                    a = V.tensor_tensor(dst[:, t], oh_g[:, t, :].unsqueeze(2).to_broadcast([P, NG, EG]),
                                        src[:, t, :].unsqueeze(1).to_broadcast([P, NG, EG]), ALU.mult)
            link(a)
            V.tensor_tensor(OHS, OH1, OH2, ALU.add).then_inc(s_one, 1)
            dve.wait_ge(s_gexp, 1)
            gw = rt[:, 920:920 + 3 * NT].rearrange("p (a t) -> p a t", a=3)
            d12f = rt[:, 900:900 + NT]
            link(V.tensor_reduce(gw[:, 0, :], gexp, AX.X, ALU.add))
            link(V.scalar_tensor_tensor(out=gw[:, 1, :], in0=d12f, scalar=1.0, in1=gw[:, 0, :], op0=ALU.add, op1=ALU.mult))
            link(V.reciprocal(gates[:, 0, :], gw[:, 1, :]))
            link(V.tensor_tensor(gates[:, 1, :], gates[:, 0, :], d12f, ALU.mult))
            pos = rt[:, 1000:1000 + NT * NE].rearrange("p (t e) -> p t e", t=NT)
            cnt = rt[:, 1100:1100 + NE]
            ov = rt[:, 1120:1120 + NE]
            base = rt[:, 1140:1140 + NE]
            t16 = rt[:, 1160:1160 + NE]
            big = rt[:, 1200:1200 + NT * NE].rearrange("p (t e) -> p t e", t=NT)
            dve.wait_ge(s_pos, 1)
            link(V.tensor_copy(pos, PS[:, 7, 0:NT * NE].rearrange("p (t e) -> p t e", t=NT)))
            link(V.tensor_copy(cnt, PS[:, 7, NT * NE:(NT + 1) * NE]))
            link(V.tensor_scalar(ov, cnt, float(CAP), None, ALU.is_gt))
            for j in range(2, NT):
                link(V.tensor_scalar(t16, cnt, float(CAP * j), None, ALU.is_gt))
                link(V.tensor_tensor(ov, ov, t16, ALU.add))
            ends = rt[:, 1180:1180 + NE]
            link(V.memset(base[:, 0:1], 0.0))
            for e in range(1, NE):
                link(V.tensor_tensor(base[:, e:e + 1], base[:, e - 1:e], ov[:, e - 1:e], ALU.add))
            link(V.tensor_tensor(ends, base, ov, ALU.add))
            over_f = rt[:, 1300:1301 + MORE]
            le = rt[:, 1320:1320 + MORE * NE].rearrange("p (i e) -> p i e", i=MORE)
            link(V.tensor_tensor(le, ends.unsqueeze(1).to_broadcast([P, MORE, NE]),
                                 const[:, C_IOTA:C_IOTA + MORE].unsqueeze(2).to_broadcast([P, MORE, NE]), ALU.is_le))
            link(V.tensor_reduce(over_f[:, 1:1 + MORE], le, AX.X, ALU.add))
            link(V.tensor_scalar(over_f[:, 1:1 + MORE], over_f[:, 1:1 + MORE], float(NE - 1), None, ALU.min))
            link(V.tensor_copy(over_f[:, 0:1], ends[:, NE - 1:NE]))
            V.tensor_copy(over_i[:, :], over_f).then_inc(s_over, 1)
            link(V.tensor_scalar(base, base, float(CAP), None, ALU.mult))
            link(V.tensor_tensor(base, base, const[:, C_OVER:C_OVER + NE], ALU.add))
            link(V.tensor_scalar(big, pos, float(CAP), None, ALU.is_ge))
            link(V.tensor_tensor(big, big, base.unsqueeze(1).to_broadcast([P, NT, NE]), ALU.mult))
            link(V.tensor_tensor(pos, pos, big, ALU.add))
            link(V.tensor_tensor(pos, pos, const[:, C_E128:C_E128 + NE].unsqueeze(1).to_broadcast([P, NT, NE]), ALU.add))
            for c, oh in ((0, OH1), (1, OH2)):
                link(V.tensor_tensor(big, pos, oh.rearrange("p t a b -> p t (a b)"), ALU.mult))
                link(V.tensor_reduce(slot_f[:, c, :], big, AX.X, ALU.add))
            V.tensor_copy(slot_i[:, :, :], slot_f).then_inc(s_slot, 1)
            dve.wait_ge(s_lt, 1)
            V.tensor_copy(list_s, PS[:, 5, 0:NE + MORE]).then_inc(s_lc, 1)

            def expert_wlo(e, b):
                dve.wait_ge(s_whi, e + E0 + 1)
                V.tensor_tensor(w_lo[:, b, :], raw[:, b, :], w_hi[:, b, :].bitcast(fp32), ALU.subtract).then_inc(s_wlo, 1)

            def expert_olo(e, b):
                dve.wait_ge(s_ohi, e + 1)
                V.tensor_tensor(wo_lo, raw_o[:, b, :].rearrange("p (k n) -> p k n", k=2), wo_hi.bitcast(fp32),
                                ALU.subtract).then_inc(s_olo, 1)

            def gathered_lo(c, b):
                dve.wait_ge(s_ghi, c + 1)
                for j in range(2):
                    a = V.tensor_tensor(hgT_lo[:, b, 4 * j:4 * j + 4, :], PS[:, 2 + j, :].rearrange("p (k t) -> p k t", k=4),
                                        hgT_hi[:, b, 4 * j:4 * j + 4, :].bitcast(fp32), ALU.subtract)
                a.then_inc(s_glo, 1)

            def silu_up(c, b):
                dve.wait_ge(s_ex, c + 1)
                V.tensor_scalar(sil[:, 1, :], sil[:, 0, :], 1.0, None, ALU.add).then_inc(s_sl, 1)
                dve.wait_ge(s_sl, 4 * c + 1)
                V.reciprocal(sil[:, 1, :], sil[:, 1, :]).then_inc(s_sl, 1)
                dve.wait_ge(s_sl, 4 * c + 2)
                V.tensor_tensor(sil[:, 1, :], sil[:, 1, :], PS[:, b, 0:DE], ALU.mult).then_inc(s_sl, 1)
                dve.wait_ge(s_sl, 4 * c + 3)
                if not isinstance(c, int) or c >= 1:
                    dve.wait_ge(s_at, c)
                V.tensor_tensor(sil[:, 2, :], sil[:, 1, :], PS[:, b, DE:2 * DE], ALU.mult).then_inc(s_sl, 1)
                dve.wait_ge(s_sl, 4 * c + 4)

            def act_lo_sub(c, b):
                dve.wait_ge(s_ahi, c + 1)
                V.tensor_tensor(aT_lo[:, b, :, :], PS[:, 4, 0:2 * P].rearrange("p (k t) -> p k t", k=2),
                                aT_hi[:, b, :, :].bitcast(fp32), ALU.subtract).then_inc(s_alo, 1)

            def y_copy(c, b):
                dve.wait_ge(s_y, c + 1)
                if not isinstance(c, int) or c >= 2:
                    dve.wait_ge(s_yst[b], 8 * (c - b))
                V.tensor_copy(y_sb[:, b, CH:2 * CH], PS[:, 7, :]).then_inc(s_yd, 1)

            expert_wlo(0, 0)
            expert_wlo(1, 1)
            gathered_lo(0, 0)

            def dve_pair(i, last=False):
                for b in range(2):
                    c = 2 * i + b
                    silu_up(c, b)
                    if not (isinstance(c, int) and c == 0):
                        y_copy(c - 1, 1 - b)
                    if not (last and b == 1):
                        gathered_lo(c + 1, 1 - b)
                    expert_olo(c, b)
                    act_lo_sub(c, b)
                    if not last:
                        expert_wlo(c + 2, b)

            dve_pair(0)
            with dve.Fori(1, NE // 2 - 1) as i:
                dve_pair(i)
            dve_pair(NE // 2 - 1, True)
            y_copy(NE - 1, 1)
            more = overflow_chunks(dve)
            with dve.If(more > 0):
                dve.wait_ge(s_yst[1], 16 * (NE // 2))
                with dve.Fori(0, more) as i:
                    expert_wlo(i + NE, 1)
                    expert_olo(i + NE, 1)
                    gathered_lo(i + NE, 1)
                    silu_up(i + NE, 1)
                    act_lo_sub(i + NE, 1)
                    dve.wait_ge(s_y, i + (NE + 1))
                    V.tensor_copy(y_sb[:, 1, CH:2 * CH], PS[:, 7, :]).then_inc(s_yd, 1)

            dve.wait_ge(s_fv, 64)
            dve.wait_ge(s_x1, NT)
            for n, t in enumerate(T_ORDER):
                b = n % 2
                dve.wait_ge(s_fy[b], 32 * (n // 2 + 1))
                y1, y2, xt = fin_y[:, b, 0, :], fin_y[:, b, 1, :], x1[:, t, :]
                link(V.tensor_scalar(y1, y1, gates[:, 0, t:t + 1], None, ALU.mult))
                link(V.scalar_tensor_tensor(out=y1, in0=y2, scalar=gates[:, 1, t:t + 1], in1=y1, op0=ALU.mult, op1=ALU.add))
                link(V.tensor_tensor(y1, y1, fin_v[:, cond_of(t), :], ALU.mult))
                link(V.scalar_tensor_tensor(out=xt, in0=xt, scalar=ALPHA, in1=y1, op0=ALU.mult, op1=ALU.add))
                link(norm(xt, NT + n))
                link(V.tensor_tensor(xt, xt, fin_v[:, 2, :], ALU.mult))
                V.tensor_tensor(xt, xt, fin_v[:, 3, :], ALU.add).then_inc(s_fin, 1)

        @block.tensor
        def _(pe):
            T = nc.tensor

            def three(out, lh, ll, rh, rl, first, last):
                T.matmul(out, lh, rh, start=first, stop=False)
                T.matmul(out, lh, rl, start=False, stop=False)
                return T.matmul(out, ll, rh, start=False, stop=last)

            pe.wait_ge(s_const, 16)
            pe.wait_ge(s_silu, 2)
            T.transpose(PS[:, 0, 0:P], rows[:, :], ident).then_inc(s_rows, 1)

            def ada(a):
                n = ADA_N[a]
                if a >= 2:
                    pe.wait_ge(s_ar, a - 1)
                wh, wl = w_slot(w_hi, n), w_slot(w_lo, n)
                for k in range(KD):
                    if k % 4 == 0:
                        pe.wait_ge(s_wlo, 2 * n + k // 4 + 1)
                    out = PS[0:4, (2 if a < 4 else 4) + a % 2, :]
                    T.matmul(out, cond_r[:, k, :], wh[:, k, :], start=(k == 0), stop=False)
                    m = T.matmul(out, cond_r[:, k, :], wl[:, k, :], start=False, stop=(k == KD - 1))
                m.then_inc(s_ada, 1)

            def ada_turn(a):
                pe.wait_ge(s_ar, a + 1)
                for j in range(4):
                    s = 4 * a + j
                    out = PS[:, 1, 4 * s:4 * s + 4] if a < 4 else PS[:, 7, 4 * s - 64:4 * s - 60]
                    m = T.transpose(out, mod_row[:, a % 2, j * P:(j + 1) * P], const[0:4, C_ID:C_ID + 4])
                m.then_inc(s_at0, 1)

            pe.wait_ge(s_cl, 1)
            ada(0)
            for a in range(1, 4):
                ada(a)
                ada_turn(a - 1)
            ada_turn(3)
            pe.wait_ge(s_x, 32)
            for k in range(KD):
                if k >= 2:
                    pe.wait_ge(s_h, k - 1)
                b = 4 + 2 * (k % 2)
                for t in range(TS):
                    T.transpose(PS[:, b, t * P:(t + 1) * P], x_nat[:, t, k * P:(k + 1) * P], ident)
                T.transpose(PS[:, b + 1, 0:P], x_nat[:, TS, k * P:(k + 1) * P], ident).then_inc(s_xt, 1)
            pe.wait_ge(s_hlo, KD)

            def project(w, m):
                n = IN_N[w]
                wh, wl = w_slot(w_hi, n), w_slot(w_lo, n)
                i = SUM0[w] + m
                if i >= 2:
                    acc_read(pe, i - 2)
                for k in range(KD):
                    if m == 0 and k % 4 == 0:
                        pe.wait_ge(s_wlo, 2 * n + k // 4 + 1)
                    f, l = k == 0, k == KD - 1
                    a, b = wh[:, k, m * P:(m + 1) * P], wl[:, k, m * P:(m + 1) * P]
                    for h in range(2):
                        out = PS[:, 2 * (i % 2) + h, 0:HALF]
                        sl = slice(h * HALF, (h + 1) * HALF)
                        T.matmul(out, a, h_hi[:, k, sl], start=f, stop=False)
                        T.matmul(out, a, h_lo[:, k, sl], start=False, stop=False)
                    for h in range(2):
                        out = PS[:, 2 * (i % 2) + h, 0:HALF]
                        sl = slice(h * HALF, (h + 1) * HALF)
                        mm = T.matmul(out, b, h_hi[:, k, sl], start=False, stop=l)
                mm.then_inc(s_acc, 1)

            def project_v(t):
                n = IN_N[3]
                wh, wl = w_slot(w_hi, n), w_slot(w_lo, n)
                i = SUM0[3] + t
                acc_read(pe, i - 2)
                ts = slice(t * P, (t + 1) * P)
                for k in range(KD):
                    if t == 0 and k % 4 == 0:
                        pe.wait_ge(s_wlo, 2 * n + k // 4 + 1)
                    mm = three(PS[:, 2 * (i % 2), :], h_hi[:, k, ts], h_lo[:, k, ts], wh[:, k, :], wl[:, k, :], k == 0, k == KD - 1)
                mm.then_inc(s_acc, 1)

            for w in range(6):
                for m in range(NT if w == 3 else 4):
                    if w == 3:
                        project_v(m)
                    else:
                        project(w, m)
                    if m == 0 and 1 <= w <= 4:
                        ada_turn(3 + 2 * w)
                    if w == 5 and m == 1:
                        pe.wait_ge(s_mod, 1)
                        T.transpose(PS[0:64, 7, 0:P], modc[:, 16:48, :].rearrange("p s j -> p (s j)"), ident).then_inc(s_mrow, 1)
                if w < 4:
                    ada(4 + 2 * w)
                    ada(5 + 2 * w)
                    ada_turn(4 + 2 * w)
                elif w == 4:
                    pe.wait_ge(s_ck, 32)
                    pe.wait_ge(s_ar, NA)
                    for m in range(HP):
                        for j in range(2):
                            mm = T.transpose(PS[:, 4 + m // 2, (2 * (m % 2) + j) * P:(2 * (m % 2) + j + 1) * P],
                                             ck_nat[:, j, m * P:(m + 1) * P], ident)
                    mm.then_inc(s_ckt, 1)
            acc_read(pe, SUM0[6] - 1)
            for m in range(HP):
                mm = T.transpose(PS[:, 6, m * P:(m + 1) * P], kT[:, m, NS:TOK], ident)
            mm.then_inc(s_kp, 1)

            def scores(u):
                if u >= 2:
                    pe.wait_ge(s_p, u - 1)
                if u < UNITS:
                    h, n = u // NB, u % NB
                    g, r = h // 2, (h % 2) * DH
                    q = qT[r:r + DH, g, n * P:(n + 1) * P]
                    keys = kT[r:r + DH, g, 0:NS].rearrange("p (w c) -> p w c", c=GRID)[:, :, KEY0[n]:KEY0[n] + SPAN]
                    T.matmul(PS[:, u % 2, 0:LOC], q, keys, start=True, stop=True)
                    T.matmul(PS[:, u % 2, LOC:LOC + PAST], q, ck_T[r:r + DH, g, :], start=True, stop=True).then_inc(s_s, 1)
                else:
                    for j in range(4):
                        h = 2 * j + u - UNITS
                        g, r = h // 2, (h % 2) * DH
                        mm = T.matmul(PS[:, u % 2, j * P:(j + 1) * P], qT[r:r + DH, g, NS:TOK], kT[r:r + DH, g, NS:TOK],
                                      start=True, stop=True)
                    mm.then_inc(s_s, 1)

            def turn(u):
                pe.wait_ge(s_p, u + 1)
                if u >= 2:
                    pe.wait_ge(s_pts, u - 1)
                for j in range(4):
                    mm = T.transpose(PS[:, 2 + u % 2, j * P:(j + 1) * P], prob[:, u % 2, j * P:(j + 1) * P], ident)
                mm.then_inc(s_pt, 1)

            def values(u):
                pe.wait_ge(s_pts, u + 1)
                if u >= 2:
                    pe.wait_ge(s_os, u - 1)
                if u < UNITS:
                    h, n = u // NB, u % NB
                    for j in range(4):
                        v = vblk[:, 2 * n + j, h * DH:(h + 1) * DH] if j < 2 else ctx_v[:, j - 2, h * DH:(h + 1) * DH]
                        mm = T.matmul(PS[:, 4 + u % 2, 0:DH], prob_T[:, u % 2, j * P:(j + 1) * P], v, start=(j == 0), stop=(j == 3))
                    mm.then_inc(s_o, 1)
                else:
                    for j in range(4):
                        h = 2 * j + u - UNITS
                        mm = T.matmul(PS[:, 4 + u % 2, j * DH:(j + 1) * DH], prob_T[:, u % 2, j * P:(j + 1) * P],
                                      stage[:, 0, h * DH:(h + 1) * DH], start=True, stop=True)
                    mm.then_inc(s_o, 1)

            def turn_out(g):
                if g < HP:
                    pe.wait_ge(s_os, 8 * (g + 1))
                else:
                    pe.wait_ge(s_os, NU)
                if g >= 2:
                    pe.wait_ge(s_mlo, g - 1)
                for n in range(NB):
                    mm = T.transpose(PS[:, 6 + g % 2, n * P:(n + 1) * P], att_o[:, g % 2, n, :], back if g < HP else ident)
                mm.then_inc(s_ot, 1)

            pe.wait_ge(s_cks, 1)
            pe.wait_ge(s_kps, 1)
            pe.wait_ge(s_mrs, 1)
            pe.wait_ge(s_vb, 128)
            pe.wait_ge(s_cv, 32)
            for u in range(NU + 3):
                if u < NU:
                    scores(u)
                if 2 <= u < NU + 2:
                    values(u - 2)
                if 1 <= u < NU + 1:
                    turn(u - 1)
                if u >= 3 and (u - 3) % 8 == 7 and u - 3 < UNITS:
                    turn_out((u - 3) // 8)
            turn_out(HP)

            def mix_out(n):
                t = T_ORDER[n]
                if n >= 2:
                    pe.wait_ge(s_mor, n - 1)
                ts = slice(t * P, (t + 1) * P)
                for c in range(2):
                    wh, wl = w_slot(w_hi, OUT_N[c]), w_slot(w_lo, OUT_N[c])
                    for k in range(KD):
                        mm = three(PS[:, 2 * (n % 2) + c, :], h_hi[:, k, ts], h_lo[:, k, ts], wh[:, k, :], wl[:, k, :],
                                   k == 0, k == KD - 1)
                mm.then_inc(s_mo, 1)

            def router(n):
                t = T_ORDER[n]
                pe.wait_ge(s_h2, n + 1)
                if n >= 1:
                    pe.wait_ge(s_h2c, n)
                for k in range(KD):
                    mm = T.transpose(PS[:, 4 + k // 4, (k % 4) * P:(k % 4 + 1) * P], ln_t[:, n % 2, k * P:(k + 1) * P], ident)
                mm.then_inc(s_h2t, 1)
                pe.wait_ge(s_h2c, n + 1)
                for k in range(KD):
                    mm = T.matmul(PS[:, 6, t * (NG + NE):(t + 1) * (NG + NE)], h2_T[:, k, :], wr[:, k, :],
                                  start=(k == 0), stop=(k == KD - 1))
                mm.then_inc(s_lg, 1)

            pe.wait_ge(s_mlo, HP + 1)
            pe.wait_ge(s_clo, 1)
            pe.wait_ge(s_wlo, E0)
            pe.wait_ge(s_wrl, 32)
            for n in range(NT + 1):
                if n < NT:
                    mix_out(n)
                if n >= 1:
                    router(n - 1)

            oh = rt[:, 740:740 + NT * NE].rearrange("p (t e) -> p t e", t=NT)
            pe.wait_ge(s_one, 2)
            for t in range(NT + 1):
                for s in range(min(t, NT - 1) + 1):
                    whole = s < t
                    mm = T.matmul(PS[:, 7, t * NE:(t + 1) * NE], ones[:, :] if whole else tri, oh[:, s, :],
                                  start=(s == 0), stop=(s == min(t, NT - 1)))
            mm.then_inc(s_pos, 1)

            def turn_rows(c, b, over=False):
                if over:
                    pe.wait_ge(s_ovg, 16 * (c - NE) + 16)
                else:
                    pe.wait_ge(s_hg[b], 16 + 8 * (c - b))
                if not isinstance(c, int) or c >= 1:
                    pe.wait_ge(s_glo, c)
                for k in range(KD):
                    mm = T.transpose(PS[:, 2 + k // 4, (k % 4) * P:(k % 4 + 1) * P], hg[:, b, k * P:(k + 1) * P], ident)
                mm.then_inc(s_hgt, 1)

            def up(c, b):
                pe.wait_ge(s_wlo, c + E0 + 1)
                pe.wait_ge(s_glo, c + 1)
                if not isinstance(c, int) or c >= 2:
                    pe.wait_ge(s_sl, 4 * c - 4)
                wh, wl = w_slot(w_hi, b), w_slot(w_lo, b)
                for k in range(KD):
                    mm = three(PS[:, b, :], hgT_hi[:, b, k, :], hgT_lo[:, b, k, :], wh[:, k, :], wl[:, k, :], k == 0, k == KD - 1)
                mm.then_inc(s_hid, 1)

            def down(c, b):
                pe.wait_ge(s_alo, c + 1)
                pe.wait_ge(s_olo, c + 1)
                if not isinstance(c, int) or c >= 1:
                    pe.wait_ge(s_ya, c)
                    pe.wait_ge(s_yd, c)
                for h in range(2):
                    for k in range(2):
                        mm = three(PS[:, 6 + h, :], aT_hi[:, b, k, :], aT_lo[:, b, k, :], wo_hi[:, k, h * CH:(h + 1) * CH],
                                   wo_lo[:, k, h * CH:(h + 1) * CH], k == 0, k == 1)
                mm.then_inc(s_y, 1)

            def turn_act(c, b):
                pe.wait_ge(s_sl, 4 * c + 4)
                if not isinstance(c, int) or c >= 1:
                    pe.wait_ge(s_alo, c)
                for k in range(2):
                    mm = T.transpose(PS[:, 4, k * P:(k + 1) * P], sil[:, 2, k * P:(k + 1) * P], ident)
                mm.then_inc(s_at, 1)

            pe.wait_ge(s_ll, 16)
            T.transpose(PS[:, 5, 0:NE + MORE], list_r[0:NE + MORE, :], const[0:NE + MORE, C_ID:C_ID + NE + MORE]).then_inc(s_lt, 1)
            turn_rows(0, 0)

            def pe_pair(i, last=False):
                for b in range(2):
                    c = 2 * i + b
                    up(c, b)
                    if not (isinstance(c, int) and c == 0):
                        down(c - 1, 1 - b)
                    if not (last and b == 1):
                        turn_rows(c + 1, 1 - b)
                    turn_act(c, b)

            pe_pair(0)
            with pe.Fori(1, NE // 2 - 1) as i:
                pe_pair(i)
            pe_pair(NE // 2 - 1, True)
            down(NE - 1, 1)
            more = overflow_chunks(pe)
            with pe.If(more > 0):
                with pe.Fori(0, more) as i:
                    turn_rows(i + NE, 1, True)
                    up(i + NE, 1)
                    turn_act(i + NE, 1)
                    down(i + NE, 1)


def constants():
    import numpy as np
    P, NE, CAP, NT, MORE, SPAN, CB, NS = 128, 16, 128, 5, 10, 32, 16, 8
    ident = np.eye(P, dtype=np.float32)
    tri = np.triu(np.ones((P, P), np.float32), 1)
    k = np.arange(SPAN)[None, :]
    c = CB - 1 - (np.arange(P) % CB)[:, None]
    masks = []
    for kind in range(3):
        key = k + (32, 8, 0)[kind]
        q = c + (48, 16, 0)[kind]
        lo = np.clip(q - 8, 0, 48)
        masks.append(np.where((key >= lo) & (key < lo + 16), 0.0, -1e30).astype(np.float32))
    row = np.concatenate([
        np.arange(4, 0, -1), np.arange(NE) * CAP, NE * CAP - CAP - np.arange(NE) * CAP]).astype(np.float32)
    tok = np.arange(NT)[None, :] * P + np.arange(P)[:, None]
    iota = np.arange(MORE)
    return np.concatenate([ident, tri, *masks, np.tile(row, (P, 1)), tok.astype(np.float32),
                           np.tile(iota, (P, 1)).astype(np.float32), ident[::-1]], axis=1).astype(np.float32)


_INS = ["x_prompt", "x_sample", "cache_k", "cache_v", "c", "c_ctx", "w_ada", "b_ada", "w_in", "conv_w", "rpb", "w_out",
        "ln1_g", "ln1_b", "w_router_group", "b_router_group", "w_router_expert", "b_router_expert", "w_expert_in",
        "w_expert_out", "ln2_g", "ln2_b"]
_OUTS = [("y_prompt", (1, 128, 1024)), ("y_sample", (1, 512, 1024)), ("new_k", (1, 1, 8, 128, 64)),
         ("new_v", (1, 1, 8, 128, 64))]


def kernel(**inputs):
    import numpy as _np
    import concourse.bacc as _bacc
    from concourse import mybir as _mybir
    from concourse.bass_utils import run_bass_kernel_spmd as _run

    nc = _bacc.Bacc("TRN2", target_bir_lowering=False, num_devices=1)
    arrays, ins, outs = {}, {}, {}
    for name in _INS:
        arrays[f"in_{name}"] = _np.ascontiguousarray(inputs[name])
    arrays["in_const"] = constants()
    for name in _INS + ["const"]:
        a = arrays[f"in_{name}"]
        ins[name] = nc.dram_tensor(f"in_{name}", a.shape, _mybir.dt.from_np(a.dtype), kind="ExternalInput").ap()
    for name, shape in _OUTS:
        outs[name] = nc.dram_tensor(f"out_{name}", shape, _mybir.dt.float32, kind="ExternalOutput").ap()
    build(nc, ins, outs)
    r = _run(nc, [arrays], core_ids=[0])
    return tuple(r.results[0][f"out_{name}"] for name, _ in _OUTS)
```

```python
import concourse.bass as bass
from concourse import mybir
from contextlib import ExitStack


def build(nc, ins, outs):
    fp32 = mybir.dt.float32
    fp32r = mybir.dt.float32r
    i32 = mybir.dt.int32
    ALU = mybir.AluOpType
    ACT = mybir.ActivationFunctionType
    AX = mybir.AxisListType

    NS = ins["x_sample"].shape[1]
    NP = ins["x_prompt"].shape[1]
    D = ins["x_sample"].shape[2]
    TOK = NS + NP
    P = 128
    KD = D // P
    NT = TOK // P
    TS = NS // P
    HEADS, PAST, DH = ins["cache_k"].shape[2:]
    AW = HEADS * DH
    HP = HEADS // 2
    GRID = 64
    ROWS = NS // GRID
    NB, CB, SPAN = 4, 16, 32
    KEY0 = [0, 8, 24, 32]
    KIND = [2, 1, 1, 0]
    LOC = ROWS * SPAN
    NE = ins["w_expert_in"].shape[1]
    NG = 4
    EG = NE // NG
    DE = ins["w_expert_out"].shape[2]
    CH = 512
    HALF = TOK // 2
    ALPHA = 2.0 ** 0.25
    EPS = 1e-5
    CAP = P
    MORE = (2 * TOK) // CAP
    SLOTS = (NE + MORE) * CAP
    NA = 2 * 6
    RP0 = CB
    RPW = 64
    DR = 2 * ROWS - 1
    TW = DR * SPAN
    UNITS = 2 * HP * NB
    NU = UNITS + 2

    C_ID, C_TRI, C_MASK = 0, P, 2 * P
    C_RANK = C_MASK + 3 * SPAN
    C_E128 = C_RANK + NG
    C_OVER = C_E128 + NE
    C_TOK = C_OVER + NE
    C_IOTA = C_TOK + NT
    C_BACK = C_IOTA + MORE
    C_CH = C_BACK + P
    C_COL = C_CH + NE + MORE + 1
    C_END = C_COL + P

    ctx = ExitStack()
    with ctx:
        def sb(name, shape, dt=fp32):
            return ctx.enter_context(nc.sbuf_tensor(name, shape, dt))

        def sem(name):
            return ctx.enter_context(nc.semaphore(name))

        act_hi = sb("act_hi", [P, KD * TOK], fp32r)
        act_lo = sb("act_lo", [P, KD * TOK], fp32r)
        w_hi = sb("w_hi", [P, 2, KD * CH], fp32r)
        w_lo = sb("w_lo", [P, 2, KD * CH], fp32r)
        raw = sb("raw", [P, 2, KD * CH])
        g1 = sb("g1", [P, NT * D])
        uni = sb("uni", [P, 11264])
        cond_r = sb("cond_r", [P, KD, 4], fp32r)
        const = sb("const", [P, C_END])
        rows = sb("rows", [P, P])
        cols = sb("cols", [P, P])
        modc = sb("modc", [P, 6 * KD, 2])
        wr = sb("wr", [P, KD, NG + NE])
        logits = sb("logits", [P, NT, NG + NE])
        small = sb("small", [P, 96])
        gates = sb("gates", [P, 2, NT])
        rb = sb("rb", [P, NG + NE])
        over_i = sb("over_i", [P, 1 + MORE], i32)
        over_col = sb("over_col", [P, 1], i32)
        slot_i = sb("slot_i", [P, 2, NT], i32)
        PS = ctx.enter_context(nc.psum_tensor("PS", [P, 8, 512], fp32))

        ones = rows
        ident = const[:, C_ID:C_ID + P]
        back = const[:, C_BACK:C_BACK + P]
        tri = const[:, C_TRI:C_TRI + P]
        mask3 = const[:, C_MASK:C_MASK + 3 * SPAN].rearrange("p (a k) -> p a k", a=3)

        def dram(name, shape, dt=fp32):
            return nc.dram_tensor(name, shape, dt, kind="Internal").ap()

        def dap(t, offset, pattern):
            return bass.AP(tensor=t.tensor, offset=offset, ap=pattern)

        v_dram = dram("v_scratch", (NS, AW))
        rp_dram = dram("rpb_padded", (HEADS * DR, RPW))
        bias_dram = dram("bias_windows", (HEADS * CB, 3 * TW))
        mod_dram = dram("mod_rows", (4 * KD * 2, P))
        h2_dram = dram("h2_rows", (TOK, D))
        y_dram = dram("expert_rows", (SLOTS, D))

        x_nat = g1[:, :].rearrange("p (t d) -> p t d", t=NT)
        qT = g1[:, 0:HP * TOK].rearrange("p (m t) -> p m t", m=HP)
        kT = g1[:, HP * TOK:2 * HP * TOK].rearrange("p (m t) -> p m t", m=HP)
        x1 = x_nat
        h_hi = act_hi[:, :].rearrange("p (k t) -> p k t", k=KD)
        h_lo = act_lo[:, :].rearrange("p (k t) -> p k t", k=KD)
        PADW = TOK + 8
        conv_y = uni[:, 0:4 * PADW].rearrange("p (m t) -> p m t", m=4)
        conv_o = uni[:, 4 * PADW:8 * PADW].rearrange("p (m t) -> p m t", m=4)
        o = 8 * PADW
        bias_t = uni[:, o:o + 3 * TW].rearrange("p (a r k) -> p a r k", a=3, r=DR)
        h_tmp = uni[:, 6700:6700 + 2 * TOK].rearrange("p (b t) -> p b t", b=2)
        rp_pad = uni[:, 8000:8000 + RPW]
        ck_nat = uni[:, 8064:8064 + 2 * AW].rearrange("p (a n) -> p a n", a=2)
        silu_t = uni[:, 9100:9100 + P]
        mod_row = uni[0:4, 9300:9300 + 2 * CH].rearrange("p (b n) -> p b n", b=2)
        stage = uni[:, 5200:5200 + 2 * AW].rearrange("p (b n) -> p b n", b=2)
        vblk = raw[:, 0, :].rearrange("p (j n) -> p j n", j=8)
        ctx_v = uni[:, 0:2 * AW].rearrange("p (j n) -> p j n", j=2)
        ck_T = uni[:, 2 * AW:2 * AW + HP * PAST].rearrange("p (m t) -> p m t", m=HP)
        bias_s = uni[:, 6224:6224 + 2 * 3 * LOC].rearrange("p (b a n) -> p b a n", b=2, a=3)
        prob = uni[:, 7760:7760 + 3 * 512].rearrange("p (b n) -> p b n", b=3)
        prob_T = uni[:, 9296:9296 + 1024].rearrange("p (b n) -> p b n", b=2)
        gate_a = raw[:, 1, 0:2 * D].rearrange("p (j d) -> p j d", j=2)
        lin_a = raw[:, 1, 2 * D:4 * D].rearrange("p (j d) -> p j d", j=2)
        lin_b = [uni[:, 0:D], uni[:, 2 * D:3 * D]]
        ln1_g = uni[:, 3 * D:4 * D]
        ln1_b = uni[:, 4 * D:5 * D]
        h2_rows = uni[:, 5200:5200 + 2 * D].rearrange("p (b d) -> p b d", b=2)
        ln_t = uni[:, 8 * D:10 * D].rearrange("p (b d) -> p b d", b=2)
        h2_T = uni[:, 10 * D:11 * D].rearrange("p (k t) -> p k t", k=KD)
        rt = uni[:, 9700:11264]
        slot_hot = uni[:, 8192:8192 + 2 * NT * P].rearrange("p (i s) -> p i s", i=2 * NT)
        chunk_ge = uni[:, 7248:7248 + 2 * NT * (NE + MORE + 1)].rearrange("p (i c) -> p i c", i=2 * NT)
        chunk_tok = uni[:, 7520:7520 + 2 * NT * (NE + MORE)].rearrange("p (i c) -> p i c", i=2 * NT)
        raw_o = uni[:, 0:2 * 2 * D].rearrange("p (b n) -> p b n", b=2)
        hg = uni[:, 4096:4096 + 2 * D].rearrange("p (b n) -> p b n", b=2)
        y_sb = uni[:, 6144:6144 + 2 * D].rearrange("p (b n) -> p b n", b=2)
        sil = uni[:, 8192:8192 + 3 * DE].rearrange("p (b n) -> p b n", b=3)
        list_s = uni[:, 9480:9480 + NE + MORE].bitcast(i32)
        slot_f = uni[:, 9510:9510 + 2 * NT].rearrange("p (c t) -> p c t", c=2)
        hgT_hi = act_hi[:, 0:2 * D].rearrange("p (b k t) -> p b k t", b=2, k=KD)
        hgT_lo = act_lo[:, 0:2 * D].rearrange("p (b k t) -> p b k t", b=2, k=KD)
        aT_hi = act_hi[:, 2 * D:2 * D + 4 * P].rearrange("p (b k t) -> p b k t", b=2, k=2)
        aT_lo = act_lo[:, 2 * D:2 * D + 4 * P].rearrange("p (b k t) -> p b k t", b=2, k=2)
        wo_hi = act_hi[:, 2560:2560 + 2 * D].rearrange("p (k n) -> p k n", k=2)
        wo_lo = act_lo[:, 2560:2560 + 2 * D].rearrange("p (k n) -> p k n", k=2)
        fin_v = raw[:, 0, :].rearrange("p (a d) -> p a d", a=4)
        fin_y = uni[:, 0:NT * 2 * D].rearrange("p (n a d) -> p n a d", n=NT, a=2)
        nmax = small[:, 0:8].rearrange("p (b n) -> p b n", b=2)
        rsum = small[:, 8:24].rearrange("p (b n) -> p b n", b=4)
        rinv = small[:, 24:32].rearrange("p (b n) -> p b n", b=2)
        stat = small[:, 32:56].rearrange("p (b n) -> p b n", b=2)
        mv = small[:, 56:60].rearrange("p (b n) -> p b n", b=2)
        rstd = small[:, 60:62]
        std = small[:, 62:64]
        nbias = small[:, 64:66]
        eps = small[:, 66:67]

        w_ada, w_in, w_out = ins["w_ada"][0], ins["w_in"][0], ins["w_out"][0]
        we_in, we_out = ins["w_expert_in"][0], ins["w_expert_out"][0]
        IN_ORDER = [4, 5, 3, 2, 0, 1]
        IN_N = [4, 7, 10, 13, 16, 17]
        ADA_N = [0, 1, 2, 3, 5, 6, 8, 9, 11, 12, 14, 15]
        OUT_N = [18, 19]
        NCH = NA + len(IN_N) + len(OUT_N)
        stream = [None] * NCH
        for i, n in enumerate(ADA_N):
            stream[n] = (w_ada, i)
        for i, n in enumerate(IN_N):
            stream[n] = (w_in, IN_ORDER[i])
        for i, n in enumerate(OUT_N):
            stream[n] = (w_out, i)
        SUM0 = [0, 4, 8, 12, 12 + NT, 16 + NT, 20 + NT]
        E0 = 2 * NCH

        s_const = sem("const_loaded")
        s_small = sem("small_rows_loaded")
        s_silu = sem("silu_steps")
        s_rows = sem("rows_transposed")
        s_cols = sem("cols_ready")
        s_raw = [[sem(f"raw_{b}_half_{h}_loaded") for h in range(2)] for b in range(2)]
        s_ada = sem("ada_chunks_multiplied")
        s_ch = sem("condition_hi_ready")
        s_cl = sem("condition_lo_ready")
        s_ar = sem("mod_sums_copied")
        s_at0 = sem("mod_sums_transposed")
        s_mod = sem("modulation_steps")
        s_x = sem("x_loaded")
        s_xt = sem("x_transposed")
        s_h = sem("h_modulated_sample")
        s_hp = sem("h_modulated_prompt")
        s_hhi = sem("h_hi_ready")
        s_hlo = sem("h_lo_ready")
        s_whi = sem("w_hi_ready")
        s_wlo = sem("w_lo_ready")
        s_wlp = sem("expert_w_lo_second_half_ready")
        s_whp = sem("expert_w_hi_second_half_ready")
        s_acc = sem("proj_sums_ready")
        s_acc_a = sem("proj_sums_read_by_scalar")
        s_acc_d = sem("proj_sums_read_by_vector")
        s_vout = [sem("v_tile_stored_0"), sem("v_tile_stored_1")]
        s_cache = sem("cache_stored")
        s_kp = sem("k_prompt_transposed")
        s_kps = sem("k_prompt_staged")
        s_ck = sem("ctx_k_loaded")
        s_ckt = sem("ctx_k_transposed")
        s_cks = sem("ctx_k_ready")
        s_rpz = sem("rpb_pad_zeroed")
        s_rp = sem("rpb_steps")
        s_bt = sem("bias_window_loaded")
        s_bm = sem("bias_masked")
        s_bd = sem("bias_stored")
        s_bias = [sem("bias_head_loaded_0"), sem("bias_head_loaded_1")]
        s_mrow = sem("mod_rows_transposed")
        s_mrs = sem("mod_rows_staged")
        s_mrd = sem("mod_rows_stored")
        s_chi = sem("conv_hi_ready")
        s_clo = sem("conv_lo_ready")
        s_vb = sem("v_blocks_loaded")
        s_cv = sem("ctx_v_loaded")
        s_s = sem("scores_ready")
        s_nm = sem("row_max_ready")
        s_dv = sem("vector_chain")
        s_p = sem("probs_ready")
        s_pt = sem("probs_transposed")
        s_pts = sem("probs_T_ready")
        s_o = sem("att_out_ready")
        s_pn = sem("probs_normed")
        s_mhi = sem("mix_hi_ready")
        s_mlo = sem("mix_lo_ready")
        s_vec = [sem("ln1_vectors_loaded_sample"), sem("ln1_vectors_loaded_prompt")]
        s_xr = [sem("x_reloaded_sample"), sem("x_reloaded_prompt")]
        s_wrl = sem("router_weights_loaded")
        s_mo = sem("mix_out_ready")
        s_mor = sem("mix_out_read")
        s_var = sem("variance_ready")
        s_std = sem("std_ready")
        s_nb = sem("norm_scale_ready")
        s_xn = sem("normed_ready")
        s_h2 = sem("h2_ready")
        s_h2s = [sem("h2_stored_0"), sem("h2_stored_1")]
        s_x1 = sem("x1_ready")
        s_plc = sem("pool_chain")
        s_h2t = sem("h2_transposed")
        s_h2c = sem("h2_T_ready")
        s_rb = sem("router_biases_loaded")
        s_sl = sem("expert_silu_steps")
        s_lg = sem("logits_sum_ready")
        s_one = sem("choices_ready")
        s_pos = sem("positions_ready")
        s_slot = sem("slots_ready")
        s_gexp = sem("group_exp_ready")
        s_hot = sem("list_one_hots_ready")
        s_lt = sem("list_sums_ready")
        s_lc = sem("list_ready")
        s_rawo = [sem("raw_out_loaded_0"), sem("raw_out_loaded_1")]
        s_hg = [sem("rows_gathered_0"), sem("rows_gathered_1")]
        s_hgt = sem("rows_transposed_for_expert")
        s_ghi = sem("gathered_hi_ready")
        s_glo = sem("gathered_lo_ready")
        s_ohi = sem("expert_out_w_hi_ready")
        s_olo = sem("expert_out_w_lo_ready")
        s_hid = sem("hidden_ready")
        s_ex = sem("silu_exp_ready")
        s_act = sem("expert_act_ready")
        s_at = sem("expert_act_transposed")
        s_ahi = sem("expert_act_hi_ready")
        s_alo = sem("expert_act_lo_ready")
        s_y = sem("expert_rows_ready")
        s_ya = sem("expert_rows_half_0_copied")
        s_yd = sem("expert_rows_half_1_copied")
        s_yst = [sem("expert_rows_stored_0"), sem("expert_rows_stored_1")]
        s_yz = sem("overflow_slots_filled")
        s_over = sem("overflow_table_ready")
        s_ovw = sem("overflow_weights_loaded")
        s_ovc = sem("overflow_column_ready")
        s_ovg = sem("overflow_rows_gathered")
        s_ovs = sem("overflow_rows_stored")
        s_fv = sem("final_vectors_loaded")
        s_fy = [sem(f"final_rows_gathered_{n}") for n in range(NT)]
        s_fg = sem("first_rows_weighted")
        s_fs = sem("rows_summed")
        s_fm = sem("rows_gated")
        s_fn = sem("final_rows_normed")
        s_fw = sem("final_rows_times_gain")
        s_fin = [sem(f"final_tile_{n}_ready") for n in range(NT)]
        s_done = sem("outputs_stored")

        block = ctx.enter_context(nc.Block())

        def raw_full(eng, n, h):
            eng.wait_ge(s_raw[n % 2][h], 16 * (n // 2 + 1))

        def chunk_src(w, c):
            return w[:, c * CH:(c + 1) * CH].rearrange("(k p) n -> p k n", p=P)

        def raw_slot(n):
            return raw[:, n % 2, :].rearrange("p (k n) -> p k n", k=KD)

        def w_slot(t, n):
            return t[:, n % 2, :].rearrange("p (k n) -> p k n", k=KD)

        def acc_read(eng, i):
            if i < 4:
                eng.wait_ge(s_acc_a, i + 1)
            elif i < 12:
                eng.wait_ge(s_acc_d, i - 3)
            else:
                eng.wait_ge(s_acc_a, i - 7)

        def w_used(eng, n):
            if n in ADA_N:
                eng.wait_ge(s_ada, ADA_N.index(n) + 1)
            elif n in IN_N:
                eng.wait_ge(s_acc, SUM0[IN_N.index(n) + 1])

        def overflow_chunks(eng):
            eng.wait_ge(s_over, 1)
            return eng.value_load(over_i[0:1, 0:1], min_val=0, max_val=MORE)

        T_ORDER = [NT - 1] + list(range(NT - 1))

        def cond_of(t):
            return 1 if t == NT - 1 else 0

        @block.sync
        def _(sp):
            sp.wait_ge(s_rpz, 1)
            sp.dma_start(rows[96:104, :], ins["c"][0].rearrange("(k c) -> k c", c=P)).then_inc(s_small, 16)
            sp.dma_start(rows[104:112, :], ins["c_ctx"].rearrange("(k c) -> k c", c=P)).then_inc(s_small, 16)
            sp.dma_start(rows[0:48, :], ins["b_ada"][0].rearrange("(s c) -> s c", c=P)).then_inc(s_small, 16)
            sp.dma_start(rows[64:76, :], ins["conv_w"][0].rearrange("k (m c) -> (k m) c", c=P)).then_inc(s_small, 16)
            sp.dma_start(const[:, :], ins["const"]).then_inc(s_const, 16)

            def load_chunk(n):
                for h in range(2):
                    if n >= 2:
                        sp.wait_ge(s_wlo, 2 * (n - 2) + h + 1)
                    sp.dma_start(raw_slot(n)[:, 4 * h:4 * h + 4, :],
                                 chunk_src(*stream[n])[:, 4 * h:4 * h + 4, :]).then_inc(s_raw[n % 2][h], 16)

            def mod_vector(dst, v, j):
                sp.dma_start(dst.rearrange("p (s c) -> p s c", s=KD),
                             dap(mod_dram, (v * KD * 2 + j) * P, [[0, P], [2 * P, KD], [1, P]])).then_inc(s_vec[j], 16)

            for n in range(4):
                load_chunk(n)
            sp.dma_start(x_nat[:, 0:TS, :], ins["x_sample"][0].rearrange("(t p) d -> p t d", p=P)).then_inc(s_x, 16)
            sp.dma_start(x_nat[:, TS, :], ins["x_prompt"][0]).then_inc(s_x, 16)
            for n in range(4, NCH):
                load_chunk(n)
            sp.wait_ge(s_wlo, 2 * (OUT_N[0] + 1))
            for b in range(2):
                sp.wait_ge(s_vout[b], 16 * (TS // 2))
            for n in range(NB):
                for j in range(2):
                    src = dap(v_dram, (j * 4 * GRID + KEY0[n]) * AW, [[GRID * AW, 4], [AW, SPAN], [1, AW]])
                    sp.dma_start(vblk[:, 2 * n + j, :], src).then_inc(s_vb, 16)
            sp.wait_ge(s_wlo, E0)
            sp.wait_ge(s_clo, 4)
            sp.wait_ge(s_mrd, 16)
            mod_vector(gate_a[:, 1, :], 0, 1)
            mod_vector(lin_a[:, 1, :], 2, 1)
            mod_vector(lin_b[1], 1, 1)
            sp.dma_start(ln1_g, dap(ins["ln1_g"], 0, [[0, P], [1, D]])).then_inc(s_vec[1], 16)
            sp.dma_start(ln1_b, dap(ins["ln1_b"], 0, [[0, P], [1, D]])).then_inc(s_vec[1], 16)
            mod_vector(gate_a[:, 0, :], 0, 0)
            mod_vector(lin_a[:, 0, :], 2, 0)
            sp.wait_ge(s_yz, 32)
            sp.wait_ge(s_o, NU)
            sp.wait_ge(s_kps, 1)
            sp.dma_start(x1[:, NT - 1, :], ins["x_prompt"][0]).then_inc(s_xr[1], 16)
            mod_vector(lin_b[0], 1, 0)
            sp.dma_start(x1[:, 0:TS, :], ins["x_sample"][0].rearrange("(t p) d -> p t d", p=P)).then_inc(s_xr[0], 16)
            def expert_in(e, slot):
                sp.wait_ge(s_wlo, e + E0 - 1)
                if isinstance(e, int) and e == 1:
                    sp.wait_ge(s_h2, NT)
                src = we_in[e].rearrange("(k p) n -> p k n", p=P)
                sp.dma_start(raw_slot(slot)[:, 0:4, :], src[:, 0:4, :]).then_inc(s_raw[slot][0], 16)
                if not isinstance(e, int) or e >= 2:
                    sp.wait_ge(s_wlp, e - 1)
                sp.dma_start(raw_slot(slot)[:, 4:8, :], src[:, 4:8, :]).then_inc(s_raw[slot][1], 16)

            def expert_out(e, slot, first):
                if first:
                    sp.wait_ge(s_h2, NT)
                    sp.wait_ge(s_x1, NT)
                else:
                    sp.wait_ge(s_olo, e - 1)
                sp.dma_start(raw_o[:, slot, :].rearrange("p (k n) -> p k n", k=2),
                             we_out[e].rearrange("(k p) n -> p k n", p=P)).then_inc(s_rawo[slot], 16)

            for b in range(2):
                expert_in(b, b)
            for b in range(2):
                expert_out(b, b, True)
            with sp.Fori(1, NE // 2) as i:
                for b in range(2):
                    expert_in(2 * i + b, b)
                    expert_out(2 * i + b, b, False)
            sp.wait_ge(s_wlo, E0 + NE - 1)
            sp.wait_ge(s_wlp, NE - 1)
            for j in range(2):
                sp.dma_start(fin_v[:, j, :].rearrange("p (s c) -> p s c", s=KD),
                             dap(mod_dram, (3 * KD * 2 + j) * P, [[0, P], [2 * P, KD], [1, P]])).then_inc(s_fv, 16)
            sp.dma_start(fin_v[:, 2, :], dap(ins["ln2_g"], 0, [[0, P], [1, D]])).then_inc(s_fv, 16)
            sp.dma_start(fin_v[:, 3, :], dap(ins["ln2_b"], 0, [[0, P], [1, D]])).then_inc(s_fv, 16)
            for n, t in enumerate(T_ORDER):
                sp.wait_ge(s_fin[n], 1)
                dst = outs["y_prompt"][0] if t == NT - 1 else outs["y_sample"][0][t * P:(t + 1) * P, :]
                sp.dma_start(dst, x1[:, t, :]).then_inc(s_done, 16)
            sp.wait_ge(s_done, 16 * NT)
            sp.wait_ge(s_cache, 32)

        @block.gpsimd
        def _(pool):
            nc.gpsimd.memset(rows[:, :], 0.0).then_inc(s_rpz, 1)
            nc.gpsimd.memset(rp_pad, 0.0).then_inc(s_rpz, 1)
            nc.gpsimd.memset(eps, EPS).then_inc(s_rpz, 1)
            pool.wait_ge(s_rpz, 3)
            pool.dma_start(rp_pad[0:HEADS * DR, RP0:RP0 + 2 * CB - 1],
                           ins["rpb"][0].rearrange("h r c -> (h r) c")).then_inc(s_rp, 16)
            pool.wait_ge(s_rp, 16)
            pool.dma_start(rp_dram, rp_pad[0:HEADS * DR, :]).then_inc(s_rp, 16)
            pool.wait_ge(s_rp, 32)
            for h in range(HEADS):
                for a in range(3):
                    src = dap(rp_dram, h * DR * RPW + RP0 - CB + 8 * a, [[1, CB], [RPW, DR], [1, SPAN]])
                    pool.dma_start(bias_t[CB * h:CB * h + CB, a, :, :], src).then_inc(s_bt, 16)
            pool.dma_start(ck_nat.rearrange("p a (h d) -> p a h d", h=HEADS)[:, 0],
                           ins["cache_k"][0, 0][:, 0:P, :].rearrange("h t d -> t h d")).then_inc(s_ck, 16)
            pool.dma_start(ck_nat.rearrange("p a (h d) -> p a h d", h=HEADS)[:, 1],
                           ins["cache_k"][0, 0][:, P:2 * P, :].rearrange("h t d -> t h d")).then_inc(s_ck, 16)
            pool.dma_start(wr[:, :, 0:NG], ins["w_router_group"][0].rearrange("(k p) n -> p k n", p=P)).then_inc(s_wrl, 16)
            pool.dma_start(wr[:, :, NG:NG + NE], ins["w_router_expert"][0].rearrange("(k p) n -> p k n", p=P)).then_inc(s_wrl, 16)
            pool.dma_start(rb[:, 0:NG], dap(ins["b_router_group"], 0, [[0, P], [1, NG]])).then_inc(s_rb, 16)
            pool.dma_start(rb[:, NG:NG + NE], dap(ins["b_router_expert"], 0, [[0, P], [1, NE]])).then_inc(s_rb, 16)
            pool.wait_ge(s_rows, 1)
            nc.gpsimd.memset(ones[:, :], 1.0).then_inc(s_rpz, 1)
            pool.wait_ge(s_bm, 1)
            pool.dma_start(bias_dram, bias_t.rearrange("p a r k -> p (a r k)")).then_inc(s_bd, 16)
            pool.wait_ge(s_bd, 16)

            def load_bias(h):
                if h >= 2:
                    pool.wait_ge(s_nm, NB * (h - 1))
                for a in range(3):
                    src = dap(bias_dram, h * CB * 3 * TW + a * TW,
                              [[SPAN, ROWS], [3 * TW, CB], [1, LOC]])
                    pool.dma_start(bias_s[:, h % 2, a, :], src).then_inc(s_bias[h % 2], 16)

            pool.wait_ge(s_acc_d, 8)
            for j in range(2):
                pool.dma_start(ctx_v[:, j, :].rearrange("p (h d) -> p h d", h=HEADS),
                               ins["cache_v"][0, 0][:, j * P:(j + 1) * P, :].rearrange("h t d -> t h d")).then_inc(s_cv, 16)
            for h in range(HEADS):
                load_bias(h)
                if h == 2:
                    for j in range(2):
                        r0 = (NE + j * MORE // 2) * CAP
                        pool.dma_start(y_dram[r0:r0 + MORE // 2 * CAP, :].rearrange("(p a) d -> p (a d)", p=P),
                                       g1[:, :]).then_inc(s_yz, 16)
            for n, t in enumerate(T_ORDER):
                pool.wait_ge(s_xn, n + 1)
                nc.gpsimd.tensor_tensor(x1[:, t, :], x1[:, t, :], ln1_g, ALU.mult).then_inc(s_plc, 1)
                pool.wait_ge(s_h2, n + 1)
                pool.dma_start(h2_dram[t * P:(t + 1) * P, :], h2_rows[:, n % 2, :]).then_inc(s_h2s[n % 2], 16)
                pool.wait_ge(s_plc, n + 1)
                nc.gpsimd.tensor_tensor(x1[:, t, :], x1[:, t, :], ln1_b, ALU.add).then_inc(s_x1, 1)
            def expert_wlo2(e, b):
                pool.wait_ge(s_whp, e + 1)
                half = slice(4 * CH, 8 * CH)
                nc.gpsimd.tensor_tensor(w_lo[:, b, half], raw[:, b, half], w_hi[:, b, half].bitcast(fp32),
                                        ALU.subtract).then_inc(s_wlp, 1)

            expert_wlo2(0, 0)
            pool.wait_ge(s_lc, 1)
            pool.wait_ge(s_x1, NT)
            for b in range(2):
                pool.wait_ge(s_h2s[b], 16 * (NT // 2 + 1 - b))

            def gather(c, b, col):
                pool.indirect_dma_start(hg[:, b, :], None, h2_dram,
                                        bass.IndirectOffsetOnAxis(ap=col, axis=0)).then_inc(s_hg[b], 16)

            def store_rows(c):
                pool.wait_ge(s_ya, c + 1)
                pool.wait_ge(s_yd, c + 1)
                pool.dma_start(y_dram[c * CAP:(c + 1) * CAP, :], y_sb[:, c % 2, :]).then_inc(s_yst[c % 2], 16)

            for c in range(NE):
                if c >= 2:
                    pool.wait_ge(s_hgt, c - 1)
                gather(c, c % 2, list_s[:, c:c + 1])
                if c == 1:
                    expert_wlo2(1, 1)
                if c >= 3:
                    expert_wlo2(c - 1, (c - 1) % 2)
                    store_rows(c - 3)
            expert_wlo2(NE - 1, 1)
            for c in range(NE - 3, NE):
                store_rows(c)
            more = overflow_chunks(pool)
            with pool.If(more > 0):
                with pool.Fori(0, more) as i:
                    expert_wlo2(i + NE, 1)
                    pool.wait_ge(s_hgt, i + NE)
                    nc.gpsimd.tensor_copy(over_col[:, :], list_s[:, bass.ds(i + NE, 1)]).then_inc(s_ovc, 1)
                    with pool.If(more > 0):
                        pool.wait_ge(s_ovc, i + 1)
                    pool.indirect_dma_start(hg[:, 1, :], None, h2_dram,
                                            bass.IndirectOffsetOnAxis(ap=over_col[:, 0:1], axis=0)).then_inc(s_ovg, 16)
                    pool.wait_ge(s_ya, i + (NE + 1))
                    pool.wait_ge(s_yd, i + (NE + 1))
                    pool.dma_start(y_dram[bass.ds((i + NE) * CAP, CAP), :], y_sb[:, 1, :]).then_inc(s_ovs, 16)
                    pool.wait_ge(s_ovs, 16 * i + 16)
            for b in range(2):
                pool.wait_ge(s_yst[b], 16 * (NE // 2))
            pool.wait_ge(s_olo, NE)
            pool.wait_ge(s_slot, 1)

            def token_rows(n):
                t = T_ORDER[n]
                for c in range(2):
                    pool.indirect_dma_start(fin_y[:, n, c, :], None, y_dram,
                                            bass.IndirectOffsetOnAxis(ap=slot_i[:, c, t:t + 1], axis=0)).then_inc(s_fy[n], 16)

            def gate_rows(n):
                pool.wait_ge(s_fs, n + 1)
                if n == 0:
                    pool.wait_ge(s_fv, 64)
                y1 = fin_y[:, n, 0, :]
                nc.gpsimd.tensor_tensor(y1, y1, fin_v[:, cond_of(T_ORDER[n]), :], ALU.mult).then_inc(s_fm, 1)

            def add_shift(n):
                pool.wait_ge(s_fw, n)
                xt = x1[:, T_ORDER[n], :]
                nc.gpsimd.tensor_tensor(xt, xt, fin_v[:, 3, :], ALU.add).then_inc(s_fin[n], 1)

            token_rows(0)
            token_rows(1)
            token_rows(2)
            for n in range(NT):
                gate_rows(n)
                if n + 3 < NT:
                    token_rows(n + 3)
                if n >= 3:
                    add_shift(n - 2)
            add_shift(NT - 2)

        @block.scalar
        def _(act):
            act.wait_ge(s_small, 64)
            nc.scalar.activation(silu_t[96:112, :], rows[96:112, :], ACT.Exp, scale=-1.0).then_inc(s_silu, 1)
            act.wait_ge(s_cols, 1)
            nc.scalar.activation(cond_r[:, :, 0:2], cols[:, 96:96 + 2 * KD].rearrange("p (j k) -> p k j", j=2),
                                 ACT.Copy).then_inc(s_ch, 1)

            def split_hi(n, halves=(0, 1)):
                if halves[0] == 0 and n >= 2:
                    w_used(act, n - 2)
                for h in halves:
                    raw_full(act, n, h)
                    half = slice(h * 4 * CH, (h + 1) * 4 * CH)
                    nc.scalar.activation(w_hi[:, n % 2, half], raw[:, n % 2, half], ACT.Copy).then_inc(s_whi, 1)

            def mod_copy(a):
                act.wait_ge(s_ada, a + 1)
                if a >= 2:
                    act.wait_ge(s_at0, a - 1)
                nc.scalar.activation(mod_row[:, a % 2, :], PS[0:4, (2 if a < 4 else 4) + a % 2, :], ACT.Copy).then_inc(s_ar, 1)

            split_hi(0)
            split_hi(1)
            mod_copy(0)
            split_hi(2)
            mod_copy(1)
            split_hi(3)
            mod_copy(2)
            mod_copy(3)
            for k in range(KD):
                if k in (3, 5):
                    split_hi(4, ((k - 3) // 2,))
                act.wait_ge(s_xt, k + 1)
                if k == 0:
                    act.wait_ge(s_mod, 1)
                if k >= 2:
                    act.wait_ge(s_hhi, k - 1)
                    act.wait_ge(s_hlo, k - 1)
                nc.scalar.activation(h_tmp[:, k % 2, NS:TOK], PS[:, 5 + 2 * (k % 2), 0:NP], ACT.Identity,
                                     bias=modc[:, k, 1:2], scale=modc[:, 8 + k, 1:2]).then_inc(s_hp, 1)
                act.wait_ge(s_hp, k + 1)
                act.wait_ge(s_h, k + 1)
                nc.scalar.activation(h_hi[:, k, :], h_tmp[:, k % 2, :], ACT.Copy).then_inc(s_hhi, 1)
            split_hi(5)

            def q_back(m, r0, r1):
                return bass.AP(tensor=g1, offset=m * TOK + P - 1 - CB * r0,
                               ap=[[NT * D, P], [-CB, r1 - r0], [P, NB], [-1, CB]])

            def evac(i):
                act.wait_ge(s_acc, i + 1)
                w = max(j for j in range(6) if SUM0[j] <= i)
                m = i - SUM0[w]
                b = 2 * (i % 2)
                if w == 0:
                    nc.scalar.activation(conv_y[:, m, 1:1 + HALF], PS[:, b, 0:HALF], ACT.Copy)
                    nc.scalar.activation(conv_y[:, m, 1 + HALF:1 + NS], PS[:, b + 1, 0:NS - HALF], ACT.Copy)
                    nc.scalar.activation(conv_y[:, m, 2 + NS:2 + TOK], PS[:, b + 1, NS - HALF:HALF], ACT.Copy).then_inc(s_acc_a, 1)
                elif w == 4:
                    r0 = HALF // GRID
                    nc.scalar.activation(q_back(m, 0, r0), PS[:, b, 0:HALF].rearrange("p (r n c) -> p r n c", n=NB, c=CB),
                                         ACT.Copy, scale=DH ** -0.5)
                    nc.scalar.activation(q_back(m, r0, ROWS), PS[:, b + 1, 0:NS - HALF].rearrange("p (r n c) -> p r n c", n=NB, c=CB),
                                         ACT.Copy, scale=DH ** -0.5)
                    nc.scalar.activation(qT[:, m, NS:TOK], PS[:, b + 1, NS - HALF:HALF], ACT.Copy,
                                         scale=DH ** -0.5).then_inc(s_acc_a, 1)
                elif w == 5:
                    nc.scalar.activation(kT[:, m, 0:HALF], PS[:, b, 0:HALF], ACT.Copy)
                    nc.scalar.activation(kT[:, m, HALF:TOK], PS[:, b + 1, 0:HALF], ACT.Copy).then_inc(s_acc_a, 1)
                else:
                    t = m
                    if t >= 2:
                        act.wait_ge(s_vout[t % 2], 16 * (t // 2))
                    else:
                        act.wait_ge(s_bd, 16)
                    nc.scalar.activation(stage[:, t % 2, :], PS[:, b, :], ACT.Copy).then_inc(s_acc_a, 1)
                    act.wait_ge(s_acc_a, i - 7)
                    if t < TS:
                        act.dma_start(v_dram[t * P:(t + 1) * P, :], stage[:, t % 2, :]).then_inc(s_vout[t % 2], 16)
                    else:
                        act.dma_start(outs["new_v"][0, 0].rearrange("h s d -> s h d"),
                                      stage[:, t % 2, :].rearrange("p (h d) -> p h d", h=HEADS)).then_inc(s_cache, 16)

            for w in range(6):
                n = IN_N[w]
                first, end = SUM0[w], SUM0[w + 1]
                scalar_reads = w not in (1, 2)
                if scalar_reads:
                    for i in range(first, end - 1):
                        evac(i)
                if w < 5:
                    split_hi(n + 2)
                if scalar_reads:
                    evac(end - 1)
                if w < 4:
                    for a in range(4 + 2 * w, 6 + 2 * w):
                        mod_copy(a)
                        split_hi(ADA_N[a] + 2)
                elif w == 4:
                    act.wait_ge(s_mrow, 1)
                    nc.scalar.activation(cols[0:64, :], PS[0:64, 7, 0:P], ACT.Copy).then_inc(s_mrs, 1)
                    act.wait_ge(s_mrs, 1)
                    act.dma_start(mod_dram, cols[0:64, :]).then_inc(s_mrd, 16)
            def prompt_k():
                act.wait_ge(s_kp, 1)
                act.wait_ge(s_vout[1], 32)
                nc.scalar.activation(stage[:, 1, :], PS[:, 6, :], ACT.Copy).then_inc(s_kps, 1)
                act.wait_ge(s_kps, 1)
                act.dma_start(outs["new_k"][0, 0].rearrange("h s d -> s h d"),
                              stage[:, 1, :].rearrange("p (h d) -> p h d", h=HEADS)).then_inc(s_cache, 16)

            def conv_hi(m):
                if m == 0:
                    act.wait_ge(s_acc_d, 8)
                    act.wait_ge(s_acc, SUM0[6])
                nc.scalar.activation(h_hi[:, 4 + m, 0:NS], conv_o[:, m, 1:1 + NS], ACT.Copy)
                nc.scalar.activation(h_hi[:, 4 + m, NS:TOK], conv_o[:, m, 2 + NS:2 + TOK], ACT.Copy).then_inc(s_chi, 1)

            def exps(u):
                act.wait_ge(s_nm, u + 1)
                if u >= 3:
                    act.wait_ge(s_pt, u - 2)
                if u < UNITS:
                    nc.scalar.activation(prob[:, u % 3, :], PS[:, u % 2, :], ACT.Exp, bias=nmax[:, u % 2, 0:1],
                                         accum_out=rsum[:, u % 4, 0:1]).then_inc(s_p, 1)
                else:
                    for j in range(4):
                        a = nc.scalar.activation(prob[:, u % 3, j * P:(j + 1) * P], PS[:, u % 2, j * P:(j + 1) * P], ACT.Exp,
                                                 bias=nmax[:, u % 2, j:j + 1], accum_out=rsum[:, u % 4, j:j + 1])
                    a.then_inc(s_p, 1)

            def copy_pt(u):
                act.wait_ge(s_pt, u + 1)
                if u >= 2:
                    act.wait_ge(s_o, u - 1)
                nc.scalar.activation(prob_T[:, u % 2, :], PS[:, 2 + u % 2, :], ACT.Copy).then_inc(s_pts, 1)

            def mix_hi(g):
                act.wait_ge(s_o, 8 * (g + 1) if g < HP else NU)
                src = PS[:, 6 + g % 2, :]
                if g < HP:
                    s4 = src.rearrange("p (n r c) -> p n r c", n=NB, r=ROWS)
                    d4 = h_hi[:, g, 0:NS].rearrange("p (r n c) -> p n r c", n=NB, r=ROWS)
                    for n in range(NB):
                        a = nc.scalar.activation(d4[:, n], s4[:, n], ACT.Copy)
                    a.then_inc(s_mhi, 1)
                else:
                    nc.scalar.activation(h_hi[:, 0:HP, NS:TOK], src.rearrange("p (m t) -> p m t", m=HP), ACT.Copy).then_inc(s_mhi, 1)

            for u in range(NU + 2):
                if u < NU:
                    exps(u)
                if u == 0:
                    prompt_k()
                if u >= 2:
                    copy_pt(u - 2)
                if u in (4, 6):
                    split_hi(OUT_N[1], ((u - 4) // 2,))
                if u in (8, 10, 12, 14):
                    conv_hi((u - 8) // 2)
                if u >= 4 and (u - 4) % 8 == 7 and u - 4 < UNITS:
                    mix_hi((u - 4) // 8)
            mix_hi(HP)

            def h2_copy(n):
                act.wait_ge(s_h2t, n + 1)
                if n >= 1:
                    act.wait_ge(s_lg, n)
                else:
                    act.wait_ge(s_mlo, HP + 1)
                nc.scalar.activation(h2_T[:, 0:4, :], PS[:, 4, :].rearrange("p (k t) -> p k t", k=4), ACT.Copy)
                nc.scalar.activation(h2_T[:, 4:8, :], PS[:, 5, :].rearrange("p (k t) -> p k t", k=4), ACT.Copy).then_inc(s_h2c, 1)

            def root(n):
                act.wait_ge(s_var, n + 1)
                nc.scalar.activation(std[:, n % 2:n % 2 + 1], mv[:, n % 2, 1:2], ACT.Sqrt, bias=eps).then_inc(s_std, 1)

            def normed(n):
                act.wait_ge(s_nb, n + 1)
                nc.scalar.activation(x1[:, T_ORDER[n], :], ln_t[:, n % 2, :], ACT.Identity, bias=nbias[:, n % 2:n % 2 + 1],
                                     scale=rstd[:, n % 2:n % 2 + 1]).then_inc(s_xn, 1)

            root(0)
            normed(0)
            for n in range(1, NT):
                h2_copy(n - 1)
                root(n)
                normed(n)

            def expert_whi(e, b, first=False):
                if first:
                    act.wait_ge(s_mo, NT)
                else:
                    act.wait_ge(s_hid, e - 1)
                for h, ready in ((0, s_whi), (1, s_whp)):
                    act.wait_ge(s_raw[b][h], 16 * (NCH // 2 + 1) + 8 * (e - b))
                    half = slice(h * 4 * CH, (h + 1) * 4 * CH)
                    nc.scalar.activation(w_hi[:, b, half], raw[:, b, half], ACT.Copy).then_inc(ready, 1)

            def expert_ohi(e, b, first=False):
                act.wait_ge(s_rawo[b], 16 + 8 * (e - b))
                if not isinstance(e, int) or e >= 1:
                    act.wait_ge(s_y, e)
                nc.scalar.activation(wo_hi, raw_o[:, b, :].rearrange("p (k n) -> p k n", k=2), ACT.Copy).then_inc(s_ohi, 1)

            def gathered_hi(c, b):
                act.wait_ge(s_hgt, c + 1)
                if not isinstance(c, int) or c >= 2:
                    act.wait_ge(s_hid, c - 1)
                nc.scalar.activation(hgT_hi[:, b, 0:4, :], PS[:, 2, :].rearrange("p (k t) -> p k t", k=4), ACT.Copy)
                nc.scalar.activation(hgT_hi[:, b, 4:8, :], PS[:, 3, :].rearrange("p (k t) -> p k t", k=4), ACT.Copy).then_inc(s_ghi, 1)

            def exp_neg(c, b):
                act.wait_ge(s_hid, c + 1)
                nc.scalar.activation(sil[:, 0, :], PS[:, b, 0:DE], ACT.Exp, scale=-1.0).then_inc(s_ex, 1)

            def act_hi_copy(c, b):
                act.wait_ge(s_at, c + 1)
                nc.scalar.activation(aT_hi[:, b, :, :], PS[:, 4, 0:2 * P].rearrange("p (k t) -> p k t", k=2), ACT.Copy).then_inc(s_ahi, 1)

            def y_copy(c, b):
                act.wait_ge(s_y, c + 1)
                if not isinstance(c, int) or c >= 2:
                    act.wait_ge(s_yst[b], 8 * (c - b))
                nc.scalar.activation(y_sb[:, b, 0:CH], PS[:, 6, :], ACT.Copy).then_inc(s_ya, 1)

            expert_whi(0, 0, True)
            h2_copy(NT - 1)
            act.wait_ge(s_one, 1)
            nc.scalar.activation(rt[:, 0:NG * NT], rt[:, 0:NG * NT], ACT.Exp)
            nc.scalar.activation(rt[:, 900:900 + NT], rt[:, 900:900 + NT], ACT.Exp).then_inc(s_gexp, 1)

            expert_whi(1, 1, True)
            gathered_hi(0, 0)

            def act_pair(i, last=False):
                for b in range(2):
                    c = 2 * i + b
                    exp_neg(c, b)
                    if not (last and b == 1):
                        gathered_hi(c + 1, 1 - b)
                    if not (isinstance(c, int) and c == 0):
                        y_copy(c - 1, 1 - b)
                    expert_ohi(c, b)
                    act_hi_copy(c, b)
                    if not last:
                        expert_whi(c + 2, b)

            act_pair(0)
            with act.Fori(1, NE // 2 - 1) as i:
                act_pair(i)
            act_pair(NE // 2 - 1, True)
            y_copy(NE - 1, 1)
            more = overflow_chunks(act)
            with act.If(more > 0):
                act.wait_ge(s_yst[1], 16 * (NE // 2))
                with act.Fori(0, more) as i:
                    e = act.value_load(over_i[0:1, bass.ds(i + 1, 1)], min_val=0, max_val=NE - 1)
                    act.wait_ge(s_wlo, i + (E0 + NE))
                    act.wait_ge(s_wlp, i + NE)
                    act.wait_ge(s_olo, i + NE)
                    act.dma_start(raw_slot(1), we_in[e].rearrange("(k p) n -> p k n", p=P)).then_inc(s_ovw, 16)
                    act.dma_start(raw_o[:, 1, :].rearrange("p (k n) -> p k n", k=2),
                                  we_out[e].rearrange("(k p) n -> p k n", p=P)).then_inc(s_ovw, 16)
                    act.wait_ge(s_ovw, 32 * i + 32)
                    act.wait_ge(s_hid, i + NE)
                    nc.scalar.activation(w_hi[:, 1, 0:4 * CH], raw[:, 1, 0:4 * CH], ACT.Copy).then_inc(s_whi, 1)
                    nc.scalar.activation(w_hi[:, 1, 4 * CH:8 * CH], raw[:, 1, 4 * CH:8 * CH], ACT.Copy).then_inc(s_whp, 1)
                    act.wait_ge(s_y, i + NE)
                    nc.scalar.activation(wo_hi, raw_o[:, 1, :].rearrange("p (k n) -> p k n", k=2), ACT.Copy).then_inc(s_ohi, 1)
                    gathered_hi(i + NE, 1)
                    exp_neg(i + NE, 1)
                    act_hi_copy(i + NE, 1)
                    act.wait_ge(s_y, i + (NE + 1))
                    nc.scalar.activation(y_sb[:, 1, 0:CH], PS[:, 6, :], ACT.Copy).then_inc(s_ya, 1)
            def weight_rows(n):
                act.wait_ge(s_fy[n], 32)
                y1 = fin_y[:, n, 0, :]
                nc.scalar.activation(y1, y1, ACT.Copy, scale=gates[:, 0, T_ORDER[n]:T_ORDER[n] + 1]).then_inc(s_fg, 1)

            act.wait_ge(s_slot, 1)
            weight_rows(0)
            weight_rows(1)
            for n in range(NT):
                if n + 2 < NT:
                    weight_rows(n + 2)
                root(NT + n)
                if 1 <= n < NT - 1:
                    act.wait_ge(s_nb, NT + n)
                    b = (NT + n) % 2
                    xt = x1[:, T_ORDER[n], :]
                    nc.scalar.activation(xt, xt, ACT.Identity, bias=nbias[:, b:b + 1], scale=rstd[:, b:b + 1]).then_inc(s_fn, 1)

        @block.vector
        def _(dve):
            chain = [0]

            def link(ins_):
                chain[0] += 1
                ins_.then_inc(s_dv, 1)
                dve.wait_ge(s_dv, chain[0])

            V = nc.vector
            dve.wait_ge(s_silu, 1)
            link(V.tensor_scalar(silu_t[96:112, :], silu_t[96:112, :], 1.0, None, ALU.add))
            link(V.reciprocal(silu_t[96:112, :], silu_t[96:112, :]))
            V.tensor_tensor(rows[96:112, :], rows[96:112, :], silu_t[96:112, :], ALU.mult).then_inc(s_silu, 1)
            dve.wait_ge(s_rows, 1)
            V.tensor_copy(cols[:, :], PS[:, 0, 0:P]).then_inc(s_cols, 1)
            dve.wait_ge(s_ch, 1)
            V.tensor_tensor(cond_r[:, :, 2:4], cols[:, 96:96 + 2 * KD].rearrange("p (j k) -> p k j", j=2),
                            cond_r[:, :, 0:2].bitcast(fp32), ALU.subtract).then_inc(s_cl, 1)

            def split_lo(n, halves=(0, 1)):
                for h in halves:
                    half = slice(h * 4 * CH, (h + 1) * 4 * CH)
                    dve.wait_ge(s_whi, 2 * n + h + 1)
                    V.tensor_tensor(w_lo[:, n % 2, half], raw[:, n % 2, half], w_hi[:, n % 2, half].bitcast(fp32),
                                    ALU.subtract).then_inc(s_wlo, 1)

            def mod_columns(bank, first, end):
                src = PS[:, bank, 0:4 * (end - first)].rearrange("p (s j) -> p s j", j=4)
                link(V.tensor_tensor(modc[:, first:end, :], src[:, :, 0:2],
                                     cols[:, first:end].unsqueeze(2).to_broadcast([P, end - first, 2]), ALU.add))
                return V.tensor_tensor(modc[:, first:end, :], src[:, :, 2:4], modc[:, first:end, :], ALU.add)

            for n in range(4):
                split_lo(n)
            dve.wait_ge(s_at0, 4)
            link(mod_columns(1, 0, 16))
            V.tensor_scalar(modc[:, 8:16, :], modc[:, 8:16, :], 1.0, None, ALU.add).then_inc(s_mod, 1)
            dve.wait_ge(s_mod, 1)
            for k in range(KD + 1):
                if k < KD:
                    dve.wait_ge(s_xt, k + 1)
                    if k >= 2:
                        dve.wait_ge(s_hhi, k - 1)
                        dve.wait_ge(s_hlo, k - 1)
                    b = 4 + 2 * (k % 2)
                    V.tensor_scalar(h_tmp[:, k % 2, 0:NS], PS[:, b, :], modc[:, 8 + k, 0:1], modc[:, k, 0:1], ALU.mult, ALU.add).then_inc(s_h, 1)
                if k >= 1:
                    dve.wait_ge(s_hhi, k)
                    V.tensor_tensor(h_lo[:, k - 1, :], h_tmp[:, (k - 1) % 2, :], h_hi[:, k - 1, :].bitcast(fp32), ALU.subtract).then_inc(s_hlo, 1)
                if k in (5, 7):
                    split_lo(4, ((k - 5) // 2,))
            dve.wait_ge(s_const, 16)
            dve.wait_ge(s_bt, 16 * 3 * HEADS)
            for a in range(3):
                m = V.tensor_tensor(bias_t[:, a, :, :], bias_t[:, a, :, :],
                                    mask3[:, a, :].unsqueeze(1).to_broadcast([P, DR, SPAN]), ALU.add)
            m.then_inc(s_bm, 1)
            split_lo(5)
            for at in (0, NS + 1, TOK + 2):
                link(V.memset(conv_y[:, :, at:at + 1], 0.0))
            for n in (6, 7, 8):
                split_lo(n)
            for m in range(4):
                dve.wait_ge(s_acc_a, m + 1)
                dve.wait_ge(s_acc, 5 + m)
                b = 2 * (m % 2)
                V.tensor_tensor(conv_y[:, m, 1:1 + HALF], PS[:, b, 0:HALF], conv_y[:, m, 1:1 + HALF], ALU.mult)
                V.tensor_tensor(conv_y[:, m, 1 + HALF:1 + NS], PS[:, b + 1, 0:NS - HALF], conv_y[:, m, 1 + HALF:1 + NS], ALU.mult)
                V.tensor_tensor(conv_y[:, m, 2 + NS:2 + TOK], PS[:, b + 1, NS - HALF:HALF],
                                conv_y[:, m, 2 + NS:2 + TOK], ALU.mult).then_inc(s_acc_d, 1)
            for n in (9, 10):
                split_lo(n)
            dve.wait_ge(s_acc_d, 4)
            for m in range(4):
                link(V.tensor_scalar(conv_o[:, m, 1:2 + TOK], conv_y[:, m, 0:1 + TOK], cols[:, 64 + m:65 + m], None, ALU.mult))
                for tap in (1, 2):
                    link(V.scalar_tensor_tensor(out=conv_o[:, m, 1:2 + TOK], in0=conv_y[:, m, tap:tap + 1 + TOK],
                                                scalar=cols[:, 64 + 4 * tap + m:65 + 4 * tap + m], in1=conv_o[:, m, 1:2 + TOK],
                                                op0=ALU.mult, op1=ALU.add))
                dve.wait_ge(s_acc, 9 + m)
                b = 2 * (m % 2)
                V.tensor_tensor(conv_o[:, m, 1:1 + HALF], PS[:, b, 0:HALF], conv_o[:, m, 1:1 + HALF], ALU.mult)
                V.tensor_tensor(conv_o[:, m, 1 + HALF:1 + NS], PS[:, b + 1, 0:NS - HALF], conv_o[:, m, 1 + HALF:1 + NS], ALU.mult)
                V.tensor_tensor(conv_o[:, m, 2 + NS:2 + TOK], PS[:, b + 1, NS - HALF:HALF],
                                conv_o[:, m, 2 + NS:2 + TOK], ALU.mult).then_inc(s_acc_d, 1)
                if m == 1:
                    split_lo(11)
            for n in range(12, 18):
                split_lo(n)
            dve.wait_ge(s_at0, NA)
            mod_columns(7, 16, 48).then_inc(s_mod, 1)
            dve.wait_ge(s_ckt, 1)
            dve.wait_ge(s_acc_d, 8)
            for j in range(2):
                a = V.tensor_copy(ck_T[:, 2 * j:2 * j + 2, :], PS[:, 4 + j, :].rearrange("p (m t) -> p m t", m=2))
            a.then_inc(s_cks, 1)
            split_lo(18)

            def conv_lo(m):
                dve.wait_ge(s_chi, m + 1)
                V.tensor_tensor(h_lo[:, 4 + m, 0:NS], conv_o[:, m, 1:1 + NS], h_hi[:, 4 + m, 0:NS].bitcast(fp32), ALU.subtract)
                V.tensor_tensor(h_lo[:, 4 + m, NS:TOK], conv_o[:, m, 2 + NS:2 + TOK],
                                h_hi[:, 4 + m, NS:TOK].bitcast(fp32), ALU.subtract).then_inc(s_clo, 1)

            def softmax_max(u):
                dve.wait_ge(s_s, u + 1)
                if u >= 2:
                    dve.wait_ge(s_p, u - 1)
                if u < UNITS:
                    h, n = u // NB, u % NB
                    if n == 0:
                        dve.wait_ge(s_bias[h % 2], 48 * (h // 2 + 1))
                    link(V.tensor_tensor(PS[:, u % 2, 0:LOC], PS[:, u % 2, 0:LOC], bias_s[:, h % 2, KIND[n], :], ALU.add))
                    V.tensor_reduce(nmax[:, u % 2, 0:1], PS[:, u % 2, :], AX.X, ALU.max, negate=True).then_inc(s_nm, 1)
                else:
                    V.tensor_reduce(nmax[:, u % 2, :], PS[:, u % 2, :].rearrange("p (j t) -> p j t", j=4), AX.X, ALU.max,
                                    negate=True).then_inc(s_nm, 1)

            def norm_probs(u):
                dve.wait_ge(s_p, u + 1)
                if u < UNITS:
                    link(V.reciprocal(rinv[:, u % 2, 0:1], rsum[:, u % 4, 0:1]))
                    V.tensor_scalar(prob[:, u % 3, :], prob[:, u % 3, :], rinv[:, u % 2, 0:1], None, ALU.mult).then_inc(s_pn, 1)
                else:
                    link(V.reciprocal(rinv[:, u % 2, :], rsum[:, u % 4, :]))
                    p4 = prob[:, u % 3, :].rearrange("p (j t) -> p j t", j=4)
                    V.tensor_tensor(p4, p4, rinv[:, u % 2, :].unsqueeze(2).to_broadcast([P, 4, P]), ALU.mult).then_inc(s_pn, 1)

            def mix_lo(g):
                dve.wait_ge(s_mhi, g + 1)
                src = PS[:, 6 + g % 2, :]
                if g < HP:
                    s4 = src.rearrange("p (n r c) -> p n r c", n=NB, r=ROWS)
                    for n in range(NB):
                        hh = h_hi[:, g, 0:NS].rearrange("p (r n c) -> p n r c", n=NB, r=ROWS)[:, n]
                        ll = h_lo[:, g, 0:NS].rearrange("p (r n c) -> p n r c", n=NB, r=ROWS)[:, n]
                        a = V.tensor_tensor(ll, s4[:, n], hh.bitcast(fp32), ALU.subtract)
                    a.then_inc(s_mlo, 1)
                else:
                    V.tensor_tensor(h_lo[:, 0:HP, NS:TOK], src.rearrange("p (m t) -> p m t", m=HP),
                                    h_hi[:, 0:HP, NS:TOK].bitcast(fp32), ALU.subtract).then_inc(s_mlo, 1)

            for u in range(NU + 1):
                if u < NU:
                    softmax_max(u)
                if u >= 1:
                    norm_probs(u - 1)
                if u in (5, 7):
                    split_lo(OUT_N[1], ((u - 5) // 2,))
                if u in (9, 11, 13, 15):
                    conv_lo((u - 9) // 2)
                if u >= 5 and (u - 5) % 8 == 7 and u - 5 < UNITS:
                    mix_lo((u - 5) // 8)
            mix_lo(HP - 1)
            mix_lo(HP)

            def moments(t_, n):
                b = n % 2
                for j in range(2):
                    a = V.bn_stats(stat[:, b, 6 * j:6 * j + 6], t_[:, j * CH:(j + 1) * CH])
                link(a)
                V.bn_aggr(mv[:, b, :], stat[:, b, :]).then_inc(s_var, 1)

            def inverse(n):
                b = n % 2
                dve.wait_ge(s_std, n + 1)
                link(V.reciprocal(rstd[:, b:b + 1], std[:, b:b + 1]))

            def scaled(dst, src, n, g, b_):
                b = n % 2
                link(V.scalar_tensor_tensor(out=dst, in0=src, scalar=mv[:, b, 0:1], in1=g, op0=ALU.subtract, op1=ALU.mult))
                return V.scalar_tensor_tensor(out=dst, in0=dst, scalar=rstd[:, b:b + 1], in1=b_, op0=ALU.mult, op1=ALU.add)

            for n, t in enumerate(T_ORDER):
                j = cond_of(t)
                if n <= 1:
                    dve.wait_ge(s_vec[j], 80 if j == 1 else 48)
                    dve.wait_ge(s_xr[j], 16)
                    if n == 0:
                        dve.wait_ge(s_cache, 32)
                    link(V.tensor_scalar(lin_a[:, j, :], lin_a[:, j, :], 1.0, None, ALU.add))
                    link(V.tensor_tensor(h2_rows[:, n, :], ln1_b, lin_a[:, j, :], ALU.mult))
                    link(V.tensor_tensor(lin_b[j], lin_b[j], h2_rows[:, n, :], ALU.add))
                    link(V.tensor_tensor(lin_a[:, j, :], lin_a[:, j, :], ln1_g, ALU.mult))
                if n >= 2:
                    dve.wait_ge(s_h2s[n % 2], 16 * (n // 2))
                    dve.wait_ge(s_h2t, n - 1)
                    dve.wait_ge(s_xn, n - 1)
                dve.wait_ge(s_mo, n + 1)
                b = 2 * (n % 2)
                row = ln_t[:, n % 2, :]
                V.tensor_tensor(row, PS[:, b:b + 2, :].rearrange("p a n -> p (a n)"), gate_a[:, j, :], ALU.mult).then_inc(s_mor, 1)
                dve.wait_ge(s_mor, n + 1)
                link(V.scalar_tensor_tensor(out=row, in0=x1[:, t, :], scalar=ALPHA, in1=row, op0=ALU.mult, op1=ALU.add))
                moments(row, n)
                inverse(n)
                V.tensor_scalar(nbias[:, n % 2:n % 2 + 1], mv[:, n % 2, 0:1], rstd[:, n % 2:n % 2 + 1], -1.0, ALU.mult,
                                ALU.mult).then_inc(s_nb, 1)
                scaled(h2_rows[:, n % 2, :], row, n, lin_a[:, j, :], lin_b[j]).then_inc(s_h2, 1)

            def expert_wlo(e, b):
                dve.wait_ge(s_whi, e + E0 + 1)
                half = slice(0, 4 * CH)
                V.tensor_tensor(w_lo[:, b, half], raw[:, b, half], w_hi[:, b, half].bitcast(fp32), ALU.subtract).then_inc(s_wlo, 1)

            expert_wlo(0, 0)
            L = logits[:, :, :]
            dve.wait_ge(s_lg, NT)
            dve.wait_ge(s_xn, NT)
            dve.wait_ge(s_rb, 32)
            link(V.tensor_tensor(L, PS[:, 6, 0:NT * (NG + NE)].rearrange("p (t n) -> p t n", t=NT),
                                 rb[:, :].unsqueeze(1).to_broadcast([P, NT, NG + NE]), ALU.add))

            def tile(at, *dims):
                n = 1
                for d in dims:
                    n *= d
                v = rt[:, at:at + NT * n]
                if len(dims) == 1:
                    return v.rearrange("p (t a) -> p t a", t=NT)
                return v.rearrange("p (t a b) -> p t a b", t=NT, a=dims[0])

            gexp, gmax, oh_g = tile(0, NG), tile(100, 1), tile(120, NG)
            tmp16, e4, oh1, oh2 = tile(200, NG, EG), tile(300, EG), tile(340, EG), tile(380, EG)
            m1, m2, e4b, tmp4 = tile(420, 1), tile(440, 1), tile(460, EG), tile(500, NG)
            d12 = rt[:, 900:900 + NT].rearrange("p (t a) -> p t a", t=NT)
            OH1, OH2, OHS = tile(540, NG, EG), tile(640, NG, EG), tile(740, NG, EG)
            V.memset(rt[:, 740 + NT * NE:740 + (NT + 1) * NE], 0.0)
            rank = const[:, C_RANK:C_RANK + NG].unsqueeze(1).to_broadcast([P, NT, NG])

            def first_of(src, top, dst):
                link(V.tensor_tensor(dst, src, top.to_broadcast([P, NT, NG]), ALU.is_equal))
                link(V.tensor_tensor(dst, dst, rank, ALU.mult))
                link(V.tensor_reduce(tmp4[:, :, 0:1], dst, AX.X, ALU.max))
                link(V.tensor_tensor(dst, rank, tmp4[:, :, 0:1].to_broadcast([P, NT, NG]), ALU.is_equal))

            link(V.tensor_reduce(gmax, L[:, :, 0:NG], AX.X, ALU.max))
            first_of(L[:, :, 0:NG], gmax, oh_g)
            link(V.tensor_tensor(gexp, L[:, :, 0:NG], gmax.to_broadcast([P, NT, NG]), ALU.subtract))
            link(V.tensor_tensor(tmp16, L[:, :, NG:NG + NE].rearrange("p t (a b) -> p t a b", a=NG),
                                 oh_g.unsqueeze(3).to_broadcast([P, NT, NG, EG]), ALU.mult))
            link(V.tensor_reduce(e4, tmp16.rearrange("p t a b -> p t b a"), AX.X, ALU.add))
            link(V.tensor_reduce(m1, e4, AX.X, ALU.max))
            first_of(e4, m1, oh1)
            link(V.scalar_tensor_tensor(out=e4b, in0=oh1, scalar=-3.0e38, in1=e4, op0=ALU.mult, op1=ALU.add))
            link(V.tensor_reduce(m2, e4b, AX.X, ALU.max))
            first_of(e4b, m2, oh2)
            V.tensor_tensor(d12, m2, m1, ALU.subtract).then_inc(s_one, 1)
            for src, dst in ((oh1, OH1), (oh2, OH2)):
                for t in range(NT):
                    a = V.tensor_tensor(dst[:, t], oh_g[:, t, :].unsqueeze(2).to_broadcast([P, NG, EG]),
                                        src[:, t, :].unsqueeze(1).to_broadcast([P, NG, EG]), ALU.mult)
            link(a)
            V.tensor_tensor(OHS, OH1, OH2, ALU.add).then_inc(s_one, 1)
            dve.wait_ge(s_gexp, 1)
            gw = rt[:, 920:920 + 3 * NT].rearrange("p (a t) -> p a t", a=3)
            d12f = rt[:, 900:900 + NT]
            link(V.tensor_reduce(gw[:, 0, :], gexp, AX.X, ALU.add))
            link(V.scalar_tensor_tensor(out=gw[:, 1, :], in0=d12f, scalar=1.0, in1=gw[:, 0, :], op0=ALU.add, op1=ALU.mult))
            link(V.reciprocal(gates[:, 0, :], gw[:, 1, :]))
            link(V.tensor_tensor(gates[:, 1, :], gates[:, 0, :], d12f, ALU.mult))
            pos = rt[:, 1000:1000 + NT * NE].rearrange("p (t e) -> p t e", t=NT)
            cnt = rt[:, 1100:1100 + NE]
            ov = rt[:, 1120:1120 + NE]
            base = rt[:, 1140:1140 + NE]
            big = rt[:, 1200:1200 + NT * NE].rearrange("p (t e) -> p t e", t=NT)
            dve.wait_ge(s_pos, 1)
            link(V.tensor_copy(pos, PS[:, 7, 0:NT * NE].rearrange("p (t e) -> p t e", t=NT)))
            link(V.tensor_copy(cnt, PS[:, 7, NT * NE:(NT + 1) * NE]))
            above = rt[:, 1320:1320 + NE * (NT - 1)].rearrange("p (e j) -> p e j", e=NE)
            link(V.tensor_tensor(above, cnt.unsqueeze(2).to_broadcast([P, NE, NT - 1]),
                                 const[:, C_CH + 1:C_CH + NT].unsqueeze(1).to_broadcast([P, NE, NT - 1]), ALU.is_gt))
            link(V.tensor_reduce(ov, above, AX.X, ALU.add))
            ends = rt[:, 1180:1180 + NE]
            steps = [ends, rt[:, 30:30 + NE]]
            src = ov
            for i in range(4):
                dst, w = steps[(i + 1) % 2], 1 << i
                V.tensor_copy(dst[:, 0:w], src[:, 0:w])
                link(V.tensor_tensor(dst[:, w:NE], src[:, w:NE], src[:, 0:NE - w], ALU.add))
                src = dst
            link(V.tensor_tensor(base, ends, ov, ALU.subtract))
            link(V.tensor_scalar(base, base, float(CAP), None, ALU.mult))
            link(V.tensor_tensor(base, base, const[:, C_OVER:C_OVER + NE], ALU.add))
            link(V.tensor_scalar(big, pos, float(CAP), None, ALU.is_ge))
            link(V.tensor_tensor(big, big, base.unsqueeze(1).to_broadcast([P, NT, NE]), ALU.mult))
            link(V.tensor_tensor(pos, pos, big, ALU.add))
            link(V.tensor_tensor(pos, pos, const[:, C_E128:C_E128 + NE].unsqueeze(1).to_broadcast([P, NT, NE]), ALU.add))
            for c, oh in ((0, OH1), (1, OH2)):
                link(V.tensor_tensor(big, pos, oh.rearrange("p t a b -> p t (a b)"), ALU.mult))
                link(V.tensor_reduce(slot_f[:, c, :], big, AX.X, ALU.add))
            slots = rt[:, 50:50 + 2 * NT]
            place = rt[:, 70:70 + 2 * NT]
            slot_v = slot_f.rearrange("p c t -> p (c t)")
            NC1 = NE + MORE + 1
            link(V.tensor_tensor(chunk_ge, slot_v.unsqueeze(2).to_broadcast([P, 2 * NT, NC1]),
                                 const[:, C_CH:C_CH + NC1].unsqueeze(1).to_broadcast([P, 2 * NT, NC1]), ALU.is_ge))
            link(V.tensor_reduce(slots, chunk_ge, AX.X, ALU.add))
            link(V.scalar_tensor_tensor(out=place, in0=slots, scalar=-float(CAP), in1=slot_v, op0=ALU.mult, op1=ALU.add))
            link(V.tensor_tensor(chunk_tok, chunk_ge[:, :, 0:NC1 - 1], chunk_ge[:, :, 1:NC1], ALU.subtract))
            for c in range(2):
                a = V.tensor_tensor(chunk_tok[:, c * NT:(c + 1) * NT, :], chunk_tok[:, c * NT:(c + 1) * NT, :],
                                    const[:, C_TOK:C_TOK + NT].unsqueeze(2).to_broadcast([P, NT, NC1 - 1]), ALU.mult)
            for c in range(2):
                V.tensor_tensor(slot_hot[:, c * NT:(c + 1) * NT, :],
                                const[:, C_COL:C_COL + P].unsqueeze(1).to_broadcast([P, NT, P]),
                                place[:, c * NT:(c + 1) * NT].unsqueeze(2).to_broadcast([P, NT, P]), ALU.is_equal).then_inc(s_hot, 1)
            V.tensor_copy(slot_i[:, :, :], slot_f).then_inc(s_slot, 1)
            over_f = rt[:, 1300:1301 + MORE]
            le = rt[:, 1320:1320 + MORE * NE].rearrange("p (i e) -> p i e", i=MORE)
            link(V.tensor_tensor(le, ends.unsqueeze(1).to_broadcast([P, MORE, NE]),
                                 const[:, C_IOTA:C_IOTA + MORE].unsqueeze(2).to_broadcast([P, MORE, NE]), ALU.is_le))
            link(V.tensor_reduce(over_f[:, 1:1 + MORE], le, AX.X, ALU.add))
            link(V.tensor_scalar(over_f[:, 1:1 + MORE], over_f[:, 1:1 + MORE], float(NE - 1), None, ALU.min))
            link(V.tensor_copy(over_f[:, 0:1], ends[:, NE - 1:NE]))
            V.tensor_copy(over_i[:, :], over_f).then_inc(s_over, 1)
            dve.wait_ge(s_lt, 1)
            V.tensor_copy(list_s, PS[:, 5, 0:NE + MORE]).then_inc(s_lc, 1)

            def expert_olo(e, b):
                dve.wait_ge(s_ohi, e + 1)
                V.tensor_tensor(wo_lo, raw_o[:, b, :].rearrange("p (k n) -> p k n", k=2), wo_hi.bitcast(fp32),
                                ALU.subtract).then_inc(s_olo, 1)

            def gathered_lo(c, b):
                dve.wait_ge(s_ghi, c + 1)
                for j in range(2):
                    a = V.tensor_tensor(hgT_lo[:, b, 4 * j:4 * j + 4, :], PS[:, 2 + j, :].rearrange("p (k t) -> p k t", k=4),
                                        hgT_hi[:, b, 4 * j:4 * j + 4, :].bitcast(fp32), ALU.subtract)
                a.then_inc(s_glo, 1)

            def silu_inverse(c, b):
                dve.wait_ge(s_ex, c + 1)
                V.tensor_scalar(sil[:, 1, :], sil[:, 0, :], 1.0, None, ALU.add).then_inc(s_sl, 1)
                dve.wait_ge(s_sl, 4 * c + 1)
                V.reciprocal(sil[:, 1, :], sil[:, 1, :]).then_inc(s_sl, 1)

            def silu_times_up(c, b):
                dve.wait_ge(s_sl, 4 * c + 2)
                V.tensor_tensor(sil[:, 1, :], sil[:, 1, :], PS[:, b, 0:DE], ALU.mult).then_inc(s_sl, 1)
                dve.wait_ge(s_sl, 4 * c + 3)
                if not isinstance(c, int) or c >= 1:
                    dve.wait_ge(s_at, c)
                V.tensor_tensor(sil[:, 2, :], sil[:, 1, :], PS[:, b, DE:2 * DE], ALU.mult).then_inc(s_sl, 1)
                dve.wait_ge(s_sl, 4 * c + 4)

            def act_lo_sub(c, b):
                dve.wait_ge(s_ahi, c + 1)
                V.tensor_tensor(aT_lo[:, b, :, :], PS[:, 4, 0:2 * P].rearrange("p (k t) -> p k t", k=2),
                                aT_hi[:, b, :, :].bitcast(fp32), ALU.subtract).then_inc(s_alo, 1)

            def y_copy(c, b):
                dve.wait_ge(s_y, c + 1)
                if not isinstance(c, int) or c >= 2:
                    dve.wait_ge(s_yst[b], 8 * (c - b))
                V.tensor_copy(y_sb[:, b, CH:2 * CH], PS[:, 7, :]).then_inc(s_yd, 1)

            expert_wlo(1, 1)
            gathered_lo(0, 0)

            def dve_pair(i, last=False):
                for b in range(2):
                    c = 2 * i + b
                    silu_inverse(c, b)
                    if not (last and b == 1):
                        gathered_lo(c + 1, 1 - b)
                    silu_times_up(c, b)
                    if not (isinstance(c, int) and c == 0):
                        y_copy(c - 1, 1 - b)
                    expert_olo(c, b)
                    act_lo_sub(c, b)
                    if not last:
                        expert_wlo(c + 2, b)

            dve_pair(0)
            with dve.Fori(1, NE // 2 - 1) as i:
                dve_pair(i)
            dve_pair(NE // 2 - 1, True)
            y_copy(NE - 1, 1)
            more = overflow_chunks(dve)
            with dve.If(more > 0):
                dve.wait_ge(s_yst[1], 16 * (NE // 2))
                with dve.Fori(0, more) as i:
                    expert_wlo(i + NE, 1)
                    expert_olo(i + NE, 1)
                    gathered_lo(i + NE, 1)
                    silu_inverse(i + NE, 1)
                    silu_times_up(i + NE, 1)
                    act_lo_sub(i + NE, 1)
                    dve.wait_ge(s_y, i + (NE + 1))
                    V.tensor_copy(y_sb[:, 1, CH:2 * CH], PS[:, 7, :]).then_inc(s_yd, 1)

            def add_rows(n):
                dve.wait_ge(s_fg, n + 1)
                y1, y2 = fin_y[:, n, 0, :], fin_y[:, n, 1, :]
                V.scalar_tensor_tensor(out=y1, in0=y2, scalar=gates[:, 1, T_ORDER[n]:T_ORDER[n] + 1], in1=y1,
                                       op0=ALU.mult, op1=ALU.add).then_inc(s_fs, 1)

            def residual(n):
                dve.wait_ge(s_fm, n + 1)
                xt = x1[:, T_ORDER[n], :]
                link(V.scalar_tensor_tensor(out=xt, in0=xt, scalar=ALPHA, in1=fin_y[:, n, 0, :], op0=ALU.mult, op1=ALU.add))
                moments(xt, NT + n)

            dve.wait_ge(s_fv, 64)
            dve.wait_ge(s_x1, NT)
            for n in range(NT + 2):
                if n < NT:
                    add_rows(n)
                if 1 <= n <= NT:
                    residual(n - 1)
                    if 1 <= n - 1 < NT - 1:
                        i = NT + n - 1
                        inverse(i)
                        V.tensor_scalar(nbias[:, i % 2:i % 2 + 1], mv[:, i % 2, 0:1], rstd[:, i % 2:i % 2 + 1], -1.0, ALU.mult,
                                        ALU.mult).then_inc(s_nb, 1)
                if n >= 2:
                    xt = x1[:, T_ORDER[n - 2], :]
                    if n - 2 in (0, NT - 1):
                        inverse(NT + n - 2)
                        scaled(xt, xt, NT + n - 2, fin_v[:, 2, :], fin_v[:, 3, :]).then_inc(s_fin[n - 2], 1)
                    else:
                        dve.wait_ge(s_fn, n - 2)
                        V.tensor_tensor(xt, xt, fin_v[:, 2, :], ALU.mult).then_inc(s_fw, 1)

        @block.tensor
        def _(pe):
            T = nc.tensor

            def three(out, lh, ll, rh, rl, first, last):
                T.matmul(out, lh, rh, start=first, stop=False)
                T.matmul(out, lh, rl, start=False, stop=False)
                return T.matmul(out, ll, rh, start=False, stop=last)

            pe.wait_ge(s_const, 16)
            pe.wait_ge(s_silu, 2)
            T.transpose(PS[:, 0, 0:P], rows[:, :], ident).then_inc(s_rows, 1)

            def ada(a):
                n = ADA_N[a]
                if a >= 2:
                    pe.wait_ge(s_ar, a - 1)
                wh, wl = w_slot(w_hi, n), w_slot(w_lo, n)
                for k in range(KD):
                    if k % 4 == 0:
                        pe.wait_ge(s_wlo, 2 * n + k // 4 + 1)
                    out = PS[0:4, (2 if a < 4 else 4) + a % 2, :]
                    T.matmul(out, cond_r[:, k, :], wh[:, k, :], start=(k == 0), stop=False)
                    m = T.matmul(out, cond_r[:, k, :], wl[:, k, :], start=False, stop=(k == KD - 1))
                m.then_inc(s_ada, 1)

            def ada_turn(a):
                pe.wait_ge(s_ar, a + 1)
                for j in range(4):
                    s = 4 * a + j
                    out = PS[:, 1, 4 * s:4 * s + 4] if a < 4 else PS[:, 7, 4 * s - 64:4 * s - 60]
                    m = T.transpose(out, mod_row[:, a % 2, j * P:(j + 1) * P], const[0:4, C_ID:C_ID + 4])
                m.then_inc(s_at0, 1)

            pe.wait_ge(s_cl, 1)
            ada(0)
            for a in range(1, 4):
                ada(a)
                ada_turn(a - 1)
            ada_turn(3)
            pe.wait_ge(s_x, 32)
            for k in range(KD):
                if k >= 2:
                    pe.wait_ge(s_h, k - 1)
                    pe.wait_ge(s_hp, k - 1)
                b = 4 + 2 * (k % 2)
                for t in range(TS):
                    T.transpose(PS[:, b, t * P:(t + 1) * P], x_nat[:, t, k * P:(k + 1) * P], ident)
                T.transpose(PS[:, b + 1, 0:P], x_nat[:, TS, k * P:(k + 1) * P], ident).then_inc(s_xt, 1)

            def project(w, m):
                n = IN_N[w]
                wh, wl = w_slot(w_hi, n), w_slot(w_lo, n)
                i = SUM0[w] + m
                if i >= 2:
                    acc_read(pe, i - 2)
                for k in range(KD):
                    if m == 0 and k % 4 == 0:
                        pe.wait_ge(s_wlo, 2 * n + k // 4 + 1)
                    if w == 0 and m == 0:
                        pe.wait_ge(s_hlo, k + 1)
                    f, l = k == 0, k == KD - 1
                    a, b = wh[:, k, m * P:(m + 1) * P], wl[:, k, m * P:(m + 1) * P]
                    for h in range(2):
                        out = PS[:, 2 * (i % 2) + h, 0:HALF]
                        sl = slice(h * HALF, (h + 1) * HALF)
                        T.matmul(out, a, h_hi[:, k, sl], start=f, stop=False)
                        T.matmul(out, a, h_lo[:, k, sl], start=False, stop=False)
                    for h in range(2):
                        out = PS[:, 2 * (i % 2) + h, 0:HALF]
                        sl = slice(h * HALF, (h + 1) * HALF)
                        mm = T.matmul(out, b, h_hi[:, k, sl], start=False, stop=l)
                mm.then_inc(s_acc, 1)

            def project_v(t):
                n = IN_N[3]
                wh, wl = w_slot(w_hi, n), w_slot(w_lo, n)
                i = SUM0[3] + t
                acc_read(pe, i - 2)
                ts = slice(t * P, (t + 1) * P)
                for k in range(KD):
                    if t == 0 and k % 4 == 0:
                        pe.wait_ge(s_wlo, 2 * n + k // 4 + 1)
                    mm = three(PS[:, 2 * (i % 2), :], h_hi[:, k, ts], h_lo[:, k, ts], wh[:, k, :], wl[:, k, :], k == 0, k == KD - 1)
                mm.then_inc(s_acc, 1)

            for w in range(6):
                for m in range(NT if w == 3 else 4):
                    if w == 3:
                        project_v(m)
                    else:
                        project(w, m)
                    if m == 0 and 1 <= w <= 4:
                        ada_turn(3 + 2 * w)
                    if w == 5 and m == 1:
                        pe.wait_ge(s_mod, 2)
                        T.transpose(PS[0:64, 7, 0:P], modc[:, 16:48, :].rearrange("p s j -> p (s j)"), ident).then_inc(s_mrow, 1)
                if w < 4:
                    ada(4 + 2 * w)
                    ada(5 + 2 * w)
                    ada_turn(4 + 2 * w)
                elif w == 4:
                    pe.wait_ge(s_ck, 32)
                    pe.wait_ge(s_ar, NA)
                    for m in range(HP):
                        for j in range(2):
                            mm = T.transpose(PS[:, 4 + m // 2, (2 * (m % 2) + j) * P:(2 * (m % 2) + j + 1) * P],
                                             ck_nat[:, j, m * P:(m + 1) * P], ident)
                    mm.then_inc(s_ckt, 1)

            def scores(u):
                if u >= 2:
                    pe.wait_ge(s_p, u - 1)
                if u < UNITS:
                    h, n = u // NB, u % NB
                    g, r = h // 2, (h % 2) * DH
                    q = qT[r:r + DH, g, n * P:(n + 1) * P]
                    keys = kT[r:r + DH, g, 0:NS].rearrange("p (w c) -> p w c", c=GRID)[:, :, KEY0[n]:KEY0[n] + SPAN]
                    T.matmul(PS[:, u % 2, 0:LOC], q, keys, start=True, stop=True)
                    T.matmul(PS[:, u % 2, LOC:LOC + PAST], q, ck_T[r:r + DH, g, :], start=True, stop=True).then_inc(s_s, 1)
                else:
                    for j in range(4):
                        h = 2 * j + u - UNITS
                        g, r = h // 2, (h % 2) * DH
                        mm = T.matmul(PS[:, u % 2, j * P:(j + 1) * P], qT[r:r + DH, g, NS:TOK], kT[r:r + DH, g, NS:TOK],
                                      start=True, stop=True)
                    mm.then_inc(s_s, 1)

            def turn(u):
                pe.wait_ge(s_pn, u + 1)
                if u >= 2:
                    pe.wait_ge(s_pts, u - 1)
                for j in range(4):
                    mm = T.transpose(PS[:, 2 + u % 2, j * P:(j + 1) * P], prob[:, u % 3, j * P:(j + 1) * P],
                                     back if u < UNITS else ident)
                mm.then_inc(s_pt, 1)

            def values(u):
                pe.wait_ge(s_pts, u + 1)
                if u < UNITS:
                    h, n = u // NB, u % NB
                    g, r = h // 2, (h % 2) * DH
                    if u % 8 == 0 and g >= 2:
                        pe.wait_ge(s_mlo, g - 1)
                    for j in range(4):
                        v = vblk[:, 2 * n + j, h * DH:(h + 1) * DH] if j < 2 else ctx_v[:, j - 2, h * DH:(h + 1) * DH]
                        mm = T.matmul(PS[r:r + DH, 6 + g % 2, n * P:(n + 1) * P], v, prob_T[:, u % 2, j * P:(j + 1) * P],
                                      start=(j == 0), stop=(j == 3))
                    mm.then_inc(s_o, 1)
                else:
                    if u == UNITS:
                        pe.wait_ge(s_mlo, HP - 1)
                    r = (u - UNITS) * DH
                    for j in range(4):
                        h = 2 * j + u - UNITS
                        mm = T.matmul(PS[r:r + DH, 6, j * P:(j + 1) * P], stage[:, 0, h * DH:(h + 1) * DH],
                                      prob_T[:, u % 2, j * P:(j + 1) * P], start=True, stop=True)
                    mm.then_inc(s_o, 1)

            pe.wait_ge(s_cks, 1)
            pe.wait_ge(s_mrs, 1)
            acc_read(pe, SUM0[6] - 1)
            pe.wait_ge(s_vb, 128)
            pe.wait_ge(s_cv, 32)
            for u in range(NU + 3):
                if u < NU:
                    scores(u)
                if u == 1:
                    for m in range(HP):
                        mm = T.transpose(PS[:, 6, m * P:(m + 1) * P], kT[:, m, NS:TOK], ident)
                    mm.then_inc(s_kp, 1)
                if u == 3:
                    pe.wait_ge(s_kps, 1)
                if 2 <= u < NU + 2:
                    turn(u - 2)
                if u >= 3:
                    values(u - 3)

            def mix_out(n):
                t = T_ORDER[n]
                if n >= 2:
                    pe.wait_ge(s_mor, n - 1)
                ts = slice(t * P, (t + 1) * P)
                for c in range(2):
                    wh, wl = w_slot(w_hi, OUT_N[c]), w_slot(w_lo, OUT_N[c])
                    for k in range(KD):
                        if n >= 1 and c == 1 and k == KD // 2:
                            turn_h2(n - 1)
                        mm = three(PS[:, 2 * (n % 2) + c, :], h_hi[:, k, ts], h_lo[:, k, ts], wh[:, k, :], wl[:, k, :],
                                   k == 0, k == KD - 1)
                mm.then_inc(s_mo, 1)

            def turn_h2(n):
                pe.wait_ge(s_h2, n + 1)
                if n >= 1:
                    pe.wait_ge(s_h2c, n)
                for k in range(KD):
                    mm = T.transpose(PS[:, 4 + k // 4, (k % 4) * P:(k % 4 + 1) * P], h2_rows[:, n % 2, k * P:(k + 1) * P], ident)
                mm.then_inc(s_h2t, 1)

            def router(n):
                t = T_ORDER[n]
                pe.wait_ge(s_h2c, n + 1)
                for k in range(KD):
                    mm = T.matmul(PS[:, 6, t * (NG + NE):(t + 1) * (NG + NE)], h2_T[:, k, :], wr[:, k, :],
                                  start=(k == 0), stop=(k == KD - 1))
                mm.then_inc(s_lg, 1)

            pe.wait_ge(s_mlo, HP + 1)
            pe.wait_ge(s_clo, 4)
            pe.wait_ge(s_wlo, E0)
            pe.wait_ge(s_wrl, 32)
            mix_out(0)
            for n in range(1, NT):
                mix_out(n)
                router(n - 1)
            turn_h2(NT - 1)
            router(NT - 1)

            oh = rt[:, 740:740 + (NT + 1) * NE].rearrange("p (t e) -> p t e", t=NT + 1)
            pe.wait_ge(s_one, 2)
            pe.wait_ge(s_rpz, 4)
            T.matmul(PS[:, 7, 0:(NT + 1) * NE], tri, oh, start=True, stop=False)
            for s in range(NT):
                mm = T.matmul(PS[:, 7, (s + 1) * NE:(NT + 1) * NE], ones[:, :],
                              oh[:, s, :].unsqueeze(1).to_broadcast([P, NT - s, NE]), start=False, stop=(s == NT - 1))
            mm.then_inc(s_pos, 1)

            def turn_rows(c, b, over=False):
                if over:
                    pe.wait_ge(s_ovg, 16 * (c - NE) + 16)
                else:
                    pe.wait_ge(s_hg[b], 16 + 8 * (c - b))
                if not isinstance(c, int) or c >= 1:
                    pe.wait_ge(s_glo, c)
                for k in range(KD):
                    mm = T.transpose(PS[:, 2 + k // 4, (k % 4) * P:(k % 4 + 1) * P], hg[:, b, k * P:(k + 1) * P], ident)
                mm.then_inc(s_hgt, 1)

            def up(c, b, turn_before=False):
                pe.wait_ge(s_wlo, c + E0 + 1)
                pe.wait_ge(s_glo, c + 1)
                if not isinstance(c, int) or c >= 2:
                    pe.wait_ge(s_sl, 4 * c - 4)
                wh, wl = w_slot(w_hi, b), w_slot(w_lo, b)
                for k in range(KD):
                    if k == 4:
                        if turn_before:
                            turn_act(c - 1, 1 - b)
                        pe.wait_ge(s_wlp, c + 1)
                    mm = three(PS[:, b, :], hgT_hi[:, b, k, :], hgT_lo[:, b, k, :], wh[:, k, :], wl[:, k, :], k == 0, k == KD - 1)
                mm.then_inc(s_hid, 1)

            def down(c, b):
                pe.wait_ge(s_alo, c + 1)
                pe.wait_ge(s_olo, c + 1)
                if not isinstance(c, int) or c >= 1:
                    pe.wait_ge(s_ya, c)
                    pe.wait_ge(s_yd, c)
                for h in range(2):
                    for k in range(2):
                        mm = three(PS[:, 6 + h, :], aT_hi[:, b, k, :], aT_lo[:, b, k, :], wo_hi[:, k, h * CH:(h + 1) * CH],
                                   wo_lo[:, k, h * CH:(h + 1) * CH], k == 0, k == 1)
                mm.then_inc(s_y, 1)

            def turn_act(c, b):
                pe.wait_ge(s_sl, 4 * c + 4)
                if not isinstance(c, int) or c >= 1:
                    pe.wait_ge(s_alo, c)
                for k in range(2):
                    mm = T.transpose(PS[:, 4, k * P:(k + 1) * P], sil[:, 2, k * P:(k + 1) * P], ident)
                mm.then_inc(s_at, 1)

            for i in range(2 * NT):
                if i % NT == 0:
                    pe.wait_ge(s_hot, i // NT + 1)
                mm = T.matmul(PS[:, 5, 0:NE + MORE], slot_hot[:, i, :], chunk_tok[:, i, :], start=(i == 0), stop=(i == 2 * NT - 1))
            mm.then_inc(s_lt, 1)
            turn_rows(0, 0)

            def pe_pair(i, last=False):
                for b in range(2):
                    c = 2 * i + b
                    after = not (isinstance(c, int) and c == 0)
                    up(c, b, after)
                    if not (last and b == 1):
                        turn_rows(c + 1, 1 - b)
                    if after:
                        down(c - 1, 1 - b)

            pe_pair(0)
            with pe.Fori(1, NE // 2 - 1) as i:
                pe_pair(i)
            pe_pair(NE // 2 - 1, True)
            turn_act(NE - 1, 1)
            down(NE - 1, 1)
            more = overflow_chunks(pe)
            with pe.If(more > 0):
                with pe.Fori(0, more) as i:
                    turn_rows(i + NE, 1, True)
                    up(i + NE, 1)
                    turn_act(i + NE, 1)
                    down(i + NE, 1)


def constants():
    import numpy as np
    P, NE, CAP, NT, MORE, SPAN, CB, NS = 128, 16, 128, 5, 10, 32, 16, 8
    ident = np.eye(P, dtype=np.float32)
    tri = np.triu(np.ones((P, P), np.float32), 1)
    k = np.arange(SPAN)[None, :]
    c = CB - 1 - (np.arange(P) % CB)[:, None]
    masks = []
    for kind in range(3):
        key = k + (32, 8, 0)[kind]
        q = c + (48, 16, 0)[kind]
        lo = np.clip(q - 8, 0, 48)
        masks.append(np.where((key >= lo) & (key < lo + 16), 0.0, -1e30).astype(np.float32))
    row = np.concatenate([
        np.arange(4, 0, -1), np.arange(NE) * CAP, NE * CAP - CAP - np.arange(NE) * CAP]).astype(np.float32)
    tok = np.arange(NT)[None, :] * P + np.arange(P)[:, None]
    iota = np.arange(MORE)
    chunks = np.concatenate([np.arange(NE + MORE + 1) * CAP, np.arange(CAP) - CAP])
    return np.concatenate([ident, tri, *masks, np.tile(row, (P, 1)), tok.astype(np.float32),
                           np.tile(iota, (P, 1)).astype(np.float32), ident[::-1],
                           np.tile(chunks, (P, 1)).astype(np.float32)], axis=1).astype(np.float32)


_INS = ["x_prompt", "x_sample", "cache_k", "cache_v", "c", "c_ctx", "w_ada", "b_ada", "w_in", "conv_w", "rpb", "w_out",
        "ln1_g", "ln1_b", "w_router_group", "b_router_group", "w_router_expert", "b_router_expert", "w_expert_in",
        "w_expert_out", "ln2_g", "ln2_b"]
_OUTS = [("y_prompt", (1, 128, 1024)), ("y_sample", (1, 512, 1024)), ("new_k", (1, 1, 8, 128, 64)),
         ("new_v", (1, 1, 8, 128, 64))]


def kernel(**inputs):
    import numpy as _np
    import concourse.bacc as _bacc
    from concourse import mybir as _mybir
    from concourse.bass_utils import run_bass_kernel_spmd as _run

    nc = _bacc.Bacc("TRN2", target_bir_lowering=False, num_devices=1)
    arrays, ins, outs = {}, {}, {}
    for name in _INS:
        arrays[f"in_{name}"] = _np.ascontiguousarray(inputs[name])
    arrays["in_const"] = constants()
    for name in _INS + ["const"]:
        a = arrays[f"in_{name}"]
        ins[name] = nc.dram_tensor(f"in_{name}", a.shape, _mybir.dt.from_np(a.dtype), kind="ExternalInput").ap()
    for name, shape in _OUTS:
        outs[name] = nc.dram_tensor(f"out_{name}", shape, _mybir.dt.float32, kind="ExternalOutput").ap()
    build(nc, ins, outs)
    r = _run(nc, [arrays], core_ids=[0])
    return tuple(r.results[0][f"out_{name}"] for name, _ in _OUTS)
```
